# Optimizing a Trainium2 kernel written in Bass

```python
import jax, jax.numpy as jnp
from jax import lax
import numpy as np

D_MODEL = 2048
BATCH = 1
SEQ = 512
DEPTH = 1

GRID_W = 64
CTX_LEN = 256
MIX_WIDTH = D_MODEL
N_DIR = 2
LRU_WIDTH = MIX_WIDTH // 2
LRU_HEADS = 16
LRU_HEAD_DIM = LRU_WIDTH // LRU_HEADS
CONV_WIDTH = 4
LRU_C = 8.0
RWKV_WIDTH = MIX_WIDTH - LRU_WIDTH
RWKV_HEAD_DIM = 64
RWKV_HEADS = RWKV_WIDTH // RWKV_HEAD_DIM
DECAY_LORA = 64
AAA_LORA = 64
GATE_LORA = 160
RWKV_COLS = 3 * RWKV_WIDTH + N_DIR * DECAY_LORA + N_DIR * AAA_LORA + GATE_LORA
IN_COLS = 2 * LRU_WIDTH + RWKV_COLS
PEER_HEADS = 8
PEER_N_KEYS = 128
PEER_N_EXPERTS = PEER_N_KEYS * PEER_N_KEYS
PEER_D_QUERY = 256
PEER_TOPK = 16
PEER_BLOCK = 128
ALPHA = (2.0 * DEPTH) ** 0.25
BETA = (8.0 * DEPTH) ** -0.25
LN_EPS = 1e-5
GN_EPS = 64e-5

kernel_name = 'hybrid_rglru_rwkv7_peer_dit_trunk'

def layer_norm(z, g, b):
    zf = z.astype(jnp.float32)
    mu = jnp.mean(zf, -1, keepdims=True)
    var = jnp.mean(jnp.square(zf - mu), -1, keepdims=True)
    return ((zf - mu) * lax.rsqrt(var + LN_EPS) * g + b).astype(z.dtype)

def modulate(z, shift, scale):
    return z * (1.0 + scale) + shift

def grid_pos_embed(rows, dim):
    t = jnp.arange(rows * GRID_W)
    row = (t // GRID_W).astype(jnp.float32)
    col = (t % GRID_W).astype(jnp.float32)
    quarter = dim // 4
    freq = 1.0 / (10000.0 ** (jnp.arange(quarter, dtype=jnp.float32) / quarter))

    def sincos(p):
        ang = p[:, None] * freq[None, :]
        return jnp.concatenate([jnp.sin(ang), jnp.cos(ang)], axis=-1)

    return jnp.concatenate([sincos(row), sincos(col)], axis=-1)

def shift_prev(z):
    return jnp.pad(z, ((0, 0), (1, 0), (0, 0)))[:, :-1]

def shift_next(z):
    return jnp.pad(z, ((0, 0), (0, 1), (0, 0)))[:, 1:]

def centred_dwconv(z, w, b):
    T = z.shape[1]
    left = CONV_WIDTH // 2
    zp = jnp.pad(z, ((0, 0), (left, CONV_WIDTH - 1 - left), (0, 0)))
    out = b
    for tap in range(CONV_WIDTH):
        out = out + zp[:, tap:tap + T] * w[tap]
    return out

def linear_scan(a, b, h0, reverse):
    if reverse:
        a, b = a[:, ::-1], b[:, ::-1]

    def combine(left, right):
        a_l, b_l = left
        a_r, b_r = right
        return a_l * a_r, a_r * b_l + b_r

    a_cum, b_cum = lax.associative_scan(combine, (a, b), axis=1)
    h = b_cum + a_cum * h0[:, None, :]
    return h[:, ::-1] if reverse else h

def block_diag_linear(z, w, b):
    zh = z.reshape(z.shape[:-1] + (LRU_HEADS, LRU_HEAD_DIM))
    out = jnp.einsum('bthi,hij->bthj', zh, w)
    return out.reshape(z.shape) + b

def rglru_coeffs(xc, wa, ba, wx, bx, lam):
    r = jax.nn.sigmoid(block_diag_linear(xc, wa, ba))
    i = jax.nn.sigmoid(block_diag_linear(xc, wx, bx))
    log_a = -LRU_C * r * jax.nn.softplus(-lam)
    return jnp.exp(log_a), jnp.sqrt(-jnp.expm1(2.0 * log_a)) * (i * xc)

def rglru_group(u_ctx, u_lat, conv_w, conv_b, wa, ba, wx, bx, lam):
    xcs = [centred_dwconv(u, conv_w, conv_b).astype(jnp.float32) for u in (u_ctx, u_lat)]
    ys = [jnp.zeros_like(xc) for xc in xcs]
    for d in range(N_DIR):
        reverse = d == 1
        h_end = jnp.zeros_like(xcs[0][:, 0])
        for s, xc in enumerate(xcs):
            a, b_in = rglru_coeffs(xc, wa[d], ba[d], wx[d], bx[d], lam[d])
            h = linear_scan(a, b_in, h_end, reverse)
            h_end = h[:, 0] if reverse else h[:, -1]
            ys[s] = ys[s] + h
    return ys

def to_heads(z):
    return z.reshape(z.shape[:-1] + (RWKV_HEADS, RWKV_HEAD_DIM))

def rwkv7_prepare(rw, mu):
    rw = rw.astype(jnp.float32)
    rw = rw + mu[0] * (shift_prev(rw) - rw) + mu[1] * (shift_next(rw) - rw)
    o = 3 * RWKV_WIDTH
    r, k, v = rw[..., :RWKV_WIDTH], rw[..., RWKV_WIDTH:2 * RWKV_WIDTH], rw[..., 2 * RWKV_WIDTH:o]
    wd = rw[..., o:o + N_DIR * DECAY_LORA].reshape(rw.shape[:-1] + (N_DIR, DECAY_LORA))
    o += N_DIR * DECAY_LORA
    ad = rw[..., o:o + N_DIR * AAA_LORA].reshape(rw.shape[:-1] + (N_DIR, AAA_LORA))
    o += N_DIR * AAA_LORA
    gd = rw[..., o:]
    return r, k, v, wd, ad, gd

def rwkv7_coeffs(k, wd, ad, w0, w2, a0, a2, k_k, k_a):
    w = -jax.nn.softplus(-(w0 + jnp.tanh(wd) @ w2)) - 0.5
    decay = jnp.exp(-jnp.exp(w))
    a = jax.nn.sigmoid(a0 + ad @ a2)
    kk = to_heads(k * k_k)
    kk = kk * lax.rsqrt(jnp.maximum(jnp.sum(kk * kk, -1, keepdims=True), 1e-24))
    kd = k * (1.0 + (a - 1.0) * k_a)
    return to_heads(decay), to_heads(kd), kk, to_heads(a)

def rwkv7_scan(r, w, k, v, a_vec, b_vec, state0, reverse):
    def step(S, inp):
        r_t, w_t, k_t, v_t, a_t, b_t = inp
        sa = jnp.einsum('bhij,bhj->bhi', S, a_t)
        S = S * w_t[:, :, None, :] + sa[..., None] * b_t[:, :, None, :] + v_t[..., None] * k_t[:, :, None, :]
        return S, jnp.einsum('bhij,bhj->bhi', S, r_t)

    xs = tuple(jnp.moveaxis(t, 1, 0) for t in (r, w, k, v, a_vec, b_vec))
    state, ys = lax.scan(step, state0, xs, reverse=reverse)
    return state, jnp.moveaxis(ys, 0, 1)

def head_groupnorm(y, g, b):
    mu = jnp.mean(y, -1, keepdims=True)
    var = jnp.mean(jnp.square(y - mu), -1, keepdims=True)
    yn = (y - mu) * lax.rsqrt(var + GN_EPS)
    return yn.reshape(y.shape[:-2] + (RWKV_WIDTH,)) * g + b

def rwkv7_group(rw_ctx, rw_lat, mu, w0, w2, a0, a2, g2, k_k, k_a, r_k, gn_g, gn_b):
    segs = [rwkv7_prepare(rw, mu) for rw in (rw_ctx, rw_lat)]
    B_ = rw_ctx.shape[0]
    ys = [jnp.zeros(s[0].shape[:-1] + (RWKV_HEADS, RWKV_HEAD_DIM), jnp.float32) for s in segs]
    bonus = [jnp.zeros_like(y) for y in ys]
    for d in range(N_DIR):
        reverse = d == 1
        state = jnp.zeros((B_, RWKV_HEADS, RWKV_HEAD_DIM, RWKV_HEAD_DIM), jnp.float32)
        for s, (r, k, v, wd, ad, gd) in enumerate(segs):
            decay, kd, kk, a = rwkv7_coeffs(k, wd[..., d, :], ad[..., d, :], w0[d], w2[d], a0[d], a2[d], k_k, k_a)
            rh, vh = to_heads(r), to_heads(v)
            state, y = rwkv7_scan(rh, decay, kd, vh, -kk, kk * a, state, reverse)
            ys[s] = ys[s] + y
            bonus[s] = bonus[s] + jnp.sum(rh * kd * r_k, -1, keepdims=True) * vh
    outs = []
    for s, (r, k, v, wd, ad, gd) in enumerate(segs):
        g = jax.nn.sigmoid(gd) @ g2
        o = head_groupnorm(ys[s], gn_g, gn_b) + bonus[s].reshape(r.shape)
        outs.append(o * g)
    return outs

def token_mixer(h_ctx, h_lat, keep_ctx, w_in, conv_w, conv_b, wa, ba, wx, bx, lam,
                mu, w0, w2, a0, a2, g2, k_k, k_a, r_k, gn_g, gn_b, w_out):
    p_ctx, p_lat = h_ctx @ w_in, h_lat @ w_in
    y_lru = rglru_group(p_ctx[..., :LRU_WIDTH], p_lat[..., :LRU_WIDTH],
                        conv_w, conv_b, wa, ba, wx, bx, lam)
    y_rwkv = rwkv7_group(p_ctx[..., 2 * LRU_WIDTH:], p_lat[..., 2 * LRU_WIDTH:],
                         mu, w0, w2, a0, a2, g2, k_k, k_a, r_k, gn_g, gn_b)

    def merge(p, yl, yr):
        gate = jax.nn.gelu(p[..., LRU_WIDTH:2 * LRU_WIDTH].astype(jnp.float32))
        return jnp.concatenate([gate * yl, yr], axis=-1).astype(p.dtype) @ w_out

    o_lat = merge(p_lat, y_lru[1], y_rwkv[1])
    o_ctx = merge(p_ctx, y_lru[0], y_rwkv[0]) if keep_ctx else None
    return o_ctx, o_lat

def peer(h, w_q, sub_keys, u, v):
    B_, T, D = h.shape
    q = (h @ w_q).reshape(B_, T, PEER_HEADS, 2, PEER_D_QUERY // 2)
    s = jnp.einsum('bthpd,hpkd->bthpk', q, sub_keys).astype(jnp.float32)
    s1, i1 = lax.top_k(s[..., 0, :], PEER_TOPK)
    s2, i2 = lax.top_k(s[..., 1, :], PEER_TOPK)
    n_cand = PEER_TOPK * PEER_TOPK
    cand_s = (s1[..., :, None] + s2[..., None, :]).reshape(B_, T, PEER_HEADS, n_cand)
    cand_i = (i1[..., :, None] * PEER_N_KEYS + i2[..., None, :]).reshape(B_, T, PEER_HEADS, n_cand)
    top_s, pos = lax.top_k(cand_s, PEER_TOPK)
    idx = jnp.take_along_axis(cand_i, pos, axis=-1)
    gates = jax.nn.softmax(top_s, axis=-1).astype(h.dtype)
    n_blocks = (B_ * T) // PEER_BLOCK
    hb = h.reshape(n_blocks, PEER_BLOCK, D)
    ib = idx.reshape(n_blocks, PEER_BLOCK, PEER_HEADS * PEER_TOPK)
    gb = gates.reshape(n_blocks, PEER_BLOCK, PEER_HEADS * PEER_TOPK)

    def expert_block(args):
        h_blk, i_blk, g_blk = args
        act = jax.nn.gelu(jnp.einsum('nkd,nd->nk', u[i_blk], h_blk), approximate=False)
        return jnp.einsum('nk,nkd->nd', g_blk * act, v[i_blk])

    return lax.map(expert_block, (hb, ib, gb)).reshape(B_, T, D)

def setup_inputs(seed: int = 0) -> dict:
    key = jax.random.key(seed)
    ks = jax.random.split(key, 40)
    ctr = [0]

    def nxt():
        k = ks[ctr[0]]
        ctr[0] += 1
        return k

    def nrm(shape, std):
        return jax.random.normal(nxt(), shape, jnp.float32) * std

    def uni(shape, lo, hi):
        return jax.random.uniform(nxt(), shape, jnp.float32, lo, hi)

    D = D_MODEL
    x = nrm((BATCH, SEQ, D), 1.0)
    c = nrm((BATCH, D), 1.0)
    ctx = nrm((BATCH, CTX_LEN, D), 1.0)
    c_ctx = nrm((D,), 1.0)
    ada_w = nrm((DEPTH, D, 6 * D), D ** -0.5)
    ada_b = nrm((DEPTH, 6 * D), 0.02)
    w_in = nrm((DEPTH, D, IN_COLS), D ** -0.5)
    lru_conv_w = nrm((DEPTH, CONV_WIDTH, LRU_WIDTH), CONV_WIDTH ** -0.5)
    lru_conv_b = nrm((DEPTH, LRU_WIDTH), 0.02)
    lru_wa = nrm((DEPTH, N_DIR, LRU_HEADS, LRU_HEAD_DIM, LRU_HEAD_DIM), LRU_HEAD_DIM ** -0.5)
    lru_ba = nrm((DEPTH, N_DIR, LRU_WIDTH), 0.02)
    lru_wx = nrm((DEPTH, N_DIR, LRU_HEADS, LRU_HEAD_DIM, LRU_HEAD_DIM), LRU_HEAD_DIM ** -0.5)
    lru_bx = nrm((DEPTH, N_DIR, LRU_WIDTH), 0.02)
    a_base = uni((DEPTH, N_DIR, LRU_WIDTH), 0.9, 0.999) ** (1.0 / LRU_C)
    lru_lambda = jnp.log(a_base) - jnp.log1p(-a_base)
    rwkv_mu = uni((DEPTH, 2, RWKV_COLS), 0.0, 0.5)
    rwkv_w0 = uni((DEPTH, N_DIR, RWKV_WIDTH), -6.0, -1.0)
    rwkv_w2 = nrm((DEPTH, N_DIR, DECAY_LORA, RWKV_WIDTH), 0.5 * DECAY_LORA ** -0.5)
    rwkv_a0 = nrm((DEPTH, N_DIR, RWKV_WIDTH), 0.1)
    rwkv_a2 = nrm((DEPTH, N_DIR, AAA_LORA, RWKV_WIDTH), AAA_LORA ** -0.5)
    rwkv_g2 = nrm((DEPTH, GATE_LORA, RWKV_WIDTH), GATE_LORA ** -0.5)
    rwkv_k_k = 0.85 + nrm((DEPTH, RWKV_WIDTH), 0.02)
    rwkv_k_a = 1.0 + nrm((DEPTH, RWKV_WIDTH), 0.02)
    rwkv_r_k = nrm((DEPTH, RWKV_HEADS, RWKV_HEAD_DIM), 0.1)
    rwkv_gn_g = 1.0 + nrm((DEPTH, RWKV_WIDTH), 0.05)
    rwkv_gn_b = nrm((DEPTH, RWKV_WIDTH), 0.02)
    w_out = nrm((DEPTH, MIX_WIDTH, D), BETA * MIX_WIDTH ** -0.5)
    ln1_g = 1.0 + nrm((DEPTH, D), 0.05)
    ln1_b = nrm((DEPTH, D), 0.02)
    peer_wq = nrm((DEPTH, D, PEER_HEADS * PEER_D_QUERY), D ** -0.5)
    peer_subkeys = nrm((DEPTH, PEER_HEADS, 2, PEER_N_KEYS, PEER_D_QUERY // 2), (PEER_D_QUERY // 2) ** -0.5)
    peer_u = nrm((DEPTH, PEER_N_EXPERTS, D), D ** -0.5)
    peer_v = nrm((DEPTH, PEER_N_EXPERTS, D), BETA)
    ln2_g = 1.0 + nrm((DEPTH, D), 0.05)
    ln2_b = nrm((DEPTH, D), 0.02)
    return {'x': x, 'c': c, 'ctx': ctx, 'c_ctx': c_ctx, 'ada_w': ada_w, 'ada_b': ada_b,
            'w_in': w_in, 'lru_conv_w': lru_conv_w, 'lru_conv_b': lru_conv_b,
            'lru_wa': lru_wa, 'lru_ba': lru_ba, 'lru_wx': lru_wx, 'lru_bx': lru_bx,
            'lru_lambda': lru_lambda, 'rwkv_mu': rwkv_mu, 'rwkv_w0': rwkv_w0, 'rwkv_w2': rwkv_w2,
            'rwkv_a0': rwkv_a0, 'rwkv_a2': rwkv_a2, 'rwkv_g2': rwkv_g2, 'rwkv_k_k': rwkv_k_k,
            'rwkv_k_a': rwkv_k_a, 'rwkv_r_k': rwkv_r_k, 'rwkv_gn_g': rwkv_gn_g, 'rwkv_gn_b': rwkv_gn_b,
            'w_out': w_out, 'ln1_g': ln1_g, 'ln1_b': ln1_b, 'peer_wq': peer_wq,
            'peer_subkeys': peer_subkeys, 'peer_u': peer_u, 'peer_v': peer_v,
            'ln2_g': ln2_g, 'ln2_b': ln2_b}

def reference(x, c, ctx, c_ctx, ada_w, ada_b, w_in, lru_conv_w, lru_conv_b, lru_wa, lru_ba,
              lru_wx, lru_bx, lru_lambda, rwkv_mu, rwkv_w0, rwkv_w2, rwkv_a0, rwkv_a2, rwkv_g2,
              rwkv_k_k, rwkv_k_a, rwkv_r_k, rwkv_gn_g, rwkv_gn_b, w_out, ln1_g, ln1_b,
              peer_wq, peer_subkeys, peer_u, peer_v, ln2_g, ln2_b):
    rows = x.shape[1] // GRID_W
    x = x + grid_pos_embed(rows, D_MODEL).astype(x.dtype)[None]
    n_ctx = ctx.shape[1]
    c_act = jax.nn.silu(c)
    cc_act = jax.nn.silu(c_ctx)
    for l in range(DEPTH):
        keep_ctx = l < DEPTH - 1
        mod_lat = (c_act @ ada_w[l] + ada_b[l])[:, None, :]
        mod_ctx = (cc_act @ ada_w[l] + ada_b[l])[None, None, :]
        sh1, sc1, gt1, sh2, sc2, gt2 = jnp.split(mod_lat, 6, axis=-1)
        csh1, csc1, cgt1, csh2, csc2, cgt2 = jnp.split(mod_ctx, 6, axis=-1)
        o_ctx, o_lat = token_mixer(
            modulate(ctx, csh1, csc1), modulate(x, sh1, sc1), keep_ctx, w_in[l],
            lru_conv_w[l], lru_conv_b[l], lru_wa[l], lru_ba[l], lru_wx[l], lru_bx[l], lru_lambda[l],
            rwkv_mu[l], rwkv_w0[l], rwkv_w2[l], rwkv_a0[l], rwkv_a2[l], rwkv_g2[l],
            rwkv_k_k[l], rwkv_k_a[l], rwkv_r_k[l], rwkv_gn_g[l], rwkv_gn_b[l], w_out[l])
        x = layer_norm(ALPHA * x + gt1 * o_lat, ln1_g[l], ln1_b[l])
        if keep_ctx:
            ctx = layer_norm(ALPHA * ctx + cgt1 * o_ctx, ln1_g[l], ln1_b[l])
            h2 = jnp.concatenate([modulate(ctx, csh2, csc2), modulate(x, sh2, sc2)], axis=1)
            f = peer(h2, peer_wq[l], peer_subkeys[l], peer_u[l], peer_v[l])
            ctx = layer_norm(ALPHA * ctx + cgt2 * f[:, :n_ctx], ln2_g[l], ln2_b[l])
            f_lat = f[:, n_ctx:]
        else:
            f_lat = peer(modulate(x, sh2, sc2), peer_wq[l], peer_subkeys[l], peer_u[l], peer_v[l])
        x = layer_norm(ALPHA * x + gt2 * f_lat, ln2_g[l], ln2_b[l])
    return x


_drawn_inputs = setup_inputs


def setup_inputs(seed=0):
    import zlib

    import numpy as np

    out = dict(_drawn_inputs(seed))
    spreads = {}
    factors = {'lru_ba': 6.027,
     'lru_bx': 4.125,
     'rwkv_w2': 3.528,
     'rwkv_a0': 5.043,
     'rwkv_gn_g': 5.529,
     'rwkv_gn_b': 22.923,
     'ln2_b': 2.845}
    for name, (base, spread) in spreads.items():
        noise = np.random.default_rng([zlib.crc32(name.encode()), seed]).standard_normal(out[name].shape)
        drawn = base * np.exp(spread * noise) if base else spread * noise
        out[name] = __import__('jax').numpy.asarray(drawn.astype(out[name].dtype))
    for name, factor in factors.items():
        out[name] = (out[name] * factor).astype(out[name].dtype)
    return out
```

```python
from contextlib import ExitStack

import numpy as np
import concourse.bass as bass
from concourse import mybir

FP32 = mybir.dt.float32
FP32R = mybir.dt.float32r
BF16 = mybir.dt.bfloat16
U32 = mybir.dt.uint32
ALU = mybir.AluOpType
ACT = mybir.ActivationFunctionType
AX = mybir.AxisListType.X

P = 128
D = 2048
KT = D // P
LAT, CTX = 512, 256
LAT0 = CTX + 1
TW = LAT0 + LAT
LRU = 1024
LT = LRU // P
N_U, N_K, N_V, N_L = LT, LT, LT, 2
BOTH_TILES = N_U + N_K + N_V + N_L
LAT_TILES = LT + LT + 2
TILES = BOTH_TILES + LAT_TILES
U0, K0, V0, LORA0 = 0, N_U, N_U + N_K, N_U + N_K + N_V
GATE0, R0, GD0 = BOTH_TILES, BOTH_TILES + LT, BOTH_TILES + 2 * LT
HD = 64
HEADS = 16
C = 128
PEER_HEADS, NK, TOPK = 8, 128, 16
HP = 2 * PEER_HEADS
GROUP = 8
DU = 256
ALPHA = 2.0 ** 0.25
LN_EPS, GN_EPS = 1e-5, 64e-5
DECAY = float(np.exp(-0.5))
LOWEST = -3.0e38
SECTIONS = 6
MOD_TILES = SECTIONS * KT
AW = 4


class Env:
    pass


def sems(nc, ctx, *names):
    handles = [nc.alloc_semaphore(n) for n in names]

    def release():
        nc.clear_and_free_semaphores(handles)
        nc.all_engine_barrier()

    ctx.callback(release)
    return handles


def modulation(nc, e, a):
    with ExitStack() as ctx:
        sb = lambda n, s, d=FP32: ctx.enter_context(nc.sbuf_tensor(n, s, d))
        cond = sb("cond", [P, KT, 2])
        cond_act = sb("cond_act", [P, KT, 2])
        w = [sb(f"ada_w{b}", [P, AW, KT * P]) for b in range(2)]
        acc = [ctx.enter_context(nc.psum_tensor(f"ada_acc{b}", [P, AW, 2], FP32)) for b in range(2)]
        cond_loaded, bias_loaded, act_ready, used, evicted, const_loaded = sems(
            nc, ctx, "cond_loaded", "adab_loaded", "cond_act_ready", "ada_w_used", "ada_evicted", "const_loaded")
        loaded = sems(nc, ctx, "ada_w0_loaded", "ada_w1_loaded")
        n_loads = MOD_TILES // AW
        with nc.Block() as block:
            @block.sync
            def _(sp):
                sp.dma_start(cond[:], a["cond"]).then_inc(cond_loaded, 16)
                for b in range(2):
                    sp.dma_start(w[b][:], a["ada_w"][b]).then_inc(loaded[b], 16)
                with sp.Fori(0, n_loads // 2 - 1) as i:
                    for b in range(2):
                        sp.wait_ge(used, 2 * i + b + 1)
                        sp.dma_start(w[b][:], a["ada_w"][bass.ds(2 * i + b + 2, 1)].rearrange("o p j n -> p (o j) n")
                                     ).then_inc(loaded[b], 16)

            @block.scalar
            def _(act):
                for dst, src in e.constants:
                    act.dma_start(dst, src).then_inc(const_loaded, 16)
                act.dma_start(e.bias[:], a["ada_b"]).then_inc(bias_loaded, 16)
                act.wait_ge(cond_loaded, 16)
                nc.scalar.activation(cond_act[:], cond[:], ACT.Silu).then_inc(act_ready, 1)
                act.wait_ge(const_loaded, 16 * len(e.constants))

            @block.tensor
            def _(pe):
                pe.wait_ge(act_ready, 1)
                with pe.Fori(0, n_loads // 2) as i:
                    for b in range(2):
                        pe.wait_ge(loaded[b], 16 * i + 16)
                        pe.wait_ge(evicted, 2 * i + b + 1)
                        for j in range(AW):
                            for k in range(KT):
                                last = nc.tensor.matmul(acc[b][:, j, :], w[b][:, j, k * P:(k + 1) * P], cond_act[:, k, :],
                                                        start=(k == 0), stop=(k == KT - 1))
                        last.then_inc(used, 1)

            @block.vector
            def _(dve):
                dve.sem_inc(evicted, 2)
                dve.wait_ge(bias_loaded, 16)
                with dve.Fori(0, n_loads // 2) as i:
                    for b in range(2):
                        dve.wait_ge(used, 2 * i + b + 1)
                        t = bass.ds((2 * i + b) * AW, AW)
                        nc.vector.tensor_tensor(e.mod[:, t, :], acc[b][:], e.bias[:, t, :], ALU.add).then_inc(evicted, 1)


def projection(nc, name, weights, first, count, rhs_hi, rhs_lo, spans, evict_vector, evict_bufs, store, prologue=None):
    with ExitStack() as ctx:
        sb = lambda n, s, d=FP32: ctx.enter_context(nc.sbuf_tensor(name + n, s, d))
        raw = [sb(f"raw{b}", [P, KT * P]) for b in range(2)]
        hi = [sb(f"hi{b}", [P, KT * P], FP32R) for b in range(2)]
        lo = [sb(f"lo{b}", [P, KT * P], FP32R) for b in range(2)]
        acc = [[ctx.enter_context(nc.psum_tensor(f"{name}acc{b}{s}", [P, w], FP32)) for s, (_, w, _) in enumerate(spans)]
               for b in range(2)]
        hi_done, lo_done, products, landed, evicted = sems(
            nc, ctx, name + "hi_done", name + "lo_done", name + "products", name + "landed", name + "evicted")
        loaded = sems(nc, ctx, name + "loaded0", name + "loaded1")
        stored, output_free = sems(nc, ctx, name + "stored", name + "output_free")
        assert count % 2 == 0
        with nc.Block() as block:
            @block.sync
            def _(sp):
                for b in range(2):
                    sp.dma_start(raw[b][:], weights[first + b]).then_inc(loaded[b], 16)
                with sp.Fori(0, count // 2 - 1) as i:
                    for b in range(2):
                        sp.wait_ge(hi_done, 2 * i + b + 1)
                        sp.wait_ge(lo_done, 2 * i + b + 1)
                        sp.dma_start(raw[b][:], weights[bass.ds(2 * i + (b + 2 + first), 1)].rearrange("o p n -> p (o n)")
                                     ).then_inc(loaded[b], 16)

            @block.scalar
            def _(act):
                act.sem_inc(landed, 2)

                def high(i, b):
                    act.wait_ge(loaded[b], 16 * i + 16)
                    act.wait_ge(products, 2 * i + b + 1)
                    nc.scalar.activation(hi[b][:], raw[b][:], ACT.Copy).then_inc(hi_done, 1)

                def land(i, b):
                    act.wait_ge(products, 2 * i + b + 3)
                    act.wait_ge(evicted, 2 * i + b + 1)
                    for s, (_, w, col) in enumerate(spans):
                        last = nc.scalar.activation(evict_bufs[b][:, col:col + w], acc[b][s][:], ACT.Copy)
                    last.then_inc(landed, 1)

                high(0, 0)
                with act.Fori(0, count // 2 - 1) as i:
                    high(i, 1)
                    land(i, 0)
                    high(i + 1, 0)
                    land(i, 1)
                high(count // 2 - 1, 1)
                land(count // 2 - 1, 0)
                land(count // 2 - 1, 1)

            @block.vector
            def _(dve):
                dve.sem_inc(evicted, 2)

                def low(i, b):
                    dve.wait_ge(hi_done, 2 * i + b + 1)
                    nc.vector.tensor_tensor(lo[b][:], raw[b][:], hi[b][:].bitcast(FP32), ALU.subtract).then_inc(lo_done, 1)

                def evict(i, b):
                    dve.wait_ge(landed, 2 * i + b + 3)
                    if store is not None:
                        dve.wait_ge(output_free, 2 * i + b + 1)
                    dve.wait_ge(evicted, 2 * i + b + 2)
                    evict_vector(dve, 2 * i + b, b).then_inc(evicted, 1)

                low(0, 0)
                with dve.Fori(0, count // 2 - 1) as i:
                    low(i, 1)
                    evict(i, 0)
                    low(i + 1, 0)
                    evict(i, 1)
                low(count // 2 - 1, 1)
                evict(count // 2 - 1, 0)
                evict(count // 2 - 1, 1)

            @block.tensor
            def _(pe):
                pe.sem_inc(products, 2)
                with pe.Fori(0, count // 2) as i:
                    for b in range(2):
                        pe.wait_ge(lo_done, 2 * i + b + 1)
                        pe.wait_ge(landed, 2 * i + b + 1)
                        for k in range(KT):
                            ks = slice(k * P, (k + 1) * P)
                            for n, (wt, x) in enumerate(((hi, rhs_hi), (hi, rhs_lo), (lo, rhs_hi))):
                                for s, (c0, w, _) in enumerate(spans):
                                    last = nc.tensor.matmul(acc[b][s][:], wt[b][:, ks], x[:, k, c0:c0 + w],
                                                            start=(k == 0 and n == 0), stop=(k == KT - 1 and n == 2))
                        last.then_inc(products, 1)

            @block.gpsimd
            def _(pool):
                if store is not None:
                    pool.sem_inc(output_free, 2)
                    with pool.Fori(0, count // 2) as i:
                        for b in range(2):
                            pool.wait_ge(evicted, 2 * i + b + 3)
                            store(pool, 2 * i + b, b).then_inc(stored, 16)
                            pool.wait_ge(stored, 32 * i + 16 * b + 16)
                            pool.sem_inc(output_free, 1)


def modulated_input(nc, e, a, x_hi, x_lo):
    with ExitStack() as ctx:
        sb = lambda n, s, d=FP32: ctx.enter_context(nc.sbuf_tensor(n, s, d))
        rows, cols = sb("pos_rows", [P, KT // 2, 8]), sb("pos_cols", [P, KT // 2, 64])
        xc = [sb(f"in_ctx{b}", [P, CTX]) for b in range(2)]
        xl = [sb(f"in_lat{b}", [P, LAT]) for b in range(2)]
        hc = [sb(f"mod_ctx{b}", [P, CTX]) for b in range(2)]
        hl = [sb(f"mod_lat{b}", [P, LAT]) for b in range(2)]
        tables_loaded, one_plus, posed, modded, hi_done, lo_done = sems(
            nc, ctx, "pos_loaded", "scale_ready", "posed", "modded", "x_hi_done", "x_lo_done")
        loaded = sems(nc, ctx, "x0_loaded", "x1_loaded")
        sc1 = e.one_plus_scale
        with nc.Block() as block:
            @block.sync
            def _(sp):
                sp.dma_start(rows[:], a["pos_rows"]).then_inc(tables_loaded, 16)
                sp.dma_start(cols[:], a["pos_cols"]).then_inc(tables_loaded, 16)
                for k in range(KT):
                    b = k % 2
                    if k >= 2:
                        sp.wait_ge(modded, k - 1)
                    sp.dma_start(xc[b][:], a["ctx"][k]).then_inc(loaded[b], 16)
                    sp.dma_start(xl[b][:], a["x"][k]).then_inc(loaded[b], 16)

            @block.vector
            def _(dve):
                nc.vector.tensor_scalar(sc1[:], e.mod[:, KT:2 * KT, :], 1.0, None, ALU.add).then_inc(one_plus, 1)
                nc.vector.tensor_scalar(e.one_plus_scale2[:], e.mod[:, 4 * KT:5 * KT, 0], 1.0, None, ALU.add).then_inc(one_plus, 1)
                dve.wait_ge(one_plus, 2)
                dve.wait_ge(tables_loaded, 32)
                for k in range(KT):
                    b = k % 2
                    dve.wait_ge(loaded[b], 32 * (k // 2 + 1))
                    table = (rows[:, k, :, None].to_broadcast([P, 8, 64]) if k < KT // 2
                             else cols[:, k - KT // 2, None, :].to_broadcast([P, 8, 64]))
                    grid = xl[b][:].rearrange("p (r c) -> p r c", c=64)
                    nc.vector.tensor_tensor(grid, grid, table, ALU.add).then_inc(posed, 1)
                    dve.wait_ge(posed, k + 1)
                    if k >= 2:
                        dve.wait_ge(lo_done, k - 1)
                    nc.vector.tensor_scalar(hc[b][:], xc[b][:], sc1[:, k, 1:2], e.mod[:, k, 1:2], ALU.mult, ALU.add)
                    nc.vector.tensor_scalar(hl[b][:], xl[b][:], sc1[:, k, 0:1], e.mod[:, k, 0:1], ALU.mult, ALU.add
                                            ).then_inc(modded, 1)
                    dve.wait_ge(hi_done, k + 1)
                    nc.vector.tensor_tensor(x_lo[:, k, 0:CTX], hc[b][:], x_hi[:, k, 0:CTX].bitcast(FP32), ALU.subtract)
                    nc.vector.tensor_tensor(x_lo[:, k, CTX:], hl[b][:], x_hi[:, k, CTX:].bitcast(FP32), ALU.subtract
                                            ).then_inc(lo_done, 1)

            @block.scalar
            def _(act):
                for k in range(KT):
                    b = k % 2
                    act.wait_ge(modded, k + 1)
                    nc.scalar.activation(x_hi[:, k, 0:CTX], hc[b][:], ACT.Copy)
                    nc.scalar.activation(x_hi[:, k, CTX:], hl[b][:], ACT.Copy).then_inc(hi_done, 1)


def in_projection(nc, e, a):
    with ExitStack() as ctx:
        sb = lambda n, s, d=FP32: ctx.enter_context(nc.sbuf_tensor(n, s, d))
        x_hi, x_lo = sb("x_hi", [P, KT, CTX + LAT], FP32R), sb("x_lo", [P, KT, CTX + LAT], FP32R)
        modulated_input(nc, e, a, x_hi, x_lo)
        mu = sb("mu", [P, TILES, 2])
        landing = [sb(f"p_landing{b}", [P, TW + 2]) for b in range(2)]
        mixed = [sb(f"p_mixed{b}", [P, TW]) for b in range(2)]
        diff, half = sb("p_diff", [P, TW]), sb("p_half", [P, TW])
        (mu_loaded, cleared) = sems(nc, ctx, "mu_loaded", "landing_cleared")
        with nc.Block() as block:
            @block.sync
            def _(sp):
                sp.dma_start(mu[:], a["mu"]).then_inc(mu_loaded, 16)
                sp.wait_ge(mu_loaded, 16)

            @block.vector
            def _(dve):
                for b in range(2):
                    nc.vector.memset(landing[b][:], 0.0)
                nc.vector.memset(diff[:], 0.0)
                nc.vector.memset(half[:], 0.0)
                for b in range(2):
                    nc.vector.memset(mixed[b][:], 0.0)
        for tag, first, count, lat_only in (("pb_", 0, BOTH_TILES, False), ("pl_", BOTH_TILES, LAT_TILES, True)):
            (step,) = sems(nc, ctx, tag + "shift_step")
            cols = slice(LAT0, TW) if lat_only else slice(0, TW)
            n_cols = cols.stop - cols.start
            prev, cur, nxt = (slice(cols.start + s, cols.start + s + n_cols) for s in range(3))

            def shift(dve, unit, b, first=first, step=step, cols=cols, prev=prev, cur=cur, nxt=nxt):
                at = bass.ds(unit + first, 1)
                m = landing[b]
                n = unit * 3
                nc.vector.tensor_tensor(diff[:, cols], m[:, prev], m[:, cur], ALU.subtract).then_inc(step, 1)
                dve.wait_ge(step, n + 1)
                nc.vector.scalar_tensor_tensor(out=half[:, cols], in0=diff[:, cols], scalar=mu[:, at, 0], in1=m[:, cur],
                                               op0=ALU.mult, op1=ALU.add).then_inc(step, 1)
                dve.wait_ge(step, n + 2)
                nc.vector.tensor_tensor(diff[:, cols], m[:, nxt], m[:, cur], ALU.subtract).then_inc(step, 1)
                dve.wait_ge(step, n + 3)
                return nc.vector.scalar_tensor_tensor(out=mixed[b][:, cols], in0=diff[:, cols], scalar=mu[:, at, 1],
                                                      in1=half[:, cols], op0=ALU.mult, op1=ALU.add)

            def store(eng, unit, b, first=first, cols=cols):
                dst = e.p_dram[bass.ds(unit + first, 1)].rearrange("o p n -> p (o n)")
                return eng.dma_start(dst[:, cols], mixed[b][:, cols])

            spans = [(CTX, LAT, LAT0 + 1)] if lat_only else [(CTX, LAT, LAT0 + 1), (0, CTX, 1)]
            projection(nc, tag, a["w_in"], first, count, x_hi, x_lo, spans, shift, landing, store)

ZW = 2 + CTX + 3 + LAT + 1
XW = ZW - 3
XL = CTX + 3
X_SEGS = ((0, CTX), (XL, LAT))


class Chain:

    def __init__(self, engine, sem, base=0):
        self.engine, self.sem, self.base, self.n = engine, sem, base, 0

    def step(self, ins):
        self.n += 1
        return ins.then_inc(self.sem, 1)

    def ordered(self, ins):
        self.step(ins)
        self.engine.wait_ge(self.sem, self.base + self.n)


def rglru(nc, e, a):
    with ExitStack() as ctx:
        sb = lambda n, s, d=FP32: ctx.enter_context(nc.sbuf_tensor("lru_" + n, s, d))
        z, xc = sb("z", [P, LT, ZW]), sb("xc", [P, LT, XW])
        gate_a, gate_x, th = sb("gate_a", [P, LT, XW]), sb("gate_x", [P, LT, XW]), sb("tanh", [P, LT, XW])
        y, gate, h = sb("y", [P, LT, LAT]), sb("gate", [P, LT, LAT]), sb("h", [P, LAT])
        h_ctx = sb("h_ctx", [P, CTX])
        w = [sb("wa", [P, 2 * LT, P]), sb("wx", [P, 2 * LT, P])]
        vec = sb("vec", [P, 11, LT])
        decay, neg_decay = sb("decay", [P, 2, LT]), sb("neg_decay", [P, 2, LT])
        tmp = [sb(f"tmp{i}", [P, 2, LT]) for i in range(4)]
        acc = [[[ctx.enter_context(nc.psum_tensor(f"lru_acc{b}{g}{s}", [P, n], FP32)) for s, (_, n) in enumerate(X_SEGS)]
                for g in range(2)] for b in range(2)]
        vec_loaded, z_loaded, w_cleared, w_loaded, gate_loaded, y_stored = sems(
            nc, ctx, "lru_vec_loaded", "z_loaded", "lru_w_cleared", "lru_w_loaded", "gate_loaded", "y_stored")
        abs_ready, exp_ready, decay_ready, conv_done, gates, gates_read, tanh_done, a_done, ratio, root, scanned, gelu_done, merged, v_step, a_step = sems(
            nc, ctx, "lam_abs", "lam_exp", "decay_ready", "conv_done", "gate_products", "gates_ready", "tanh_done",
            "a_done", "ratio_done", "root_done", "scanned", "gelu_done", "lru_merged", "lru_v_step", "lru_a_step")
        with nc.Block() as block:
            @block.sync
            def _(sp):
                sp.dma_start(vec[:], a["lru_vec"]).then_inc(vec_loaded, 16)
                tiles = e.p_dram[U0:U0 + LT].rearrange("t p n -> p t n")
                sp.dma_start(z[:, :, 2:2 + CTX], tiles[:, :, 0:CTX]).then_inc(z_loaded, 16)
                sp.dma_start(z[:, :, 2 + XL:2 + XL + LAT], tiles[:, :, LAT0:]).then_inc(z_loaded, 16)
                sp.wait_ge(w_cleared, 1)
                for g, name in enumerate(("lru_wa", "lru_wx")):
                    for s in range(2):
                        sp.dma_start(w[g][s * HD:(s + 1) * HD, :, s * HD:(s + 1) * HD], a[name][s]).then_inc(w_loaded, 16)
                sp.dma_start(gate[:], e.p_dram[GATE0:GATE0 + LT].rearrange("t p n -> p t n")[:, :, LAT0:]).then_inc(gate_loaded, 16)
                sp.wait_ge(merged, 1)
                sp.dma_start(e.merged_dram[0:LT].rearrange("t p n -> p t n"), y[:]).then_inc(y_stored, 16)
                sp.wait_ge(y_stored, 16)

            @block.gpsimd
            def _(pool):
                nc.gpsimd.memset(w[0][:], 0.0)
                nc.gpsimd.memset(w[1][:], 0.0).then_inc(w_cleared, 1)

            @block.vector
            def _(dve):
                c = Chain(dve, v_step)
                for seg in ((0, 2), (2 + CTX, 3), (ZW - 1, 1)):
                    nc.vector.memset(z[:, :, seg[0]:seg[0] + seg[1]], 0.0)
                for t in (gate_a, gate_x):
                    c.ordered(nc.vector.memset(t[:, :, CTX:XL], 0.0))
                dve.wait_ge(exp_ready, 1)
                lam, (ex, s1, s2, poly) = vec[:, 9:11, :], (t[:] for t in tmp)
                c.ordered(nc.vector.tensor_scalar(s1, ex, 2.0, None, ALU.add))
                c.ordered(nc.vector.reciprocal(s1, s1))
                c.ordered(nc.vector.tensor_tensor(s1, s1, ex, ALU.mult))
                c.ordered(nc.vector.tensor_tensor(s2, s1, s1, ALU.mult))
                c.ordered(nc.vector.memset(poly, 1.0 / 19))
                for k in range(8, -1, -1):
                    c.ordered(nc.vector.tensor_tensor(poly, poly, s2, ALU.mult))
                    c.ordered(nc.vector.tensor_scalar(poly, poly, 1.0 / (2 * k + 1), None, ALU.add))
                c.ordered(nc.vector.tensor_tensor(poly, poly, s1, ALU.mult))
                c.ordered(nc.vector.tensor_scalar(s2, lam, -1.0, 0.0, ALU.mult, ALU.max))
                c.ordered(nc.vector.scalar_tensor_tensor(out=poly, in0=poly, scalar=2.0, in1=s2, op0=ALU.mult, op1=ALU.add))
                c.ordered(nc.vector.tensor_scalar(decay[:], poly, 8.0, None, ALU.mult))
                nc.vector.tensor_scalar(neg_decay[:], poly, -8.0, None, ALU.mult).then_inc(decay_ready, 1)
                dve.wait_ge(z_loaded, 32)
                for j in range(LT):
                    c.step(nc.vector.tensor_scalar(xc[:, j, :], z[:, j, 0:XW], vec[:, 0, j:j + 1], vec[:, 4, j:j + 1], ALU.mult, ALU.add))
                for tap in range(1, 4):
                    for j in range(LT):
                        dve.wait_ge(v_step, c.n - LT + 1)
                        ins = nc.vector.scalar_tensor_tensor(out=xc[:, j, :], in0=z[:, j, tap:tap + XW], scalar=vec[:, tap, j:j + 1],
                                                             in1=xc[:, j, :], op0=ALU.mult, op1=ALU.add)
                        c.step(ins)
                        if tap == 3:
                            dve.wait_ge(v_step, c.n)
                            dve.sem_inc(conv_done, 1)
                inv = z[:, :, 0:XW]
                for d in range(2):
                    dve.wait_ge(gates_read, 2 * LT * (d + 1))
                    c.ordered(nc.vector.tensor_tensor(gate_x[:], gate_x[:], xc[:], ALU.mult))
                    dve.wait_ge(tanh_done, d + 1)
                    c.ordered(nc.vector.tensor_scalar(inv, th[:], 1.0, None, ALU.add))
                    c.ordered(nc.vector.reciprocal(inv, inv))
                    nc.vector.tensor_tensor(th[:], th[:], inv, ALU.mult).then_inc(ratio, 1)
                    dve.wait_ge(root, d + 1)
                    c.ordered(nc.vector.tensor_tensor(gate_x[:], gate_x[:], th[:], ALU.mult))
                    for j in range(LT):
                        flip = slice(None, None, -1) if d else slice(None)
                        if d == 0:
                            h_out = y[:, j, :]
                        else:
                            h_out = h[:]
                            if j:
                                dve.wait_ge(v_step, c.n)
                        A, B = gate_a[:, j, :], gate_x[:, j, :]
                        c.ordered(nc.vector.tensor_tensor_scan(h_ctx[:, flip], A[:, 0:CTX][:, flip], B[:, 0:CTX][:, flip], 0.0,
                                                               ALU.mult, ALU.add))
                        end = h_ctx[:, 0:1] if d else h_ctx[:, CTX - 1:CTX]
                        c.ordered(nc.vector.tensor_tensor_scan(h_out[:, flip], A[:, XL:][:, flip], B[:, XL:][:, flip], end,
                                                               ALU.mult, ALU.add))
                        if d:
                            c.ordered(nc.vector.tensor_tensor(y[:, j, :], y[:, j, :], h[:], ALU.add))
                    dve.sem_inc(scanned, 1)
                dve.wait_ge(gelu_done, 1)
                nc.vector.tensor_tensor(y[:], y[:], gate[:], ALU.mult).then_inc(merged, 1)

            @block.scalar
            def _(act):
                c = Chain(act, a_step)
                act.wait_ge(vec_loaded, 16)
                c.ordered(nc.scalar.activation(tmp[1][:], vec[:, 9:11, :], ACT.Abs))
                nc.scalar.activation(tmp[0][:], tmp[1][:], ACT.Exp, scale=-1.0).then_inc(exp_ready, 1)
                for d in range(2):
                    if d:
                        act.wait_ge(scanned, d)
                    for j in range(LT):
                        n = d * LT + j
                        act.wait_ge(gates, n + 1)
                        for g, (dst, bias) in enumerate(((gate_a, 5 + d), (gate_x, 7 + d))):
                            for s, (c0, w_) in enumerate(X_SEGS):
                                ins = nc.scalar.activation(dst[:, j, c0:c0 + w_], acc[n % 2][g][s][:], ACT.Sigmoid,
                                                           bias=vec[:, bias, j:j + 1])
                            ins.then_inc(gates_read, 1)
                    act.wait_ge(gates_read, 2 * LT * (d + 1))
                    act.wait_ge(decay_ready, 1)
                    for j in range(LT):
                        ins = nc.scalar.activation(th[:, j, :], gate_a[:, j, :], ACT.Tanh, scale=decay[:, d, j:j + 1])
                    ins.then_inc(tanh_done, 1)
                    act.wait_ge(tanh_done, d + 1)
                    for j in range(LT):
                        ins = nc.scalar.activation(gate_a[:, j, :], gate_a[:, j, :], ACT.Exp, scale=neg_decay[:, d, j:j + 1])
                    c.ordered(ins)
                    act.wait_ge(ratio, d + 1)
                    nc.scalar.activation(th[:], th[:], ACT.Sqrt, scale=2.0).then_inc(root, 1)
                act.wait_ge(gate_loaded, 16)
                nc.scalar.activation(gate[:], gate[:], ACT.Gelu_apprx_tanh).then_inc(gelu_done, 1)

            @block.tensor
            def _(pe):
                pe.wait_ge(w_loaded, 64)
                for d in range(2):
                    for j in range(LT):
                        n = d * LT + j
                        pe.wait_ge(conv_done, j + 1)
                        if n >= 2:
                            pe.wait_ge(gates_read, 2 * (n - 1))
                        for g in range(2):
                            for s, (c0, w_) in enumerate(X_SEGS):
                                last = nc.tensor.matmul(acc[n % 2][g][s][:], w[g][:, d * LT + j, :], xc[:, j, c0:c0 + w_],
                                                        start=True, stop=True)
                        last.then_inc(gates, 1)


LEVELS = 7
PAIRS = HEADS // 2
BANKS = 8
BANK = 512


def slot(p, s):
    return (p // 2) * 4 + s * 2 + p % 2


def chunk_fills(lat):
    fills = [(("zw", h), "act") for h in range(2)] + [(("za", h), "act") for h in range(2)]
    fills += [(("norm", h), "dve") for h in range(2)]
    if lat:
        fills += [(("bonus", h), "dve") for h in range(2)]
    fills += [((t, h), "act") for t in ("bT", "kT", "vT") for h in range(2)]
    fills += [((m, q, s), "dve") for q in range(4) for m in ("Mb", "Mk") for s in range(2)]
    for level in range(1, LEVELS + 1):
        fills += [(("X", level, q), "dve") for q in range(4)]
        for q in range(4):
            if 1 < level < LEVELS:
                fills.append((("T", level, q), "act"))
            fills.append((("Tt", level, q), "act"))
    fills += [(("rhs", h), "act") for h in range(2)] + [(("U", h), "act") for h in range(2)]
    if lat:
        fills += [(("Y", h), "dve") for h in range(2)]
    return fills + [(("S",), "dve")]


def fill_tables(lat):
    bank, count, total = {}, {}, {"act": 0, "dve": 0}
    for n, (name, engine) in enumerate(chunk_fills(lat)):
        bank[name] = n % BANKS
        total[engine] += 1
        count[name] = total[engine]
    return bank, count, total


V_STEPS = {False: 10, True: 12}


def rwkv(nc, e, a):
    with ExitStack() as ctx:
        sb = lambda n, s, d=FP32: ctx.enter_context(nc.sbuf_tensor("rw_" + n, s, d))
        y_acc, bonus = sb("y_acc", [P, PAIRS, LAT]), sb("bonus_acc", [P, PAIRS, LAT])
        ident, ones = sb("ident", [P, P]), sb("head_ones", [P, P])
        vec = sb("vec", [P, 9, PAIRS])
        with ExitStack() as inner:
            rwkv_scan(nc, e, a, ctx, inner, y_acc, bonus, ident, ones, vec)
        rwkv_out(nc, e, a, y_acc, bonus, ones, vec)


def rwkv_scan(nc, e, a, ctx, inner, y_acc, bonus, ident, ones, vec):
    sb = lambda n, s, d=FP32: inner.enter_context(nc.sbuf_tensor("rw_" + n, s, d))
    full = [P, PAIRS, C]
    k, v, r = sb("k", full), sb("v", full), sb("r", full)
    lora = sb("lora", [P, 2, C])
    w2, a2 = sb("w2", [P, LRU]), sb("a2", [P, LRU])
    ident_b = sb("ident_b", [P, P], BF16)
    tri = sb("tri", [P, 2, 2, C])
    level_mask = sb("level_mask", [P, 2, LEVELS, C])
    restart = sb("restart", full)
    tw = sb("tanh_w", [P, C])
    sg, rate, kraw, kd, cum, cum_ex = (sb(n, full) for n in ("sg", "rate", "kraw", "kd", "cum", "cum_ex"))
    w_r, w_inv, w_ex = (sb(n, full) for n in ("w_r", "w_inv", "w_ex"))
    sq, rk = w_ex, w_r
    nrm = cum_ex
    mid, w_mid = sb("mid", [P, PAIRS]), sb("w_mid", [P, PAIRS])
    AR, Bt, Kt = sb("AR", [P, PAIRS, 2, C]), sb("Bt", full), sb("Kt", full)
    BT, KTT, VT = (sb(n, [P, LRU]) for n in ("B_T", "K_T", "V_T"))
    Mb, Mk = sb("Mb", [P, HEADS, 2, C]), sb("Mk", [P, HEADS, 2, C])
    X, T, Tt = (sb(n, [P, HEADS, C]) for n in ("X", "T", "Tt"))
    rhs, U = sb("rhs", [P, LRU]), sb("U", [P, LRU])
    S, S_mid, S_sum = (sb(n, [P, PAIRS, HD]) for n in ("S", "S_mid", "S_sum"))
    banks = [inner.enter_context(nc.psum_tensor(f"rw_bank{b}", [P, BANK], FP32)) for b in range(BANKS)]
    (const_loaded, raw_loaded, tanh_done, sq_ready, norm_ready, rsqrt_ready, rk_ready, cum_ready, weights_ready, tilde_ready,
     state_ready, filled_act, filled_dve, act_read, dve_read, v_step, raw_free, a_step, bonus_done) = sems(
        nc, ctx, "rw_const_loaded", "rw_raw_loaded", "rw_tanh_done", "sq_ready", "norm_ready", "rsqrt_ready", "rk_ready", "cum_ready",
        "weights_ready", "tilde_ready", "state_ready", "filled_for_act", "filled_for_dve", "act_read", "dve_read", "rw_v_step",
        "raw_free", "rw_a_step", "bonus_done")
    tables = {lat: fill_tables(lat) for lat in (False, True)}

    def bcast(t, n):
        return t[:, :, None].to_broadcast([P, PAIRS, n])

    class Loops:

        def __iter__(self):
            n, act, dve, v, loads, n_lat = 0, 0, 0, 0, 0, 0
            for d in range(2):
                for lat, count in ((False, CTX // C), (True, LAT // C)):
                    yield d, lat, count, dict(n=n, act=act, dve=dve, v=v, loads=loads, lat=n_lat)
                    n += count
                    act += count * tables[lat][2]["act"]
                    dve += count * tables[lat][2]["dve"]
                    v += count * V_STEPS[lat]
                    loads += count * (64 if lat else 48)
                    n_lat += count * lat

    def token(d, lat, count, i):
        return i * -C + (count - 1) * C if d else i * C

    with nc.Block() as block:
        @block.sync
        def _(sp):
            consts = [(ident, a["ident"]), (ones, a["rwkv_ones"]), (vec, a["rwkv_vec"]), (w2, a["rwkv_w2"]), (a2, a["rwkv_a2"]),
                      (tri, a["rwkv_tri"]), (level_mask, a["rwkv_level"])]
            for dst, src in consts:
                sp.dma_start(dst[:], src).then_inc(const_loaded, 16)
            for d, lat, count, base in Loops():
                with sp.Fori(0, count) as i:
                    first = sp.snap(token(d, lat, count, i) + (LAT0 if lat else 0))
                    sp.wait_ge(raw_free, base["n"] + i + 1)
                    at = bass.ds(first, C)
                    for dst, tile in ((k, K0), (v, V0)) + (((r, R0),) if lat else ()):
                        sp.dma_start(dst[:], e.p_dram[tile:tile + LT].rearrange("t p n -> p t n")[:, :, at]).then_inc(raw_loaded, 16)
                    sp.dma_start(lora[:], e.p_dram[LORA0:LORA0 + 2].rearrange("t p n -> p t n")[:, :, at]).then_inc(raw_loaded, 16)

        @block.scalar
        def _(act):
            act.sem_inc(act_read, 1)
            for d, lat, count, base in Loops():
                bank_of, count_at, per_chunk = tables[lat]
                loads = 64 if lat else 48
                with act.Fori(0, count) as i:
                    n = base["n"] + i

                    def read(name):
                        act.wait_ge(filled_act, base["act"] + i * per_chunk["act"] + count_at[name])
                        return banks[bank_of[name]]

                    act.wait_ge(raw_loaded, base["loads"] + i * loads + loads)
                    nc.scalar.activation(tw[:], lora[:, 0, :], ACT.Tanh).then_inc(tanh_done, 1)
                    for kind, dst, row in (("zw", sg, 0), ("za", rate, 2)):
                        for h in range(2):
                            src = read((kind, h))
                            for q in range(4):
                                p = 4 * h + q
                                ins = nc.scalar.activation(dst[:, p, :], src[:, q * C:(q + 1) * C], ACT.Sigmoid,
                                                           bias=vec[:, row + d, p:p + 1])
                            ins.then_inc(act_read, 1)
                    act.wait_ge(norm_ready, n + 1)
                    nc.scalar.activation(nrm[:], nrm[:], ACT.Ln).then_inc(a_step, 1)
                    act.wait_ge(a_step, n + 1)
                    nc.scalar.activation(nrm[:], nrm[:], ACT.Exp, scale=-0.5).then_inc(rsqrt_ready, 1)
                    act.wait_ge(cum_ready, n + 1)
                    nc.scalar.activation(w_inv[:], cum[:], ACT.Exp, scale=DECAY)
                    nc.scalar.activation(w_r[:], cum[:], ACT.Exp, scale=-DECAY)
                    nc.scalar.activation(w_ex[:], w_ex[:], ACT.Exp, scale=-DECAY)
                    nc.scalar.activation(w_mid[:], mid[:], ACT.Exp, scale=-DECAY).then_inc(weights_ready, 1)
                    for kind, dst in (("bT", BT), ("kT", KTT), ("vT", VT)):
                        for h in range(2):
                            nc.scalar.activation(dst[:, h * BANK:(h + 1) * BANK], read((kind, h))[:], ACT.Copy).then_inc(act_read, 1)
                    for level in range(1, LEVELS + 1):
                        for q in range(4):
                            if 1 < level < LEVELS:
                                nc.scalar.activation(T[:, 4 * q:4 * q + 4, :].rearrange("p h n -> p (h n)"), read(("T", level, q))[:],
                                                     ACT.Copy).then_inc(act_read, 1)
                            nc.scalar.activation(Tt[:, 4 * q:4 * q + 4, :].rearrange("p h n -> p (h n)"), read(("Tt", level, q))[:],
                                                 ACT.Copy).then_inc(act_read, 1)
                    for s in range(2):
                        nc.scalar.activation(rhs[:].rearrange("p (q s n) -> p q s n", s=2, n=HD)[:, :, s, :],
                                             read(("rhs", s))[:].rearrange("p (q n) -> p q n", n=HD), ACT.Copy).then_inc(act_read, 1)
                    for h in range(2):
                        nc.scalar.activation(U[:, h * BANK:(h + 1) * BANK], read(("U", h))[:], ACT.Copy).then_inc(act_read, 1)

        @block.vector
        def _(dve):
            dve.sem_inc(dve_read, 1)
            dve.sem_inc(raw_free, 1)
            dve.wait_ge(const_loaded, 16 * 7)
            nc.vector.tensor_copy(ident_b[:], ident[:])
            nc.vector.memset(restart[:], 1.0).then_inc(v_step, 1)
            dve.wait_ge(v_step, 1)
            nc.vector.memset(restart[:, :, 0:1], 0.0)
            nc.vector.memset(bonus[:], 0.0).then_inc(v_step, 1)
            dve.wait_ge(v_step, 2)
            for d, lat, count, base in Loops():
                bank_of, count_at, per_chunk = tables[lat]
                loads = 64 if lat else 48
                if not lat:
                    nc.vector.memset(S[:], 0.0)
                with dve.Fori(0, count) as i:
                    n = base["n"] + i
                    tok = bass.ds(dve.snap(token(d, lat, count, i)), C)
                    c = Chain(dve, v_step, base["v"] + 2 + i * V_STEPS[lat])

                    def read(name):
                        dve.wait_ge(filled_dve, base["dve"] + i * per_chunk["dve"] + count_at[name])
                        return banks[bank_of[name]]

                    def act_has_read(name):
                        dve.wait_ge(act_read, base["act"] + i * per_chunk["act"] + count_at[name] + 1)

                    dve.wait_ge(raw_loaded, base["loads"] + i * loads + loads)
                    c.ordered(nc.vector.tensor_tensor(kraw[:], k[:], bcast(vec[:, 4, :], C), ALU.mult))
                    nc.vector.tensor_tensor(sq[:], kraw[:], kraw[:], ALU.mult).then_inc(sq_ready, 1)
                    act_has_read(("zw", 1))
                    flat = lambda t: t[:].rearrange("p h n -> p (h n)")
                    flip = slice(None, None, -1) if d else slice(None)
                    c.ordered(nc.vector.tensor_tensor_scan(flat(cum)[:, flip], flat(restart), flat(sg)[:, flip], 0.0, ALU.mult, ALU.add))
                    m = C // 2 if d else C // 2 - 1
                    c.ordered(nc.vector.tensor_copy(mid[:], cum[:, :, m]))
                    c.ordered(nc.vector.tensor_tensor(cum[:], cum[:], bcast(mid, C), ALU.subtract))
                    act_has_read(("za", 1))
                    c.ordered(nc.vector.scalar_tensor_tensor(out=kd[:], in0=rate[:], scalar=1.0, in1=bcast(vec[:, 5, :], C),
                                                             op0=ALU.subtract, op1=ALU.mult))
                    c.ordered(nc.vector.scalar_tensor_tensor(out=kd[:], in0=kd[:], scalar=1.0, in1=k[:], op0=ALU.add, op1=ALU.mult))
                    if lat:
                        c.ordered(nc.vector.tensor_tensor(rk[:], r[:], kd[:], ALU.mult))
                        nc.vector.tensor_tensor(rk[:], rk[:], bcast(vec[:, 6, :], C), ALU.mult).then_inc(rk_ready, 1)
                    for h in range(2):
                        ins = nc.vector.tensor_scalar(nrm[:, 4 * h:4 * h + 4, :].rearrange("p h n -> p (h n)"), read(("norm", h))[:],
                                                      1e-24, None, ALU.max)
                        ins.then_inc(dve_read, 1)
                    dve.wait_ge(dve_read, base["dve"] + i * per_chunk["dve"] + count_at[("norm", 1)] + 1)
                    dve.sem_inc(norm_ready, 1)
                    if lat:
                        for h in range(2):
                            half = slice(4 * h, 4 * h + 4)
                            nc.vector.tensor_tensor(Kt[:, half, :], read(("bonus", h))[:].rearrange("p (h n) -> p h n", n=C), v[:, half, :],
                                                    ALU.mult).then_inc(dve_read, 1)
                        dve.wait_ge(dve_read, base["dve"] + i * per_chunk["dve"] + count_at[("bonus", 1)] + 1)
                        c.ordered(nc.vector.tensor_tensor(bonus[:, :, tok], bonus[:, :, tok], Kt[:], ALU.add))
                    nc.vector.tensor_tensor(w_ex[:], cum[:], sg[:], ALU.subtract).then_inc(cum_ready, 1)
                    dve.wait_ge(rsqrt_ready, n + 1)
                    c.ordered(nc.vector.tensor_tensor(kraw[:], kraw[:], nrm[:], ALU.mult))
                    c.ordered(nc.vector.tensor_tensor(rate[:], rate[:], kraw[:], ALU.mult))
                    dve.wait_ge(weights_ready, n + 1)
                    nc.vector.scalar_tensor_tensor(out=AR[:, :, 0, :], in0=kraw[:], scalar=-1.0, in1=w_ex[:], op0=ALU.mult, op1=ALU.mult)
                    nc.vector.tensor_tensor(Bt[:], rate[:], w_inv[:], ALU.mult)
                    if lat:
                        nc.vector.tensor_tensor(AR[:, :, 1, :], r[:], w_r[:], ALU.mult)
                    c.ordered(nc.vector.tensor_tensor(Kt[:], kd[:], w_inv[:], ALU.mult))
                    dve.sem_inc(tilde_ready, 1)
                    nc.vector.tensor_tensor(S_mid[:], S[:], bcast(w_mid, HD), ALU.mult).then_inc(state_ready, 1)
                    act_has_read(("vT", 1))
                    dve.sem_inc(raw_free, 1)
                    for q in range(4):
                        for m_, dst in (("Mb", Mb), ("Mk", Mk)):
                            for s in range(2):
                                src = read((m_, q, s))
                                at = slice(4 * q + 2 * s, 4 * q + 2 * s + 2)
                                if lat:
                                    mask = tri[:, d, None, :, :].to_broadcast([P, 2, 2, C])
                                    nc.vector.tensor_tensor(dst[:, at, :, :], src[:].rearrange("p (h m n) -> p h m n", h=2, m=2),
                                                            mask, ALU.mult).then_inc(dve_read, 1)
                                else:
                                    mask = tri[:, d, 0, None, :].to_broadcast([P, 2, C])
                                    nc.vector.tensor_tensor(dst[:, at, 0, :], src[:, 0:2 * C].rearrange("p (h n) -> p h n", h=2),
                                                            mask, ALU.mult).then_inc(dve_read, 1)
                    for level in range(1, LEVELS + 1):
                        for q in range(4):
                            mask = level_mask[:, d, level - 1, None, :].to_broadcast([P, 4, C])
                            nc.vector.tensor_tensor((X if level > 1 else T)[:, 4 * q:4 * q + 4, :],
                                                    read(("X", level, q))[:].rearrange("p (h n) -> p h n", h=4), mask, ALU.mult
                                                    ).then_inc(dve_read, 1)
                    if lat:
                        for h in range(2):
                            half = slice(4 * h, 4 * h + 4)
                            src = read(("Y", h))[:].rearrange("p (h n) -> p h n", n=C)
                            if d:
                                ins = nc.vector.tensor_tensor(y_acc[:, half, tok], y_acc[:, half, tok], src, ALU.add)
                            else:
                                ins = nc.vector.tensor_copy(y_acc[:, half, tok], src)
                            ins.then_inc(dve_read, 1)
                    nc.vector.tensor_tensor(S_sum[:], read(("S",))[:].rearrange("p (h n) -> p h n", n=HD), S_mid[:], ALU.add
                                            ).then_inc(dve_read, 1)
                    dve.wait_ge(dve_read, base["dve"] + (i + 1) * per_chunk["dve"] + 1)
                    end = 0 if d else C - 1
                    c.ordered(nc.vector.tensor_tensor(S[:], S_sum[:], w_r[:, :, end, None].to_broadcast([P, PAIRS, HD]), ALU.mult))
                    assert c.n == V_STEPS[lat], c.n

        @block.tensor
        def _(pe):
            pe.wait_ge(v_step, 2)
            for d, lat, count, base in Loops():
                bank_of, count_at, per_chunk = tables[lat]
                with pe.Fori(0, count) as i:
                    n = base["n"] + i

                    def fill(name):
                        return banks[bank_of[name]]

                    def wait_act(name):
                        pe.wait_ge(act_read, base["act"] + i * per_chunk["act"] + count_at[name] + 1)

                    def wait_dve(name):
                        pe.wait_ge(dve_read, base["dve"] + i * per_chunk["dve"] + count_at[name] + 1)

                    pe.wait_ge(act_read, base["act"] + i * per_chunk["act"] + 1)
                    pe.wait_ge(dve_read, base["dve"] + i * per_chunk["dve"] + 1)
                    rows = slice(d * HD, (d + 1) * HD)
                    pe.wait_ge(tanh_done, n + 1)
                    for kind, wt, src in (("zw", w2, tw[rows, :]), ("za", a2, lora[rows, 1, :])):
                        for h in range(2):
                            out = fill((kind, h))
                            for q in range(4):
                                p = 4 * h + q
                                ins = nc.tensor.matmul(out[:, q * C:(q + 1) * C], wt[rows, p * P:(p + 1) * P], src, start=True, stop=True)
                            ins.then_inc(filled_act, 1)
                    pe.wait_ge(sq_ready, n + 1)
                    for h in range(2):
                        nc.tensor.matmul(fill(("norm", h))[:], ones[:], sq[:, 4 * h:4 * h + 4, :], start=True, stop=True).then_inc(filled_dve, 1)
                    if lat:
                        pe.wait_ge(rk_ready, base["lat"] + i + 1)
                        for h in range(2):
                            nc.tensor.matmul(fill(("bonus", h))[:], ones[:], rk[:, 4 * h:4 * h + 4, :], start=True, stop=True
                                             ).then_inc(filled_dve, 1)
                    pe.wait_ge(tilde_ready, n + 1)
                    for kind, src in (("bT", Bt), ("kT", Kt), ("vT", v)):
                        for h in range(2):
                            out = fill((kind, h))
                            for q in range(4):
                                ins = nc.tensor.transpose(out[:, q * C:(q + 1) * C], src[:, 4 * h + q, :], ident[:])
                            ins.then_inc(filled_act, 1)
                    width = 2 if lat else 1
                    for q in range(4):
                        if q == 0:
                            wait_act(("bT", 1))
                        elif q == 1:
                            wait_act(("vT", 1))
                        else:
                            wait_dve(("Mk", q - 2, 1))
                        for m, src in (("Mb", Bt), ("Mk", Kt)):
                            for s in range(2):
                                out = fill((m, q, s))
                                half = slice(s * HD, (s + 1) * HD)
                                for pp in range(2):
                                    p = 2 * q + pp
                                    ins = nc.tensor.matmul(out[:, pp * width * C:(pp + 1) * width * C], src[half, p, :],
                                                           AR[half, p, 0:width, :], start=True, stop=True)
                                ins.then_inc(filled_dve, 1)
                    for level in range(1, LEVELS + 1):
                        for q in range(4):
                            if level == 1:
                                wait_dve(("Mk", 2 if q < 3 else 3, 1))
                            elif level > 2:
                                wait_act(("T", level - 1, q))
                            out = fill(("X", level, q))
                            nc.tensor.matmul(out[:], ident_b[:], ident_b[:, None, :].to_broadcast([P, 4, P]), start=True, stop=False)
                            for j in range(4):
                                sl = 4 * q + j
                                ins = nc.tensor.matmul(out[:, j * C:(j + 1) * C], Mb[:, sl, 0, :],
                                                       ident[:] if level == 1 else T[:, sl, :], start=False, stop=j == 3)
                            ins.then_inc(filled_dve, 1)
                        x = X if level > 1 else T
                        for q in range(4):
                            if level > 1 and q == 0:
                                wait_act(("Tt", level - 1, 3))
                            wait_dve(("X", level, q))
                            if 1 < level < LEVELS:
                                out = fill(("T", level, q))
                                for j in range(4):
                                    sl = 4 * q + j
                                    ins = nc.tensor.matmul(out[:, j * C:(j + 1) * C], Tt[:, sl, :], x[:, sl, :], start=True, stop=True)
                                ins.then_inc(filled_act, 1)
                            out = fill(("Tt", level, q))
                            for j in range(4):
                                sl = 4 * q + j
                                ins = nc.tensor.matmul(out[:, j * C:(j + 1) * C], x[:, sl, :], ident[:] if level == 1 else Tt[:, sl, :],
                                                       start=True, stop=True)
                            ins.then_inc(filled_act, 1)
                    pe.wait_ge(state_ready, n + 1)
                    heads = [(h, q, s) for h in range(2) for q in range(4) for s in range(2)]
                    for s, p in [(s, p) for s in range(2) for p in range(PAIRS)]:
                        half, at = slice(s * HD, (s + 1) * HD), slice(p * HD, (p + 1) * HD)
                        if p == 0:
                            out = fill(("rhs", s))
                        nc.tensor.matmul(out[:, at], Mk[:, slot(p, s), 0, :], VT[:, p * P + s * HD:p * P + (s + 1) * HD], start=True, stop=False)
                        ins = nc.tensor.matmul(out[:, at], AR[half, p, 0, :], S_mid[half, p, :], start=False, stop=True)
                        if p == PAIRS - 1:
                            ins.then_inc(filled_act, 1)
                    for h, q, s in heads:
                        p, at = 4 * h + q, slice(q * P + s * HD, q * P + (s + 1) * HD)
                        if (q, s) == (0, 0):
                            if h == 0:
                                wait_act(("rhs", 1))
                            out = fill(("U", h))
                        ins = nc.tensor.matmul(out[:, at], Tt[:, slot(p, s), :], rhs[:, p * P + s * HD:p * P + (s + 1) * HD], start=True, stop=True)
                        if (q, s) == (3, 1):
                            ins.then_inc(filled_act, 1)
                    if lat:
                        for h, q, s in heads:
                            p, half, at = 4 * h + q, slice(s * HD, (s + 1) * HD), slice(q * C, (q + 1) * C)
                            col = slice(p * P + s * HD, p * P + (s + 1) * HD)
                            if (q, s) == (0, 0):
                                wait_act(("U", h))
                                out = fill(("Y", h))
                            nc.tensor.matmul(out[half, at], VT[:, col], Mk[:, slot(p, s), 1, :], start=True, stop=False)
                            nc.tensor.matmul(out[half, at], U[:, col], Mb[:, slot(p, s), 1, :], start=False, stop=False)
                            ins = nc.tensor.matmul(out[half, at], S_mid[half, p, :], AR[half, p, 1, :], start=False, stop=True)
                            if (q, s) == (3, 1):
                                ins.then_inc(filled_dve, 1)
                    if not lat:
                        wait_act(("U", 1))
                    out = fill(("S",))
                    for h, q, s in heads:
                        p, half = 4 * h + q, slice(s * HD, (s + 1) * HD)
                        col = slice(p * P + s * HD, p * P + (s + 1) * HD)
                        nc.tensor.matmul(out[half, p * HD:(p + 1) * HD], BT[:, col], U[:, col], start=True, stop=False)
                        ins = nc.tensor.matmul(out[half, p * HD:(p + 1) * HD], KTT[:, col], VT[:, col], start=False, stop=True)
                    ins.then_inc(filled_dve, 1)


def rwkv_out(nc, e, a, y_acc, bonus, ones, vec):
    with ExitStack() as ctx:
        sb = lambda n, s, d=FP32: ctx.enter_context(nc.sbuf_tensor("ro_" + n, s, d))
        gd, g2 = sb("gd", [P, 2, LAT]), sb("g2", [P, 2, LRU])
        yc, sq, rstd = ([sb(f"{n}{b}", [P, LAT]) for b in range(2)] for n in ("yc", "sq", "rstd"))
        eps = sb("eps", [P, 1])
        psum = lambda n: [ctx.enter_context(nc.psum_tensor(f"ro_{n}{b}", [P, LAT], FP32)) for b in range(2)]
        mean, var, gate = psum("mean"), psum("var"), psum("gate")
        loaded, gd_ready, eps_ready, summed, centred, squared, var_done, rstd_done, gate_done, finished, stored, a_step, v_step = sems(
            nc, ctx, "ro_loaded", "gd_ready", "ro_eps_ready", "ro_summed", "ro_centred", "ro_squared", "ro_var_done", "ro_rstd_done",
            "ro_gate_done", "ro_finished", "ro_stored", "ro_a_step", "ro_v_step")
        rest = 32
        with nc.Block() as block:
            @block.sync
            def _(sp):
                sp.dma_start(gd[:], e.p_dram[GD0:GD0 + 2].rearrange("t p n -> p t n")[:, :, LAT0:]).then_inc(loaded, 16)
                sp.dma_start(g2[:], a["rwkv_g2"]).then_inc(loaded, 16)
                sp.wait_ge(finished, PAIRS)
                sp.dma_start(e.merged_dram[LT:].rearrange("t p n -> p t n"), y_acc[:]).then_inc(stored, 16)
                sp.wait_ge(stored, 16)

            @block.tensor
            def _(pe):
                for p in range(PAIRS):
                    b = p % 2
                    if p >= 2:
                        pe.wait_ge(finished, p - 1)
                    nc.tensor.matmul(mean[b][:], ones[:], y_acc[:, p, :], start=True, stop=True).then_inc(summed, 1)
                    if p == 0:
                        pe.wait_ge(gd_ready, 1)
                    nc.tensor.matmul(gate[b][:], g2[:, 0, p * P:(p + 1) * P], gd[:, 0, :], start=True, stop=False)
                    nc.tensor.matmul(gate[b][:], g2[0:rest, 1, p * P:(p + 1) * P], gd[0:rest, 1, :], start=False, stop=True
                                     ).then_inc(gate_done, 1)
                    pe.wait_ge(squared, p + 1)
                    nc.tensor.matmul(var[b][:], ones[:], sq[b][:], start=True, stop=True).then_inc(var_done, 1)

            @block.scalar
            def _(act):
                act.wait_ge(loaded, 32)
                nc.scalar.activation(gd[:], gd[:], ACT.Sigmoid).then_inc(gd_ready, 1)
                act.wait_ge(eps_ready, 1)
                for p in range(PAIRS):
                    b = p % 2
                    act.wait_ge(var_done, p + 1)
                    nc.scalar.activation(rstd[b][:], var[b][:], ACT.Ln, bias=eps[:], scale=1.0 / HD).then_inc(a_step, 1)
                    act.wait_ge(a_step, p + 1)
                    nc.scalar.activation(rstd[b][:], rstd[b][:], ACT.Exp, scale=-0.5).then_inc(rstd_done, 1)

            @block.vector
            def _(dve):
                nc.vector.memset(eps[:], GN_EPS).then_inc(eps_ready, 1)
                c = Chain(dve, v_step)
                for p in range(PAIRS):
                    b = p % 2
                    y = y_acc[:, p, :]
                    dve.wait_ge(summed, p + 1)
                    c.ordered(nc.vector.scalar_tensor_tensor(out=yc[b][:], in0=mean[b][:], scalar=-1.0 / HD, in1=y, op0=ALU.mult, op1=ALU.add))
                    nc.vector.tensor_tensor(sq[b][:], yc[b][:], yc[b][:], ALU.mult).then_inc(squared, 1)
                    dve.wait_ge(rstd_done, p + 1)
                    c.ordered(nc.vector.tensor_tensor(yc[b][:], yc[b][:], rstd[b][:], ALU.mult))
                    c.ordered(nc.vector.tensor_scalar(yc[b][:], yc[b][:], vec[:, 7, p:p + 1], vec[:, 8, p:p + 1], ALU.mult, ALU.add))
                    c.ordered(nc.vector.tensor_tensor(yc[b][:], yc[b][:], bonus[:, p, :], ALU.add))
                    dve.wait_ge(gate_done, p + 1)
                    nc.vector.tensor_tensor(y, yc[b][:], gate[b][:], ALU.mult).then_inc(finished, 1)


def residual_input(nc, e, a, z, hi, lo):
    with ExitStack() as ctx:
        sb = lambda n, s, d=FP32: ctx.enter_context(nc.sbuf_tensor("ri_" + n, s, d))
        rows, cols = sb("rows", [P, KT // 2, 8]), sb("cols", [P, KT // 2, 64])
        merged = [sb(f"merged{b}", [P, 4, LAT]) for b in range(2)]
        x_loaded, hi_done, lo_done, posed, scaled = sems(nc, ctx, "ri_x_loaded", "ri_hi_done", "ri_lo_done", "ri_posed", "ri_scaled")
        loaded = sems(nc, ctx, "ri_merged0_loaded", "ri_merged1_loaded")
        with nc.Block() as block:
            @block.sync
            def _(sp):
                sp.dma_start(rows[:], a["pos_rows"]).then_inc(x_loaded, 16)
                sp.dma_start(cols[:], a["pos_cols"]).then_inc(x_loaded, 16)
                sp.dma_start(z[:], a["x"].rearrange("t p n -> p t n")).then_inc(x_loaded, 16)
                for q in range(4):
                    if q >= 2:
                        sp.wait_ge(hi_done, q - 1)
                        sp.wait_ge(lo_done, q - 1)
                    sp.dma_start(merged[q % 2][:], e.merged_dram[4 * q:4 * q + 4].rearrange("t p n -> p t n")).then_inc(loaded[q % 2], 16)

            @block.scalar
            def _(act):
                for q in range(4):
                    act.wait_ge(loaded[q % 2], 16 * (q // 2 + 1))
                    nc.scalar.activation(hi[:, 4 * q:4 * q + 4, :], merged[q % 2][:], ACT.Copy).then_inc(hi_done, 1)

            @block.vector
            def _(dve):
                for q in range(4):
                    dve.wait_ge(hi_done, q + 1)
                    at = slice(4 * q, 4 * q + 4)
                    nc.vector.tensor_tensor(lo[:, at, :], merged[q % 2][:], hi[:, at, :].bitcast(FP32), ALU.subtract).then_inc(lo_done, 1)
                dve.wait_ge(x_loaded, 48)
                for k in range(KT):
                    table = (rows[:, k, :, None].to_broadcast([P, 8, 64]) if k < KT // 2
                             else cols[:, k - KT // 2, None, :].to_broadcast([P, 8, 64]))
                    grid = z[:, k, :].rearrange("p (r c) -> p r c", c=64)
                    ins = nc.vector.tensor_tensor(grid, grid, table, ALU.add)
                ins.then_inc(posed, 1)
                dve.wait_ge(posed, 1)
                nc.vector.tensor_scalar(z[:], z[:], ALPHA, None, ALU.mult).then_inc(scaled, 1)
                dve.wait_ge(scaled, 1)


def layer_norm(nc, a, name, z, gain, bias, finish):
    with ExitStack() as ctx:
        sb = lambda n, s, d=FP32: ctx.enter_context(nc.sbuf_tensor(name + n, s, d))
        mean_of = sb("mean_of", [P, P])
        eps, rstd = sb("eps", [P, 1]), sb("rstd", [P, LAT])
        sq = [sb(f"sq{b}", [P, LAT]) for b in range(2)]
        mean, var = (ctx.enter_context(nc.psum_tensor(name + n, [P, LAT], FP32)) for n in ("mean", "var"))
        const, mean_done, centred, squared, sq_used, var_done, rstd_done, scaled, normed, a_step, g_loaded = sems(
            nc, ctx, *(name + n for n in ("const", "mean_done", "centred", "squared", "sq_used", "var_done", "rstd_done", "scaled",
                                          "normed", "a_step", "g_loaded")))
        gb = sb("gain_bias", [P, 2, KT])
        on_act, on_dve, on_sp = finish(ctx, sb, normed)
        with nc.Block() as block:
            @block.sync
            def _(sp):
                sp.dma_start(gb[:, 0, :], gain).then_inc(g_loaded, 16)
                sp.dma_start(gb[:, 1, :], bias).then_inc(g_loaded, 16)
                on_sp(sp)

            @block.tensor
            def _(pe):
                pe.wait_ge(const, 1)
                for k in range(KT):
                    ins = nc.tensor.matmul(mean[:], mean_of[:], z[:, k, :], start=(k == 0), stop=(k == KT - 1))
                ins.then_inc(mean_done, 1)
                for k in range(KT):
                    pe.wait_ge(squared, k + 1)
                    nc.tensor.matmul(var[:], mean_of[:], sq[k % 2][:], start=(k == 0), stop=(k == KT - 1)).then_inc(sq_used, 1)

            @block.scalar
            def _(act):
                for k in range(KT):
                    act.wait_ge(centred, k + 1)
                    if k >= 2:
                        act.wait_ge(sq_used, k - 1)
                    nc.scalar.activation(sq[k % 2][:], z[:, k, :], ACT.Square).then_inc(squared, 1)
                act.wait_ge(sq_used, KT)
                nc.scalar.activation(rstd[:], var[:], ACT.Ln, bias=eps[:]).then_inc(a_step, 1)
                act.wait_ge(a_step, 1)
                nc.scalar.activation(rstd[:], rstd[:], ACT.Exp, scale=-0.5).then_inc(rstd_done, 1)
                on_act(act)

            @block.vector
            def _(dve):
                nc.vector.memset(mean_of[:], 1.0 / D)
                nc.vector.memset(eps[:], LN_EPS).then_inc(const, 1)
                dve.wait_ge(mean_done, 1)
                for k in range(KT):
                    nc.vector.tensor_tensor(z[:, k, :], z[:, k, :], mean[:], ALU.subtract).then_inc(centred, 1)
                dve.wait_ge(rstd_done, 1)
                dve.wait_ge(g_loaded, 32)
                for k in range(KT):
                    nc.vector.tensor_tensor(z[:, k, :], z[:, k, :], rstd[:], ALU.mult).then_inc(scaled, 1)
                    if k:
                        dve.wait_ge(scaled, k)
                        nc.vector.tensor_scalar(z[:, k - 1, :], z[:, k - 1, :], gb[:, 0, k - 1:k], gb[:, 1, k - 1:k], ALU.mult, ALU.add
                                                ).then_inc(normed, 1)
                        if k >= 2:
                            on_dve(dve, k - 2)
                dve.wait_ge(scaled, KT)
                nc.vector.tensor_scalar(z[:, KT - 1, :], z[:, KT - 1, :], gb[:, 0, KT - 1:KT], gb[:, 1, KT - 1:KT], ALU.mult, ALU.add
                                        ).then_inc(normed, 1)
                on_dve(dve, KT - 2)
                on_dve(dve, KT - 1)


def out_projection(nc, e, a):
    with ExitStack() as ctx:
        sb = lambda n, s, d=FP32: ctx.enter_context(nc.sbuf_tensor(n, s, d))
        z = sb("z1", [P, KT, LAT])
        with ExitStack() as inner:
            hi, lo = e.h_hi, e.h_lo
            landing = [inner.enter_context(nc.sbuf_tensor(f"o_landing{b}", [P, LAT], FP32)) for b in range(2)]
            residual_input(nc, e, a, z, hi, lo)

            def add(dve, unit, b):
                at = bass.ds(unit, 1)
                zt = z[:, at, :].rearrange("p o n -> p (o n)")
                return nc.vector.scalar_tensor_tensor(out=zt, in0=landing[b][:], scalar=e.mod[:, bass.ds(unit + 2 * KT, 1), 0],
                                                      in1=zt, op0=ALU.mult, op1=ALU.add)

            projection(nc, "o_", a["w_out"], 0, KT, hi, lo, [(0, LAT, 0)], add, landing, None)

        def finish(ctx, sb, normed):
            h2 = [sb(f"h2{b}", [P, LAT]) for b in range(2)]
            modded, hi_done, lo_done, stored = sems(nc, ctx, "h2_modded", "h2_hi_done", "h2_lo_done", "x1_stored")

            def on_dve(dve, k):
                dve.wait_ge(normed, k + 1)
                nc.vector.tensor_scalar(h2[k % 2][:], z[:, k, :], e.one_plus_scale2[:, k:k + 1], e.mod[:, 3 * KT + k, 0:1], ALU.mult, ALU.add
                                        ).then_inc(modded, 1)
                dve.wait_ge(hi_done, k + 1)
                nc.vector.tensor_tensor(e.h_lo[:, k, :], h2[k % 2][:], e.h_hi[:, k, :].bitcast(FP32), ALU.subtract).then_inc(lo_done, 1)

            def on_act(act):
                for k in range(KT):
                    act.wait_ge(modded, k + 1)
                    nc.scalar.activation(e.h_hi[:, k, :], h2[k % 2][:], ACT.Copy).then_inc(hi_done, 1)

            def on_sp(sp):
                sp.wait_ge(normed, KT)
                sp.dma_start(e.x1_dram, z[:]).then_inc(stored, 16)
                sp.wait_ge(stored, 16)

            return on_act, on_dve, on_sp

        layer_norm(nc, a, "ln1_", z, a["ln1_g"], a["ln1_b"], finish)


def queries(nc, e, a):
    with ExitStack() as ctx:
        landing = [ctx.enter_context(nc.sbuf_tensor(f"q_landing{b}", [P, LAT], FP32)) for b in range(2)]
        q = [ctx.enter_context(nc.sbuf_tensor(f"q_out{b}", [P, LAT], FP32)) for b in range(2)]

        def copy(dve, unit, b):
            return nc.vector.tensor_copy(q[b][:], landing[b][:])

        def store(eng, unit, b):
            return eng.dma_start(e.q_dram[bass.ds(unit, 1)].rearrange("o p n -> p (o n)"), q[b][:])

        projection(nc, "q_", a["peer_wq"], 0, KT, e.h_hi, e.h_lo, [(0, LAT, 0)], copy, landing, store)


R_STEPS = 21
ONE_HOTS = 8
SPREAD = 16
BANKFUL = 4


def route(nc, e, a):
    with ExitStack() as ctx:
        sb = lambda n, s, d=FP32: ctx.enter_context(nc.sbuf_tensor("rt_" + n, s, d))
        keys, q = sb("keys", [P, HP, NK]), sb("q", [P, HP, P])
        ident, iota = sb("ident", [P, P]), sb("iota", [P, P])
        score, rest = sb("score", [P, HP, NK]), sb("rest", [P, HP, NK])
        one_of = score
        val, idx, idx_f = sb("val", [P, HP, TOPK]), sb("idx", [P, HP, TOPK], U32), sb("idx_f", [P, HP, TOPK])
        top, pos = sb("top", [P, PEER_HEADS, TOPK]), sb("pos", [P, PEER_HEADS, TOPK], U32)
        k12, k12_f = sb("k12", [P, 2, P], U32), sb("k12_f", [P, 2, P])
        chosen = sb("chosen", [P, 3, P])
        total, landed = sb("total", [P, PEER_HEADS]), sb("landed", [P, 1])
        sel = sb("sel", [P, 3, P])
        now = [sb(f"now{b}", [P, 3, SPREAD]) for b in range(2)]
        hot1, hot2 = ([sb(f"{n}{b}", [P, NK]) for b in range(ONE_HOTS)] for n in ("hot1_", "hot2_"))
        dense = sb("dense", [P, NK, P])
        s_acc = [ctx.enter_context(nc.psum_tensor(f"rt_s{b}", [P, 4 * NK], FP32)) for b in range(2)]
        t_acc = ctx.enter_context(nc.psum_tensor("rt_t", [P, 3 * P], FP32))
        g_acc = [ctx.enter_context(nc.psum_tensor(f"rt_g{b}", [P, BANKFUL * NK], FP32)) for b in range(4)]
        (const_loaded, q_loaded, scored, score_read, shifted, exp_done, chosen_ready, turned, sel_ready, sel_used, hot_ready, hot_used,
         dense_free, bank_read, stored, v_step) = sems(
            nc, ctx, "rt_const_loaded", "rt_q_loaded", "scored", "score_read", "top_shifted", "top_exp_done", "chosen_ready", "turned",
            "sel_ready", "sel_used", "hot_ready", "hot_used", "dense_free", "gate_bank_read", "gates_stored", "rt_v_step")
        tiles, turns, fills = LAT // P, P // SPREAD, P // BANKFUL
        per_turn = SPREAD // BANKFUL
        with nc.Block() as block:
            @block.sync
            def _(sp):
                sp.sem_inc(dense_free, 1)
                for dst, src in ((keys, a["peer_keys"]), (ident, a["ident"]), (iota, a["iota"])):
                    sp.dma_start(dst[:], src).then_inc(const_loaded, 16)
                with sp.Fori(0, tiles) as t:
                    at = bass.ds(t * P, P)
                    sp.wait_ge(scored, 4 * t + 1)
                    sp.dma_start(q[:], e.q_dram.rearrange("t p n -> p t n")[:, :, at]).then_inc(q_loaded, 16)
                    sp.wait_ge(bank_read, (t + 1) * fills + 4)
                    sp.dma_start(e.gates_dram[:, :, at], dense[:]).then_inc(stored, 16)
                    sp.wait_ge(stored, 16 * t + 16)
                    sp.sem_inc(dense_free, 1)

            @block.tensor
            def _(pe):
                pe.sem_inc(hot_used, ONE_HOTS)
                pe.sem_inc(scored, 1)
                pe.sem_inc(turned, 1)
                pe.wait_ge(const_loaded, 48)
                with pe.Fori(0, tiles) as t:
                    pe.wait_ge(q_loaded, 16 * t + 16)
                    for g in range(4):
                        pe.wait_ge(score_read, 4 * t + g + 1)
                        for j in range(4):
                            last = nc.tensor.matmul(s_acc[g % 2][:, j * NK:(j + 1) * NK], q[:, 4 * g + j, :], keys[:, 4 * g + j, :],
                                                    start=True, stop=True)
                        last.then_inc(scored, 1)
                    pe.wait_ge(chosen_ready, t + 2)
                    pe.wait_ge(sel_ready, t + 1)
                    for j in range(3):
                        last = nc.tensor.transpose(t_acc[:, j * P:(j + 1) * P], chosen[:, j, :], ident[:])
                    last.then_inc(turned, 1)
                    with pe.Fori(0, turns) as i:
                        turn = pe.snap(t * turns + i)
                        for n in range(SPREAD):
                            if n % BANKFUL == 0:
                                pe.wait_ge(bank_read, turn * per_turn + n // BANKFUL + 1)
                            pe.wait_ge(hot_ready, turn * SPREAD + n + 1)
                            ins = nc.tensor.matmul(g_acc[n // BANKFUL % 4][:, (n % BANKFUL) * NK:(n % BANKFUL + 1) * NK],
                                                   hot1[n % ONE_HOTS][:], hot2[n % ONE_HOTS][:], start=True, stop=True)
                            ins.then_inc(hot_used, 1)

            @block.scalar
            def _(act):
                act.sem_inc(score_read, 2)
                act.sem_inc(sel_ready, 1)
                act.sem_inc(bank_read, 4)
                with act.Fori(0, tiles) as t:
                    for g in range(4):
                        act.wait_ge(scored, 4 * t + g + 2)
                        if g == 0:
                            act.wait_ge(chosen_ready, t + 1)
                        nc.scalar.activation(score[:, 4 * g:4 * g + 4, :].rearrange("p h n -> p (h n)"), s_acc[g % 2][:], ACT.Copy
                                             ).then_inc(score_read, 1)
                    act.wait_ge(shifted, t + 1)
                    nc.scalar.activation(chosen[:, 2, :], top[:].rearrange("p h k -> p (h k)"), ACT.Exp).then_inc(exp_done, 1)
                    act.wait_ge(turned, t + 2)
                    act.wait_ge(sel_used, turns * t + 1)
                    nc.scalar.activation(sel[:].rearrange("p a n -> p (a n)"), t_acc[:], ACT.Copy).then_inc(sel_ready, 1)
                    act.wait_ge(dense_free, t + 1)
                    with act.Fori(0, turns) as i:
                        turn = act.snap(t * turns + i)
                        for f in range(per_turn):
                            act.wait_ge(hot_used, turn * SPREAD + (f + 1) * BANKFUL + ONE_HOTS)
                            at = bass.ds(i * SPREAD + f * BANKFUL, BANKFUL)
                            nc.scalar.activation(dense[:, :, at].rearrange("p i t -> p t i"),
                                                 g_acc[f % 4][:].rearrange("p (t i) -> p t i", i=NK), ACT.Copy).then_inc(bank_read, 1)

            @block.vector
            def _(dve):
                dve.sem_inc(chosen_ready, 1)
                dve.sem_inc(sel_used, 1)
                dve.wait_ge(const_loaded, 48)
                with dve.Fori(0, tiles) as t:
                    c = Chain(dve, v_step, t * R_STEPS)

                    def best(vals, positions, source, other, n):
                        for half in range(2):
                            at = slice(8 * half, 8 * half + 8)
                            src = other if half else source
                            nc.vector.tensor_copy(landed[:], iota[:, 0:1])
                            for r in range(n):
                                ins = nc.vector.max(vals[:, r, at], src[:, r, :])
                            c.ordered(ins)
                            nc.vector.tensor_copy(landed[:], iota[:, 0:1])
                            for r in range(n):
                                ins = nc.vector.max_index(positions[:, r, at], vals[:, r, at], src[:, r, :])
                            if not half:
                                for r in range(n):
                                    ins = nc.vector.match_replace(other[:, r, :], vals[:, r, at], src[:, r, :], LOWEST)
                            c.ordered(ins)

                    dve.wait_ge(score_read, 4 * t + 6)
                    best(val, idx, score, rest, HP)
                    c.ordered(nc.vector.tensor_copy(idx_f[:], idx[:]))
                    halves = val[:].rearrange("p (h s) k -> p h s k", s=2)
                    cand = score[:].rearrange("p (h s) n -> p h (s n)", s=2)
                    left = rest[:].rearrange("p (h s) n -> p h (s n)", s=2)
                    full = [P, PEER_HEADS, TOPK, TOPK]
                    c.ordered(nc.vector.tensor_tensor(cand.rearrange("p h (i j) -> p h i j", j=TOPK), halves[:, :, 0, :, None].to_broadcast(full),
                                                      halves[:, :, 1, None, :].to_broadcast(full), ALU.add))
                    best(top, pos, cand, left, PEER_HEADS)
                    flat_pos = pos[:].rearrange("p h k -> p (h k)")
                    nc.vector.tensor_scalar(k12[:, 0, :], flat_pos, 4, None, ALU.logical_shift_right)
                    nc.vector.tensor_scalar(k12[:, 1, :], flat_pos, 15, None, ALU.bitwise_and)
                    best_of = total[:]
                    c.ordered(nc.vector.tensor_copy(best_of, top[:, :, 0]))
                    c.ordered(nc.vector.tensor_copy(k12_f[:], k12[:]))
                    dve.wait_ge(turned, t + 1)
                    nc.vector.tensor_tensor(top[:], top[:], best_of[:, :, None].to_broadcast([P, PEER_HEADS, TOPK]), ALU.subtract
                                            ).then_inc(shifted, 1)
                    by_half = idx_f[:].rearrange("p (h s) k -> p h s k", s=2)
                    for s in range(2):
                        one = one_of[:].rearrange("p h n -> p (h n)").rearrange("p (k j) -> p k j", j=TOPK)
                        c.ordered(nc.vector.tensor_tensor(one, iota[:, None, 0:TOPK].to_broadcast([P, P, TOPK]),
                                                          k12_f[:, s, :, None].to_broadcast([P, P, TOPK]), ALU.is_equal))
                        four = one.rearrange("p (h k) j -> p h k j", h=PEER_HEADS)
                        c.ordered(nc.vector.tensor_tensor(four, four, by_half[:, :, s, None, :].to_broadcast(full), ALU.mult))
                        c.ordered(nc.vector.tensor_reduce(chosen[:, s, :], one, AX, ALU.add))
                    dve.wait_ge(exp_done, t + 1)
                    gate = chosen[:, 2, :].rearrange("p (h k) -> p h k", k=TOPK)
                    c.ordered(nc.vector.tensor_reduce(total[:], gate, AX, ALU.add))
                    c.ordered(nc.vector.reciprocal(total[:], total[:]))
                    c.ordered(nc.vector.tensor_tensor(gate, gate, total[:, :, None].to_broadcast([P, PEER_HEADS, TOPK]), ALU.mult))
                    dve.sem_inc(chosen_ready, 1)
                    assert c.n == R_STEPS, c.n
                    with dve.Fori(0, turns // 2) as i:
                        for half in range(2):
                            turn = t * turns + 2 * i + half
                            cur = now[half]
                            if half == 0:
                                dve.wait_ge(sel_ready, t + 2)
                            nc.vector.tensor_copy(cur[:], sel[:, :, bass.ds((2 * i + half) * SPREAD, SPREAD)]).then_inc(sel_used, 1)
                            dve.wait_ge(sel_used, turn + 2)
                            for n in range(SPREAD):
                                dve.wait_ge(hot_used, turn * SPREAD + n + 1)
                                nc.vector.tensor_scalar(hot1[n % ONE_HOTS][:], iota[:], cur[:, 0, n:n + 1], cur[:, 2, n:n + 1],
                                                        ALU.is_equal, ALU.mult)
                                nc.vector.tensor_scalar(hot2[n % ONE_HOTS][:], iota[:], cur[:, 1, n:n + 1], None, ALU.is_equal
                                                        ).then_inc(hot_ready, 1)


def experts(nc, e, a, f):
    chunks, v_units = NK, D // DU
    groups, units = chunks // GROUP, GROUP + v_units
    with ExitStack() as ctx:
        sb = lambda n, s, d=FP32: ctx.enter_context(nc.sbuf_tensor("ex_" + n, s, d))
        raw = [sb(f"raw{b}", [P, KT * P]) for b in range(2)]
        hi, lo = ([sb(f"{n}{b}", [P, KT * P], FP32R) for b in range(2)] for n in ("hi", "lo"))
        w_hi, w_lo = (sb(n, [P, GROUP, LAT], FP32R) for n in ("w_hi", "w_lo"))
        gates, act_, w = ([sb(f"{n}{b}", [P, LAT]) for b in range(2)] for n in ("gates", "act", "w"))
        u_acc = [ctx.enter_context(nc.psum_tensor(f"ex_u{b}", [P, LAT], FP32)) for b in range(2)]
        v_acc = [[ctx.enter_context(nc.psum_tensor(f"ex_v{b}{h}", [P, LAT], FP32)) for h in range(2)] for b in range(2)]
        hi_done, lo_done, products, gelu_done, weighted, w_ready, added, w_step, gates_free = sems(
            nc, ctx, "ex_hi_done", "ex_lo_done", "ex_products", "gelu_ready", "act_weighted", "w_ready", "v_added", "w_step", "gates_free")
        loaded = sems(nc, ctx, "ex_raw0_loaded", "ex_raw1_loaded")
        g_loaded = sems(nc, ctx, "gates0_loaded", "gates1_loaded")
        assert units % 2 == 0 and GROUP % 2 == 0
        with nc.Block() as block:
            @block.sync
            def _(sp):
                with sp.Fori(0, groups) as g:
                    for u in range(units):
                        sp.wait_ge(hi_done, g * units + u + 1)
                        sp.wait_ge(lo_done, g * units + u + 1)
                        src = (a["peer_u"][bass.ds(g * GROUP + u, 1)] if u < GROUP
                               else a["peer_v"][bass.ds(g * v_units + (u - GROUP), 1)])
                        sp.dma_start(raw[u % 2][:], src.rearrange("o p n -> p (o n)")).then_inc(loaded[u % 2], 16)

            @block.gpsimd
            def _(pool):
                with pool.Fori(0, groups) as g:
                    for c in range(GROUP):
                        pool.wait_ge(weighted, g * GROUP + c + 1)
                        pool.dma_start(gates[c % 2][:], e.gates_dram[:, bass.ds(g * GROUP + c, 1), :].rearrange("p o n -> p (o n)")
                                       ).then_inc(g_loaded[c % 2], 16)

            @block.scalar
            def _(act):
                act.sem_inc(hi_done, 2)
                with act.Fori(0, groups) as g:
                    for u in range(units):
                        act.wait_ge(loaded[u % 2], (g * (units // 2) + u // 2 + 1) * 16)
                        act.wait_ge(products, g * units + u + 1)
                        nc.scalar.activation(hi[u % 2][:], raw[u % 2][:], ACT.Copy).then_inc(hi_done, 1)
                        if 0 < u <= GROUP:
                            c = u - 1
                            act.wait_ge(products, g * units + c + 3)
                            act.wait_ge(weighted, g * GROUP + c + 1)
                            nc.scalar.activation(act_[c % 2][:], u_acc[c % 2][:], ACT.Gelu).then_inc(gelu_done, 1)

            @block.vector
            def _(dve):
                dve.sem_inc(lo_done, 2)
                dve.sem_inc(weighted, 2)

                def low(g, u):
                    dve.wait_ge(hi_done, g * units + u + 3)
                    nc.vector.tensor_tensor(lo[u % 2][:], raw[u % 2][:], hi[u % 2][:].bitcast(FP32), ALU.subtract).then_inc(lo_done, 1)

                def weigh(g, c):
                    n = g * GROUP + c
                    dve.wait_ge(gelu_done, n + 1)
                    dve.wait_ge(g_loaded[c % 2], (g * (GROUP // 2) + c // 2 + 1) * 16)
                    nc.vector.tensor_tensor(w[c % 2][:], act_[c % 2][:], gates[c % 2][:], ALU.mult).then_inc(weighted, 1)
                    dve.wait_ge(weighted, n + 3)
                    nc.vector.tensor_copy(w_hi[:, c, :], w[c % 2][:]).then_inc(w_step, 1)
                    dve.wait_ge(w_step, n + 1)
                    nc.vector.tensor_tensor(w_lo[:, c, :], w[c % 2][:], w_hi[:, c, :].bitcast(FP32), ALU.subtract).then_inc(w_ready, 1)

                def add(g, v):
                    dve.wait_ge(products, g * units + GROUP + v + 3)
                    for h in range(2):
                        t = f[:, 2 * v + h, :]
                        nc.vector.tensor_tensor(t, t, v_acc[v % 2][h][:], ALU.add).then_inc(added, 1)

                def group(g, last):
                    for u in range(1, units):
                        low(g, u)
                        if u <= GROUP:
                            weigh(g, u - 1)
                        else:
                            add(g, u - GROUP - 1)
                    if not last:
                        low(g + 1, 0)
                    add(g, v_units - 1)

                nc.vector.memset(f[:], 0.0).then_inc(added, 4)
                dve.wait_ge(added, 4)
                low(0, 0)
                with dve.Fori(0, groups - 1) as g:
                    group(g, False)
                group(groups - 1, True)

            @block.tensor
            def _(pe):
                pe.sem_inc(products, 2)

                def three(out, ws, xs, first, last):
                    for n, (wt, x) in enumerate(((ws[0], xs[0]), (ws[0], xs[1]), (ws[1], xs[0]))):
                        ins = nc.tensor.matmul(out, wt, x, start=first and n == 0, stop=last and n == 2)
                    return ins

                with pe.Fori(0, groups) as g:
                    for u in range(units):
                        b = u % 2
                        pe.wait_ge(lo_done, g * units + u + 3)
                        if u < GROUP:
                            pe.wait_ge(gelu_done, g * GROUP + u - 1) if u >= 2 else None
                            for k in range(KT):
                                ks = slice(k * P, (k + 1) * P)
                                ins = three(u_acc[b][:], (hi[b][:, ks], lo[b][:, ks]), (e.h_hi[:, k, :], e.h_lo[:, k, :]), k == 0, k == KT - 1)
                        else:
                            v = u - GROUP
                            for h in range(2):
                                pe.wait_ge(added, (g * v_units + v) * 2 + h + 1)
                                for c in range(GROUP):
                                    if v == 0 and h == 0:
                                        pe.wait_ge(w_ready, g * GROUP + c + 1)
                                    ds = slice(c * DU + h * P, c * DU + (h + 1) * P)
                                    ins = three(v_acc[v % 2][h][:], (hi[b][:, ds], lo[b][:, ds]), (w_hi[:, c, :], w_lo[:, c, :]),
                                                c == 0, c == GROUP - 1)
                        ins.then_inc(products, 1)


def final(nc, e, a, f, out):
    with ExitStack() as ctx:
        x1 = [ctx.enter_context(nc.sbuf_tensor(f"x1_{b}", [P, LAT], FP32)) for b in range(2)]
        scaled, added, step = sems(nc, ctx, "x1_scaled", "x1_added", "gate2_step")
        loaded = sems(nc, ctx, "x1_0_loaded", "x1_1_loaded")
        with nc.Block() as block:
            @block.sync
            def _(sp):
                for k in range(KT):
                    if k >= 2:
                        sp.wait_ge(added, k - 1)
                    sp.dma_start(x1[k % 2][:], e.x1_dram[:, k, :]).then_inc(loaded[k % 2], 16)

            @block.vector
            def _(dve):
                for k in range(KT):
                    nc.vector.tensor_scalar(f[:, k, :], f[:, k, :], e.mod[:, 5 * KT + k, 0:1], None, ALU.mult).then_inc(step, 1)
                for k in range(KT):
                    dve.wait_ge(step, KT)
                    dve.wait_ge(loaded[k % 2], 16 * (k // 2 + 1))
                    nc.vector.scalar_tensor_tensor(out=f[:, k, :], in0=x1[k % 2][:], scalar=ALPHA, in1=f[:, k, :], op0=ALU.mult, op1=ALU.add
                                                   ).then_inc(added, 1)

        def finish(ctx, sb, normed):
            (stored,) = sems(nc, ctx, "out_stored")

            def on_sp(sp):
                for q in range(4):
                    sp.wait_ge(normed, 4 * q + 4)
                    sp.dma_start(out[4 * q:4 * q + 4].rearrange("t p n -> p t n"), f[:, 4 * q:4 * q + 4, :]).then_inc(stored, 16)
                sp.wait_ge(stored, 64)

            return (lambda act: None), (lambda dve, k: None), on_sp

        layer_norm(nc, a, "ln2_", f, a["ln2_g"], a["ln2_b"], finish)


def build(nc, a, out, dbg=None, only=False):
    e = Env()
    with ExitStack() as ctx:
        sb = lambda n, s, d=FP32: ctx.enter_context(nc.sbuf_tensor(n, s, d))
        e.p_dram = nc.dram_tensor("p_scratch", [TILES, P, TW], FP32, kind="Internal").ap()
        e.merged_dram = nc.dram_tensor("merged_scratch", [KT, P, LAT], FP32, kind="Internal").ap()
        e.bias, e.mod = sb("ada_bias", [P, MOD_TILES, 2]), sb("mod", [P, MOD_TILES, 2])
        e.one_plus_scale, e.one_plus_scale2 = sb("one_plus_scale", [P, KT, 2]), sb("one_plus_scale2", [P, KT])
        e.constants = []
        e.x1_dram = nc.dram_tensor("x1_scratch", [P, KT, LAT], FP32, kind="Internal").ap()
        e.q_dram = nc.dram_tensor("q_scratch", [KT, P, LAT], FP32, kind="Internal").ap()
        e.gates_dram = nc.dram_tensor("gates_scratch", [NK, NK, LAT], FP32, kind="Internal").ap()
        if dbg == "tail":
            e.merged_dram = a["merged"]
            with nc.semaphore("dbg_mod") as dm, nc.Block() as block:
                @block.sync
                def _(sp):
                    sp.dma_start(e.mod[:], a["mod"]).then_inc(dm, 16)
                    sp.wait_ge(dm, 16)
                    sp.dma_start(e.one_plus_scale2[:], a["ops2"]).then_inc(dm, 16)
                    sp.wait_ge(dm, 32)
            return tail(nc, e, a, out)
        if only:
            e.p_dram = a["p"]
            {"lru": rglru, "rwkv": rwkv}[dbg](nc, e, a)
            return dump(nc, e.merged_dram[0:LT] if dbg == "lru" else e.merged_dram[LT:], out)
        modulation(nc, e, a)
        if dbg == "mod":
            return dump(nc, e.mod[:].rearrange("p a b -> p (a b)"), out)
        in_projection(nc, e, a)
        if dbg == "p":
            dump(nc, e.p_dram[0:BOTH_TILES], out[0:BOTH_TILES])
            return dump(nc, e.p_dram[BOTH_TILES:, :, LAT0:], out[BOTH_TILES:, :, LAT0:])
        rglru(nc, e, a)
        if dbg == "lru":
            return dump(nc, e.merged_dram[0:LT], out)
        rwkv(nc, e, a)
        tail(nc, e, a, out)


def tail(nc, e, a, out):
    with ExitStack() as ctx:
        with ExitStack() as inner:
            e.h_hi, e.h_lo = (inner.enter_context(nc.sbuf_tensor(n, [P, KT, LAT], FP32R)) for n in ("h_hi", "h_lo"))
            out_projection(nc, e, a)
            queries(nc, e, a)
            route(nc, e, a)
            f = inner.enter_context(nc.sbuf_tensor("f", [P, KT, LAT], FP32))
            experts(nc, e, a, f)
            final(nc, e, a, f, out)


def dump(nc, src, out):
    with nc.semaphore(f"dumped{id(src)}") as s, nc.Block() as block:
        @block.sync
        def _(sp):
            sp.dma_start(out, src).then_inc(s, 16)
            sp.wait_ge(s, 16)


def position_tables():
    quarter = D // 4
    freq = (1.0 / (10000.0 ** (np.arange(quarter, dtype=np.float32) / quarter))).astype(np.float32)

    def table(n):
        ang = (np.arange(n, dtype=np.float32)[:, None] * freq[None, :]).astype(np.float32)
        t = np.concatenate([np.sin(ang), np.cos(ang)], axis=-1).T.astype(np.float32)
        return np.ascontiguousarray(t.reshape(KT // 2, P, n).transpose(1, 0, 2))

    return table(LAT // 64), table(64)


def shape_constants():
    i = np.arange(P)
    row, col = i[:, None], i[None, :]
    f = lambda m: np.asarray(m, np.float32)
    tri = np.stack([np.stack([f(row < col), f(row <= col)], 1), np.stack([f(row > col), f(row >= col)], 1)], 1)
    levels = []
    for d in range(2):
        late, early = (row, col) if d == 0 else (col, row)
        levels.append(np.stack([f((row == col) | ((row >> k == col >> k) & (late >> (k - 1) & 1 == 1) & (early >> (k - 1) & 1 == 0)))
                                for k in range(1, LEVELS + 1)], 1))
    return {"iota": f(0 * row + col), "ident": f(row == col), "rwkv_ones": f(row // HD == col // HD), "rwkv_tri": np.ascontiguousarray(tri),
            "rwkv_level": np.ascontiguousarray(np.stack(levels, 1))}


def weight_tiles(w):
    n = w.shape[1] // P
    return np.ascontiguousarray(w.reshape(KT, P, n, P).transpose(2, 1, 0, 3)).reshape(n, P, KT * P)


def columns(v):
    return np.ascontiguousarray(np.asarray(v).reshape(-1, P).T)


def lay_out(inputs):
    g = {k: np.asarray(v) for k, v in inputs.items()}
    a = {}
    a["cond"] = np.ascontiguousarray(np.stack([columns(g["c"][0]), columns(g["c_ctx"])], axis=-1))
    a["ada_w"] = weight_tiles(g["ada_w"][0]).reshape(MOD_TILES // AW, AW, P, KT * P).transpose(0, 2, 1, 3).copy()
    b = columns(g["ada_b"][0])
    a["ada_b"] = np.ascontiguousarray(np.stack([b, b], axis=-1))
    a["pos_rows"], a["pos_cols"] = position_tables()
    a["ctx"] = np.ascontiguousarray(g["ctx"][0].T).reshape(KT, P, CTX)
    a["x"] = np.ascontiguousarray(g["x"][0].T).reshape(KT, P, LAT)
    w = g["w_in"][0]
    o = 2 * LRU
    r, k, v, lora, gd = o, o + LRU, o + 2 * LRU, o + 3 * LRU, o + 3 * LRU + 2 * P
    order = [w[:, 0:LRU], w[:, k:v], w[:, v:lora], w[:, lora:gd], w[:, LRU:o], w[:, r:k],
             w[:, gd:], np.zeros((D, 2 * P - (w.shape[1] - gd)), w.dtype)]
    a["w_in"] = weight_tiles(np.concatenate(order, axis=1))
    m = g["rwkv_mu"][0]
    z = np.zeros((2, LRU), m.dtype)
    m = np.concatenate([z, m[:, LRU:2 * LRU], m[:, 2 * LRU:3 * LRU], m[:, 3 * LRU:3 * LRU + 2 * P], z, m[:, 0:LRU],
                        m[:, 3 * LRU + 2 * P:], np.zeros((2, 2 * P - (w.shape[1] - gd)), m.dtype)], axis=1)
    a["mu"] = np.ascontiguousarray(np.stack([columns(m[0]), columns(m[1])], axis=-1))
    more_layout(g, a)
    return a


def more_layout(g, a):
    v = [columns(g["lru_conv_w"][0, t]) for t in range(4)] + [columns(g["lru_conv_b"][0])]
    v += [columns(g[n][0, d]) for n in ("lru_ba", "lru_bx", "lru_lambda") for d in range(2)]
    a["lru_vec"] = np.ascontiguousarray(np.stack(v, axis=1))
    for n in ("lru_wa", "lru_wx"):
        a[n] = np.ascontiguousarray(g[n][0].reshape(2 * LT, 2, HD, HD).transpose(1, 2, 0, 3))
    v = [columns(g[n][0, d]) for n in ("rwkv_w0", "rwkv_a0") for d in range(2)]
    v += [columns(g[n][0].reshape(-1)) for n in ("rwkv_k_k", "rwkv_k_a", "rwkv_r_k", "rwkv_gn_g", "rwkv_gn_b")]
    a["rwkv_vec"] = np.ascontiguousarray(np.stack(v, axis=1))
    a["rwkv_w2"], a["rwkv_a2"] = g["rwkv_w2"][0].reshape(P, LRU), g["rwkv_a2"][0].reshape(P, LRU)
    g2 = g["rwkv_g2"][0]
    a["rwkv_g2"] = np.ascontiguousarray(np.concatenate([g2, np.zeros((2 * P - len(g2), LRU), g2.dtype)]).reshape(2, P, LRU).transpose(1, 0, 2))
    a.update(shape_constants())
    a["w_out"], a["peer_wq"] = weight_tiles(g["w_out"][0]), weight_tiles(g["peer_wq"][0])
    for n in ("ln1_g", "ln1_b", "ln2_g", "ln2_b"):
        a[n] = columns(g[n][0])
    a["peer_keys"] = np.ascontiguousarray(g["peer_subkeys"][0].reshape(HP, NK, P).transpose(2, 0, 1))
    a["peer_u"] = np.ascontiguousarray(g["peer_u"][0].reshape(NK, NK, KT, P).transpose(1, 3, 2, 0)).reshape(NK, P, KT * P)
    a["peer_v"] = np.ascontiguousarray(g["peer_v"][0].reshape(NK, NK // GROUP, GROUP, D // DU, DU).transpose(1, 3, 0, 2, 4)
                                       ).reshape(NK, P, GROUP * DU)


_OUT = (KT, P, LAT)


def kernel(**inputs):
    import concourse.bacc as bacc
    from concourse.bass_utils import run_bass_kernel_spmd

    arrays = lay_out(inputs)
    nc = bacc.Bacc("TRN2", target_bir_lowering=False, num_devices=1)
    a = {n: nc.dram_tensor("in_" + n, v.shape, mybir.dt.from_np(v.dtype), kind="ExternalInput").ap() for n, v in arrays.items()}
    out = nc.dram_tensor("out_dram", _OUT, FP32, kind="ExternalOutput").ap()
    build(nc, a, out)
    r = run_bass_kernel_spmd(nc, [{"in_" + n: v for n, v in arrays.items()}], core_ids=[0])
    return np.ascontiguousarray(r.results[0]["out_dram"].reshape(D, LAT).T)[None]
```

```python
from contextlib import ExitStack

import numpy as np
import concourse.bass as bass
from concourse import mybir

FP32 = mybir.dt.float32
FP32R = mybir.dt.float32r
BF16 = mybir.dt.bfloat16
U32 = mybir.dt.uint32
ALU = mybir.AluOpType
ACT = mybir.ActivationFunctionType
AX = mybir.AxisListType.X

P = 128
D = 2048
KT = D // P
LAT, CTX = 512, 256
LAT0 = CTX + 1
TW = LAT0 + LAT
LRU = 1024
LT = LRU // P
N_U, N_K, N_V, N_L = LT, LT, LT, 2
BOTH_TILES = N_U + N_K + N_V + N_L
LAT_TILES = LT + LT + 2
TILES = BOTH_TILES + LAT_TILES
U0, K0, V0, LORA0 = 0, N_U, N_U + N_K, N_U + N_K + N_V
GATE0, R0, GD0 = BOTH_TILES, BOTH_TILES + LT, BOTH_TILES + 2 * LT
HD = 64
HEADS = 16
C = 128
PEER_HEADS, NK, TOPK = 8, 128, 16
HP = 2 * PEER_HEADS
GROUP = 8
DU = 256
ALPHA = 2.0 ** 0.25
LN_EPS, GN_EPS = 1e-5, 64e-5
DECAY = float(np.exp(-0.5))
LOWEST = -3.0e38
SECTIONS = 6
MOD_TILES = SECTIONS * KT
MW = 512
MOD_UNITS = MOD_TILES * P // MW
MOD_BUFS = 4


class Env:
    pass


def sems(nc, ctx, *names):
    handles = [nc.alloc_semaphore(n) for n in names]

    def release():
        nc.clear_and_free_semaphores(handles)
        nc.all_engine_barrier()

    ctx.callback(release)
    return handles


def modulation(nc, e, a):
    with ExitStack() as ctx:
        sb = lambda n, s, d=FP32: ctx.enter_context(nc.sbuf_tensor(n, s, d))
        cond = sb("cond", [P, KT, 2])
        cond_act = sb("cond_act", [P, KT, 2])
        two = sb("two_by_two", [2, 2])
        w = [sb(f"ada_w{b}", [P, KT, MW]) for b in range(MOD_BUFS)]
        row = [sb(f"ada_row{b}", [2, MW]) for b in range(2)]
        acc = [ctx.enter_context(nc.psum_tensor(f"ada_acc{b}", [2, MW], FP32)) for b in range(2)]
        turned = [ctx.enter_context(nc.psum_tensor(f"ada_turned{b}", [P, MW // P, 2], FP32)) for b in range(2)]
        cond_loaded, bias_loaded, act_ready, used, row_ready, columns_ready, evicted = sems(
            nc, ctx, "cond_loaded", "adab_loaded", "cond_act_ready", "ada_w_used", "ada_row_ready", "ada_columns_ready", "ada_evicted")
        loaded = sems(nc, ctx, *[f"ada_w{b}_loaded" for b in range(MOD_BUFS)])
        with nc.Block() as block:
            @block.sync
            def _(sp):
                sp.dma_start(cond[:], a["cond"]).then_inc(cond_loaded, 16)
                for u in range(MOD_UNITS):
                    if u >= MOD_BUFS:
                        sp.wait_ge(used, u - MOD_BUFS + 1)
                    sp.dma_start(w[u % MOD_BUFS][:], a["ada_w"][u].rearrange("p (k n) -> p k n", k=KT)
                                 ).then_inc(loaded[u % MOD_BUFS], 16)

            @block.scalar
            def _(act):
                act.dma_start(e.bias[:], a["ada_b"]).then_inc(bias_loaded, 16)
                act.dma_start(two[:], a["two_by_two"]).then_inc(bias_loaded, 16)
                act.wait_ge(cond_loaded, 16)
                nc.scalar.activation(cond_act[:], cond[:], ACT.Silu).then_inc(act_ready, 1)
                for u in range(MOD_UNITS):
                    act.wait_ge(used, u + 1)
                    if u >= 2:
                        act.wait_ge(columns_ready, u - 1)
                    nc.scalar.activation(row[u % 2][:], acc[u % 2][:], ACT.Copy).then_inc(row_ready, 1)

            @block.tensor
            def _(pe):
                def turn(u):
                    pe.wait_ge(row_ready, u + 1)
                    if u >= 2:
                        pe.wait_ge(evicted, u - 1)
                    for j in range(MW // P):
                        last = nc.tensor.matmul(turned[u % 2][:, j, :], row[u % 2][:, j * P:(j + 1) * P], two[:],
                                                start=True, stop=True)
                    last.then_inc(columns_ready, 1)

                pe.wait_ge(act_ready, 1)
                pe.wait_ge(bias_loaded, 32)
                for u in range(MOD_UNITS):
                    pe.wait_ge(loaded[u % MOD_BUFS], 16 * (u // MOD_BUFS + 1))
                    if u >= 2:
                        pe.wait_ge(row_ready, u - 1)
                    for k in range(KT):
                        last = nc.tensor.matmul(acc[u % 2][:], cond_act[:, k, :], w[u % MOD_BUFS][:, k, :],
                                                start=(k == 0), stop=(k == KT - 1))
                    last.then_inc(used, 1)
                    if u >= 1:
                        turn(u - 1)
                turn(MOD_UNITS - 1)

            @block.vector
            def _(dve):
                dve.wait_ge(bias_loaded, 32)
                for u in range(MOD_UNITS):
                    dve.wait_ge(columns_ready, u + 1)
                    t = slice(u * (MW // P), (u + 1) * (MW // P))
                    nc.vector.tensor_tensor(e.mod[:, t, :], turned[u % 2][:], e.bias[:, t, :], ALU.add).then_inc(evicted, 1)


def projection(nc, name, weights, first, count, rhs_hi, rhs_lo, spans, evict_vector, evict_bufs, store, prologue=None):
    with ExitStack() as ctx:
        sb = lambda n, s, d=FP32: ctx.enter_context(nc.sbuf_tensor(name + n, s, d))
        raw = [sb(f"raw{b}", [P, KT * P]) for b in range(2)]
        hi = [sb(f"hi{b}", [P, KT * P], FP32R) for b in range(2)]
        lo = [sb(f"lo{b}", [P, KT * P], FP32R) for b in range(2)]
        acc = [[ctx.enter_context(nc.psum_tensor(f"{name}acc{b}{s}", [P, w], FP32)) for s, (_, w, _) in enumerate(spans)]
               for b in range(2)]
        hi_done, lo_done, products, landed, evicted = sems(
            nc, ctx, name + "hi_done", name + "lo_done", name + "products", name + "landed", name + "evicted")
        loaded = sems(nc, ctx, name + "loaded0", name + "loaded1")
        stored, output_free = sems(nc, ctx, name + "stored", name + "output_free")
        assert count % 2 == 0
        with nc.Block() as block:
            @block.sync
            def _(sp):
                for b in range(2):
                    sp.dma_start(raw[b][:], weights[first + b]).then_inc(loaded[b], 16)
                with sp.Fori(0, count // 2 - 1) as i:
                    for b in range(2):
                        sp.wait_ge(hi_done, 2 * i + b + 1)
                        sp.wait_ge(lo_done, 2 * i + b + 1)
                        sp.dma_start(raw[b][:], weights[bass.ds(2 * i + (b + 2 + first), 1)].rearrange("o p n -> p (o n)")
                                     ).then_inc(loaded[b], 16)

            @block.scalar
            def _(act):
                act.sem_inc(landed, 2)

                def high(i, b):
                    act.wait_ge(loaded[b], 16 * i + 16)
                    act.wait_ge(products, 2 * i + b + 1)
                    nc.scalar.activation(hi[b][:], raw[b][:], ACT.Copy).then_inc(hi_done, 1)

                def land(i, b):
                    act.wait_ge(products, 2 * i + b + 3)
                    act.wait_ge(evicted, 2 * i + b + 1)
                    for s, (_, w, col) in enumerate(spans):
                        last = nc.scalar.activation(evict_bufs[b][:, col:col + w], acc[b][s][:], ACT.Copy)
                    last.then_inc(landed, 1)

                high(0, 0)
                with act.Fori(0, count // 2 - 1) as i:
                    high(i, 1)
                    land(i, 0)
                    high(i + 1, 0)
                    land(i, 1)
                high(count // 2 - 1, 1)
                land(count // 2 - 1, 0)
                land(count // 2 - 1, 1)

            @block.vector
            def _(dve):
                dve.sem_inc(evicted, 2)

                def low(i, b):
                    dve.wait_ge(hi_done, 2 * i + b + 1)
                    nc.vector.tensor_tensor(lo[b][:], raw[b][:], hi[b][:].bitcast(FP32), ALU.subtract).then_inc(lo_done, 1)

                def evict(i, b):
                    dve.wait_ge(landed, 2 * i + b + 3)
                    if store is not None:
                        dve.wait_ge(output_free, 2 * i + b + 1)
                    dve.wait_ge(evicted, 2 * i + b + 2)
                    evict_vector(dve, 2 * i + b, b).then_inc(evicted, 1)

                low(0, 0)
                with dve.Fori(0, count // 2 - 1) as i:
                    low(i, 1)
                    evict(i, 0)
                    low(i + 1, 0)
                    evict(i, 1)
                low(count // 2 - 1, 1)
                evict(count // 2 - 1, 0)
                evict(count // 2 - 1, 1)

            @block.tensor
            def _(pe):
                pe.sem_inc(products, 2)
                with pe.Fori(0, count // 2) as i:
                    for b in range(2):
                        pe.wait_ge(lo_done, 2 * i + b + 1)
                        pe.wait_ge(landed, 2 * i + b + 1)
                        for k in range(KT):
                            ks = slice(k * P, (k + 1) * P)
                            for n, (wt, x) in enumerate(((hi, rhs_hi), (hi, rhs_lo), (lo, rhs_hi))):
                                for s, (c0, w, _) in enumerate(spans):
                                    last = nc.tensor.matmul(acc[b][s][:], wt[b][:, ks], x[:, k, c0:c0 + w],
                                                            start=(k == 0 and n == 0), stop=(k == KT - 1 and n == 2))
                        last.then_inc(products, 1)

            @block.gpsimd
            def _(pool):
                if store is not None:
                    pool.sem_inc(output_free, 2)
                    with pool.Fori(0, count // 2) as i:
                        for b in range(2):
                            pool.wait_ge(evicted, 2 * i + b + 3)
                            store(pool, 2 * i + b, b).then_inc(stored, 16)
                            pool.wait_ge(stored, 32 * i + 16 * b + 16)
                            pool.sem_inc(output_free, 1)


def modulated_input(nc, e, a, x_hi, x_lo):
    with ExitStack() as ctx:
        sb = lambda n, s, d=FP32: ctx.enter_context(nc.sbuf_tensor(n, s, d))
        rows, cols = sb("pos_rows", [P, KT // 2, 8]), sb("pos_cols", [P, KT // 2, 64])
        xc = [sb(f"in_ctx{b}", [P, CTX]) for b in range(2)]
        xl = [sb(f"in_lat{b}", [P, LAT]) for b in range(2)]
        hc = [sb(f"mod_ctx{b}", [P, CTX]) for b in range(2)]
        hl = [sb(f"mod_lat{b}", [P, LAT]) for b in range(2)]
        tables_loaded, one_plus, posed, modded, hi_done, lo_done = sems(
            nc, ctx, "pos_loaded", "scale_ready", "posed", "modded", "x_hi_done", "x_lo_done")
        loaded = sems(nc, ctx, "x0_loaded", "x1_loaded")
        sc1 = e.one_plus_scale
        with nc.Block() as block:
            @block.sync
            def _(sp):
                sp.dma_start(rows[:], a["pos_rows"]).then_inc(tables_loaded, 16)
                sp.dma_start(cols[:], a["pos_cols"]).then_inc(tables_loaded, 16)
                for k in range(KT):
                    b = k % 2
                    if k >= 2:
                        sp.wait_ge(modded, k - 1)
                    sp.dma_start(xc[b][:], a["ctx"][k]).then_inc(loaded[b], 16)
                    sp.dma_start(xl[b][:], a["x"][k]).then_inc(loaded[b], 16)

            @block.vector
            def _(dve):
                nc.vector.tensor_scalar(sc1[:], e.mod[:, KT:2 * KT, :], 1.0, None, ALU.add).then_inc(one_plus, 1)
                nc.vector.tensor_scalar(e.one_plus_scale2[:], e.mod[:, 4 * KT:5 * KT, 0], 1.0, None, ALU.add).then_inc(one_plus, 1)
                dve.wait_ge(one_plus, 2)
                dve.wait_ge(tables_loaded, 32)
                for k in range(KT):
                    b = k % 2
                    dve.wait_ge(loaded[b], 32 * (k // 2 + 1))
                    table = (rows[:, k, :, None].to_broadcast([P, 8, 64]) if k < KT // 2
                             else cols[:, k - KT // 2, None, :].to_broadcast([P, 8, 64]))
                    grid = xl[b][:].rearrange("p (r c) -> p r c", c=64)
                    nc.vector.tensor_tensor(grid, grid, table, ALU.add).then_inc(posed, 1)
                    dve.wait_ge(posed, k + 1)
                    if k >= 2:
                        dve.wait_ge(lo_done, k - 1)
                    nc.vector.tensor_scalar(hc[b][:], xc[b][:], sc1[:, k, 1:2], e.mod[:, k, 1:2], ALU.mult, ALU.add)
                    nc.vector.tensor_scalar(hl[b][:], xl[b][:], sc1[:, k, 0:1], e.mod[:, k, 0:1], ALU.mult, ALU.add
                                            ).then_inc(modded, 1)
                    dve.wait_ge(hi_done, k + 1)
                    nc.vector.tensor_tensor(x_lo[:, k, 0:CTX], hc[b][:], x_hi[:, k, 0:CTX].bitcast(FP32), ALU.subtract)
                    nc.vector.tensor_tensor(x_lo[:, k, CTX:], hl[b][:], x_hi[:, k, CTX:].bitcast(FP32), ALU.subtract
                                            ).then_inc(lo_done, 1)

            @block.scalar
            def _(act):
                for k in range(KT):
                    b = k % 2
                    act.wait_ge(modded, k + 1)
                    nc.scalar.activation(x_hi[:, k, 0:CTX], hc[b][:], ACT.Copy)
                    nc.scalar.activation(x_hi[:, k, CTX:], hl[b][:], ACT.Copy).then_inc(hi_done, 1)


def in_projection(nc, e, a):
    with ExitStack() as ctx:
        sb = lambda n, s, d=FP32: ctx.enter_context(nc.sbuf_tensor(n, s, d))
        x_hi, x_lo = sb("x_hi", [P, KT, CTX + LAT], FP32R), sb("x_lo", [P, KT, CTX + LAT], FP32R)
        modulated_input(nc, e, a, x_hi, x_lo)
        mu = sb("mu", [P, TILES, 2])
        landing = [sb(f"p_landing{b}", [P, TW + 2]) for b in range(2)]
        mixed = [sb(f"p_mixed{b}", [P, TW]) for b in range(2)]
        diff, half = sb("p_diff", [P, TW]), sb("p_half", [P, TW])
        (mu_loaded, cleared) = sems(nc, ctx, "mu_loaded", "landing_cleared")
        with nc.Block() as block:
            @block.sync
            def _(sp):
                sp.dma_start(mu[:], a["mu"]).then_inc(mu_loaded, 16)
                sp.wait_ge(mu_loaded, 16)

            @block.vector
            def _(dve):
                for b in range(2):
                    nc.vector.memset(landing[b][:], 0.0)
                nc.vector.memset(diff[:], 0.0)
                nc.vector.memset(half[:], 0.0)
                for b in range(2):
                    nc.vector.memset(mixed[b][:], 0.0)
        for tag, first, count, lat_only in (("pb_", 0, BOTH_TILES, False), ("pl_", BOTH_TILES, LAT_TILES, True)):
            (step,) = sems(nc, ctx, tag + "shift_step")
            cols = slice(LAT0, TW) if lat_only else slice(0, TW)
            n_cols = cols.stop - cols.start
            prev, cur, nxt = (slice(cols.start + s, cols.start + s + n_cols) for s in range(3))

            def shift(dve, unit, b, first=first, step=step, cols=cols, prev=prev, cur=cur, nxt=nxt):
                at = bass.ds(unit + first, 1)
                m = landing[b]
                n = unit * 3
                nc.vector.tensor_tensor(diff[:, cols], m[:, prev], m[:, cur], ALU.subtract).then_inc(step, 1)
                dve.wait_ge(step, n + 1)
                nc.vector.scalar_tensor_tensor(out=half[:, cols], in0=diff[:, cols], scalar=mu[:, at, 0], in1=m[:, cur],
                                               op0=ALU.mult, op1=ALU.add).then_inc(step, 1)
                dve.wait_ge(step, n + 2)
                nc.vector.tensor_tensor(diff[:, cols], m[:, nxt], m[:, cur], ALU.subtract).then_inc(step, 1)
                dve.wait_ge(step, n + 3)
                return nc.vector.scalar_tensor_tensor(out=mixed[b][:, cols], in0=diff[:, cols], scalar=mu[:, at, 1],
                                                      in1=half[:, cols], op0=ALU.mult, op1=ALU.add)

            def store(eng, unit, b, first=first, cols=cols):
                dst = e.p_dram[bass.ds(unit + first, 1)].rearrange("o p n -> p (o n)")
                return eng.dma_start(dst[:, cols], mixed[b][:, cols])

            spans = [(CTX, LAT, LAT0 + 1)] if lat_only else [(CTX, LAT, LAT0 + 1), (0, CTX, 1)]
            projection(nc, tag, a["w_in"], first, count, x_hi, x_lo, spans, shift, landing, store)

ZW = 2 + CTX + 3 + LAT + 1
XW = ZW - 3
XL = CTX + 3
X_SEGS = ((0, CTX), (XL, LAT))


class Chain:

    def __init__(self, engine, sem, base=0):
        self.engine, self.sem, self.base, self.n = engine, sem, base, 0

    def step(self, ins):
        self.n += 1
        return ins.then_inc(self.sem, 1)

    def ordered(self, ins):
        self.step(ins)
        self.engine.wait_ge(self.sem, self.base + self.n)


def rglru(nc, e, a):
    with ExitStack() as ctx:
        sb = lambda n, s, d=FP32: ctx.enter_context(nc.sbuf_tensor("lru_" + n, s, d))
        z, xc = sb("z", [P, LT, ZW]), sb("xc", [P, LT, XW])
        gate_a, gate_x, th = sb("gate_a", [P, LT, XW]), sb("gate_x", [P, LT, XW]), sb("tanh", [P, LT, XW])
        y, gate, h = sb("y", [P, LT, LAT]), sb("gate", [P, LT, LAT]), sb("h", [P, LAT])
        h_ctx = sb("h_ctx", [P, CTX])
        w = [sb("wa", [P, 2 * LT, P]), sb("wx", [P, 2 * LT, P])]
        vec = sb("vec", [P, 11, LT])
        decay, neg_decay = sb("decay", [P, 2, LT]), sb("neg_decay", [P, 2, LT])
        tmp = [sb(f"tmp{i}", [P, 2, LT]) for i in range(4)]
        acc = [[[ctx.enter_context(nc.psum_tensor(f"lru_acc{b}{g}{s}", [P, n], FP32)) for s, (_, n) in enumerate(X_SEGS)]
                for g in range(2)] for b in range(2)]
        vec_loaded, z_loaded, w_cleared, w_loaded, gate_loaded, y_stored = sems(
            nc, ctx, "lru_vec_loaded", "z_loaded", "lru_w_cleared", "lru_w_loaded", "gate_loaded", "y_stored")
        abs_ready, exp_ready, decay_ready, conv_done, gates, gates_read, tanh_done, a_done, ratio, root, scanned, gelu_done, merged, v_step, a_step = sems(
            nc, ctx, "lam_abs", "lam_exp", "decay_ready", "conv_done", "gate_products", "gates_ready", "tanh_done",
            "a_done", "ratio_done", "root_done", "scanned", "gelu_done", "lru_merged", "lru_v_step", "lru_a_step")
        with nc.Block() as block:
            @block.sync
            def _(sp):
                sp.dma_start(vec[:], a["lru_vec"]).then_inc(vec_loaded, 16)
                tiles = e.p_dram[U0:U0 + LT].rearrange("t p n -> p t n")
                sp.dma_start(z[:, :, 2:2 + CTX], tiles[:, :, 0:CTX]).then_inc(z_loaded, 16)
                sp.dma_start(z[:, :, 2 + XL:2 + XL + LAT], tiles[:, :, LAT0:]).then_inc(z_loaded, 16)
                sp.wait_ge(w_cleared, 1)
                for g, name in enumerate(("lru_wa", "lru_wx")):
                    for s in range(2):
                        sp.dma_start(w[g][s * HD:(s + 1) * HD, :, s * HD:(s + 1) * HD], a[name][s]).then_inc(w_loaded, 16)
                sp.dma_start(gate[:], e.p_dram[GATE0:GATE0 + LT].rearrange("t p n -> p t n")[:, :, LAT0:]).then_inc(gate_loaded, 16)
                sp.wait_ge(merged, 1)
                sp.dma_start(e.merged_dram[0:LT].rearrange("t p n -> p t n"), y[:]).then_inc(y_stored, 16)
                sp.wait_ge(y_stored, 16)

            @block.gpsimd
            def _(pool):
                nc.gpsimd.memset(w[0][:], 0.0)
                nc.gpsimd.memset(w[1][:], 0.0).then_inc(w_cleared, 1)

            @block.vector
            def _(dve):
                c = Chain(dve, v_step)
                for seg in ((0, 2), (2 + CTX, 3), (ZW - 1, 1)):
                    nc.vector.memset(z[:, :, seg[0]:seg[0] + seg[1]], 0.0)
                for t in (gate_a, gate_x):
                    c.ordered(nc.vector.memset(t[:, :, CTX:XL], 0.0))
                dve.wait_ge(exp_ready, 1)
                lam, (ex, s1, s2, poly) = vec[:, 9:11, :], (t[:] for t in tmp)
                c.ordered(nc.vector.tensor_scalar(s1, ex, 2.0, None, ALU.add))
                c.ordered(nc.vector.reciprocal(s1, s1))
                c.ordered(nc.vector.tensor_tensor(s1, s1, ex, ALU.mult))
                c.ordered(nc.vector.tensor_tensor(s2, s1, s1, ALU.mult))
                c.ordered(nc.vector.memset(poly, 1.0 / 19))
                for k in range(8, -1, -1):
                    c.ordered(nc.vector.tensor_tensor(poly, poly, s2, ALU.mult))
                    c.ordered(nc.vector.tensor_scalar(poly, poly, 1.0 / (2 * k + 1), None, ALU.add))
                c.ordered(nc.vector.tensor_tensor(poly, poly, s1, ALU.mult))
                c.ordered(nc.vector.tensor_scalar(s2, lam, -1.0, 0.0, ALU.mult, ALU.max))
                c.ordered(nc.vector.scalar_tensor_tensor(out=poly, in0=poly, scalar=2.0, in1=s2, op0=ALU.mult, op1=ALU.add))
                c.ordered(nc.vector.tensor_scalar(decay[:], poly, 8.0, None, ALU.mult))
                nc.vector.tensor_scalar(neg_decay[:], poly, -8.0, None, ALU.mult).then_inc(decay_ready, 1)
                dve.wait_ge(z_loaded, 32)
                for j in range(LT):
                    c.step(nc.vector.tensor_scalar(xc[:, j, :], z[:, j, 0:XW], vec[:, 0, j:j + 1], vec[:, 4, j:j + 1], ALU.mult, ALU.add))
                for tap in range(1, 4):
                    for j in range(LT):
                        dve.wait_ge(v_step, c.n - LT + 1)
                        ins = nc.vector.scalar_tensor_tensor(out=xc[:, j, :], in0=z[:, j, tap:tap + XW], scalar=vec[:, tap, j:j + 1],
                                                             in1=xc[:, j, :], op0=ALU.mult, op1=ALU.add)
                        c.step(ins)
                        if tap == 3:
                            dve.wait_ge(v_step, c.n)
                            dve.sem_inc(conv_done, 1)
                inv = z[:, :, 0:XW]
                for d in range(2):
                    dve.wait_ge(gates_read, 2 * LT * (d + 1))
                    c.ordered(nc.vector.tensor_tensor(gate_x[:], gate_x[:], xc[:], ALU.mult))
                    dve.wait_ge(tanh_done, d + 1)
                    c.ordered(nc.vector.tensor_scalar(inv, th[:], 1.0, None, ALU.add))
                    c.ordered(nc.vector.reciprocal(inv, inv))
                    nc.vector.tensor_tensor(th[:], th[:], inv, ALU.mult).then_inc(ratio, 1)
                    dve.wait_ge(root, d + 1)
                    c.ordered(nc.vector.tensor_tensor(gate_x[:], gate_x[:], th[:], ALU.mult))
                    for j in range(LT):
                        flip = slice(None, None, -1) if d else slice(None)
                        if d == 0:
                            h_out = y[:, j, :]
                        else:
                            h_out = h[:]
                            if j:
                                dve.wait_ge(v_step, c.n)
                        A, B = gate_a[:, j, :], gate_x[:, j, :]
                        c.ordered(nc.vector.tensor_tensor_scan(h_ctx[:, flip], A[:, 0:CTX][:, flip], B[:, 0:CTX][:, flip], 0.0,
                                                               ALU.mult, ALU.add))
                        end = h_ctx[:, 0:1] if d else h_ctx[:, CTX - 1:CTX]
                        c.ordered(nc.vector.tensor_tensor_scan(h_out[:, flip], A[:, XL:][:, flip], B[:, XL:][:, flip], end,
                                                               ALU.mult, ALU.add))
                        if d:
                            c.ordered(nc.vector.tensor_tensor(y[:, j, :], y[:, j, :], h[:], ALU.add))
                    dve.sem_inc(scanned, 1)
                dve.wait_ge(gelu_done, 1)
                nc.vector.tensor_tensor(y[:], y[:], gate[:], ALU.mult).then_inc(merged, 1)

            @block.scalar
            def _(act):
                c = Chain(act, a_step)
                act.wait_ge(vec_loaded, 16)
                c.ordered(nc.scalar.activation(tmp[1][:], vec[:, 9:11, :], ACT.Abs))
                nc.scalar.activation(tmp[0][:], tmp[1][:], ACT.Exp, scale=-1.0).then_inc(exp_ready, 1)
                for d in range(2):
                    if d:
                        act.wait_ge(scanned, d)
                    for j in range(LT):
                        n = d * LT + j
                        act.wait_ge(gates, n + 1)
                        for g, (dst, bias) in enumerate(((gate_a, 5 + d), (gate_x, 7 + d))):
                            for s, (c0, w_) in enumerate(X_SEGS):
                                ins = nc.scalar.activation(dst[:, j, c0:c0 + w_], acc[n % 2][g][s][:], ACT.Sigmoid,
                                                           bias=vec[:, bias, j:j + 1])
                            ins.then_inc(gates_read, 1)
                    act.wait_ge(gates_read, 2 * LT * (d + 1))
                    act.wait_ge(decay_ready, 1)
                    for j in range(LT):
                        ins = nc.scalar.activation(th[:, j, :], gate_a[:, j, :], ACT.Tanh, scale=decay[:, d, j:j + 1])
                    ins.then_inc(tanh_done, 1)
                    act.wait_ge(tanh_done, d + 1)
                    for j in range(LT):
                        ins = nc.scalar.activation(gate_a[:, j, :], gate_a[:, j, :], ACT.Exp, scale=neg_decay[:, d, j:j + 1])
                    c.ordered(ins)
                    act.wait_ge(ratio, d + 1)
                    nc.scalar.activation(th[:], th[:], ACT.Sqrt, scale=2.0).then_inc(root, 1)
                act.wait_ge(gate_loaded, 16)
                nc.scalar.activation(gate[:], gate[:], ACT.Gelu_apprx_tanh).then_inc(gelu_done, 1)

            @block.tensor
            def _(pe):
                pe.wait_ge(w_loaded, 64)
                for d in range(2):
                    for j in range(LT):
                        n = d * LT + j
                        pe.wait_ge(conv_done, j + 1)
                        if n >= 2:
                            pe.wait_ge(gates_read, 2 * (n - 1))
                        for g in range(2):
                            for s, (c0, w_) in enumerate(X_SEGS):
                                last = nc.tensor.matmul(acc[n % 2][g][s][:], w[g][:, d * LT + j, :], xc[:, j, c0:c0 + w_],
                                                        start=True, stop=True)
                        last.then_inc(gates, 1)


LEVELS = 7
PAIRS = HEADS // 2
BANKS = 6
BANK = 512


def slot(p, s):
    return (p // 2) * 4 + s * 2 + p % 2


def chunk_fills(lat):
    fills = [((t, h), "act") for t in ("bT", "kT", "vT") for h in range(2)]
    fills += [((m, q, s), "dve") for q in range(4) for m in ("Mb", "Mk") for s in range(2)]
    for level in range(1, LEVELS):
        fills += [(("X", level, q), "dve") for q in range(4)]
        if level > 1:
            fills += [((t, level, q), "act") for q in range(4) for t in ("T", "Tt")]
    fills += [(("X", LEVELS, h), "dve") for h in range(2)] + [(("Tt", LEVELS, h), "act") for h in range(2)]
    fills += [(("rhs", s), "act") for s in range(2)] + [(("U", s), "act") for s in range(2)]
    if lat:
        fills += [(("Y", h), "dve") for h in range(2)]
    return fills + [(("S",), "dve")]


def fill_tables(lat):
    bank, count, total = {}, {}, {"act": 0, "dve": 0}
    for n, (name, engine) in enumerate(chunk_fills(lat)):
        bank[name] = n % BANKS
        total[engine] += 1
        count[name] = total[engine]
    return bank, count, total


TABLES = {lat: fill_tables(lat) for lat in (False, True)}
PRE_STEPS = {False: 10, True: 12}


class Chunk:

    def __init__(self, d, lat, count, base, i):
        self.d, self.lat, self.i = d, lat, i
        self.n = base["n"] + i
        self.n_lat = base["n_lat"] + i
        self.act = base["act"] + i * TABLES[lat][2]["act"]
        self.dve = base["dve"] + i * TABLES[lat][2]["dve"]
        self.steps = base["steps"] + i * PRE_STEPS[lat]
        self.loads_end = base["loads"] + i * (64 if lat else 48) + (64 if lat else 48)
        self.first_of_direction = not lat and isinstance(i, int) and i == 0
        halves = (slice(0, HD), slice(HD, C))
        self.halves = (halves[1], halves[0]) if d else halves
        self.token = i * -C + (count - 1) * C if d else i * C


def chunk_loop(engine, body):
    runs, base = [], dict(n=0, n_lat=0, act=0, dve=0, steps=0, loads=0)
    for d in range(2):
        for lat, count in ((False, CTX // C), (True, LAT // C)):
            runs.append((d, lat, count, dict(base)))
            base["n"] += count
            base["n_lat"] += count * lat
            base["act"] += count * TABLES[lat][2]["act"]
            base["dve"] += count * TABLES[lat][2]["dve"]
            base["steps"] += count * PRE_STEPS[lat]
            base["loads"] += count * (64 if lat else 48)
    for k, run in enumerate(runs):
        count = run[2]
        if count > 2:
            with engine.Fori(0, count - 1) as i:
                body(Chunk(*run, i), Chunk(*run, i + 1))
        else:
            body(Chunk(*run, 0), Chunk(*run, 1))
        body(Chunk(*run, count - 1), Chunk(*runs[k + 1], 0) if k + 1 < len(runs) else None)


FIRST_CHUNK = (0, False, CTX // C, dict(n=0, n_lat=0, act=0, dve=0, steps=0, loads=0), 0)


def rwkv(nc, e, a):
    with ExitStack() as ctx:
        sb = lambda n, s, d=FP32: ctx.enter_context(nc.sbuf_tensor("rw_" + n, s, d))
        y_acc, bonus = sb("y_acc", [P, PAIRS, LAT]), sb("bonus_acc", [P, PAIRS, LAT])
        ident, ones = sb("ident", [P, P]), sb("head_ones", [P, P])
        vec = sb("vec", [P, 9, PAIRS])
        with ExitStack() as inner:
            rwkv_scan(nc, e, a, ctx, inner, y_acc, bonus, ident, ones, vec)
        rwkv_out(nc, e, a, y_acc, bonus, ones, vec)


def rwkv_scan(nc, e, a, ctx, inner, y_acc, bonus, ident, ones, vec):
    sb = lambda n, s, d=FP32: inner.enter_context(nc.sbuf_tensor("rw_" + n, s, d))
    full = [P, PAIRS, C]
    k, v, r = sb("k", full), sb("v", full), sb("r", full)
    lora = sb("lora", [P, 2, C])
    w2, a2 = sb("w2", [P, LRU]), sb("a2", [P, LRU])
    zeros = sb("zeros", [P, P], BF16)
    pool_scratch = sb("pool_scratch", [P, 1])
    tri = sb("tri", [P, 2, 2, C])
    level_mask = sb("level_mask", [P, 2, LEVELS, C])
    restart = sb("restart", full)
    tw = sb("tanh_w", [P, C])
    sg, rate, kraw, kd, cum, nrm = (sb(n, full) for n in ("sg", "rate", "kraw", "kd", "cum", "nrm"))
    w_r, w_inv, w_ex = (sb(n, full) for n in ("w_r", "w_inv", "w_ex"))
    sq, rk = w_ex, w_r
    mid, w_mid, w_end = (sb(n, [P, PAIRS]) for n in ("mid", "w_mid", "w_end"))
    AR, Bt, Kt = sb("AR", [P, PAIRS, 2, C]), sb("Bt", full), sb("Kt", full)
    AR_kept = sb("AR_kept", [P, PAIRS, 2, C])
    BT, KTT, VT = (sb(n, [P, LRU]) for n in ("B_T", "K_T", "V_T"))
    Mb, Mk = sb("Mb", [P, HEADS, 2, C]), sb("Mk", [P, HEADS, 2, C])
    X, T, Tt = (sb(n, [P, HEADS, C]) for n in ("X", "T", "Tt"))
    rhs, U = (t[:].rearrange("p h n -> p (h n)")[:, 0:LRU] for t in (X, T))
    S, S_mid, S_sum = (sb(n, [P, PAIRS, HD]) for n in ("S", "S_mid", "S_sum"))
    banks = [inner.enter_context(nc.psum_tensor(f"rw_bank{b}", [P, BANK], FP32)) for b in range(BANKS)]
    pre_bank = [inner.enter_context(nc.psum_tensor(f"rw_pre_bank{h}", [P, BANK], FP32)) for h in range(2)]
    (const_loaded, raw_loaded, tanh_done, sq_ready, rsqrt_ready, rk_ready, cum_ready, weights_ready, tilde_ready) = sems(
        nc, ctx, "rw_const_loaded", "rw_raw_loaded", "rw_tanh_done", "sq_ready", "rsqrt_ready", "rk_ready", "cum_ready",
        "weights_ready", "tilde_ready")
    lora_filled, lora_taken, norm_filled, norm_taken, bonus_filled, bonus_taken = sems(
        nc, ctx, "lora_filled", "lora_taken", "norm_filled", "norm_taken", "bonus_filled", "bonus_taken")
    filled_act, filled_dve, act_taken, dve_taken = sems(nc, ctx, "filled_for_act", "filled_for_dve", "act_taken", "dve_taken")
    state_ready, state_done, kept, one_plus_m, first_level, start_step, pre_step, raw_free, ln_done, state_cleared = sems(
        nc, ctx, "state_ready", "state_done", "AR_is_kept", "one_plus_m", "first_level", "rw_start_step", "rw_pre_step", "raw_free", "ln_done", "state_cleared")

    def bcast(t, n):
        return t[:, :, None].to_broadcast([P, PAIRS, n])

    with nc.Block() as block:
        @block.sync
        def _(sp):
            consts = [(ident, a["ident"]), (ones, a["rwkv_ones"]), (vec, a["rwkv_vec"]), (w2, a["rwkv_w2"]), (a2, a["rwkv_a2"]),
                      (tri, a["rwkv_tri"]), (level_mask, a["rwkv_level"])]

            def load(chunk):
                at = bass.ds(sp.snap(chunk.token + (LAT0 if chunk.lat else 0)), C)
                for dst, tile in ((k, K0), (v, V0)) + (((r, R0),) if chunk.lat else ()):
                    sp.dma_start(dst[:], e.p_dram[tile:tile + LT].rearrange("t p n -> p t n")[:, :, at]).then_inc(raw_loaded, 16)
                sp.dma_start(lora[:], e.p_dram[LORA0:LORA0 + 2].rearrange("t p n -> p t n")[:, :, at]).then_inc(raw_loaded, 16)

            def body(chunk, after):
                if after is not None:
                    sp.wait_ge(raw_free, chunk.n + 1)
                    load(after)

            load(Chunk(*FIRST_CHUNK))
            for dst, src in consts:
                sp.dma_start(dst[:], src).then_inc(const_loaded, 16)
            chunk_loop(sp, body)

        @block.gpsimd
        def _(pool):
            def body(chunk, after):
                pool.wait_ge(tilde_ready, chunk.n + 1)
                pool.wait_ge(state_done, chunk.n + 1)
                width = 2 if chunk.lat else 1
                nc.gpsimd.tensor_tensor(pool_scratch[:], AR[:, 0, 0, 0:1], AR[:, 0, 0, 0:1], ALU.mult)
                nc.gpsimd.tensor_copy(AR_kept[:, :, 0:width, :], AR[:, :, 0:width, :]).then_inc(kept, 1)

            chunk_loop(pool, body)

        @block.scalar
        def _(act):
            act.sem_inc(act_taken, 1)

            def prepare(chunk, part):
                n = chunk.n
                if part == 0:
                    act.wait_ge(raw_loaded, chunk.loads_end)
                    nc.scalar.activation(tw[:], lora[:, 0, :], ACT.Tanh).then_inc(tanh_done, 1)
                if part in (2, 3):
                    dst, row, turn = ((sg, 0, 0), (rate, 2, 2))[part - 2]
                    for h in range(2):
                        act.wait_ge(lora_filled, 4 * n + turn + h + 1)
                        for q in range(4):
                            p = 4 * h + q
                            ins = nc.scalar.activation(dst[:, p, :], pre_bank[h][:, q * C:(q + 1) * C], ACT.Sigmoid,
                                                       bias=vec[:, row + chunk.d, p:p + 1])
                        ins.then_inc(lora_taken, 1)
                if part == 5:
                    act.wait_ge(norm_taken, 2 * n + 2)
                    nc.scalar.activation(nrm[:], nrm[:], ACT.Ln).then_inc(ln_done, 1)
                    act.wait_ge(ln_done, n + 1)
                    nc.scalar.activation(nrm[:], nrm[:], ACT.Exp, scale=-0.5).then_inc(rsqrt_ready, 1)
                if part == 6:
                    act.wait_ge(cum_ready, n + 1)
                    nc.scalar.activation(w_inv[:], cum[:], ACT.Exp, scale=DECAY)
                    nc.scalar.activation(w_r[:], cum[:], ACT.Exp, scale=-DECAY)
                    nc.scalar.activation(w_ex[:], w_ex[:], ACT.Exp, scale=-DECAY)
                    nc.scalar.activation(w_mid[:], mid[:], ACT.Exp, scale=-DECAY).then_inc(weights_ready, 1)

            def body(chunk, after):
                bank_of, count_at, _ = TABLES[chunk.lat]

                def take(name):
                    act.wait_ge(filled_act, chunk.act + count_at[name])
                    return banks[bank_of[name]]

                for kind, dst in (("bT", BT), ("kT", KTT), ("vT", VT)):
                    for h in range(2):
                        nc.scalar.activation(dst[:, h * BANK:(h + 1) * BANK], take((kind, h))[:], ACT.Copy).then_inc(act_taken, 1)
                if after is not None:
                    prepare(after, 0)
                for level in range(1, LEVELS + 1):
                    if 1 < level < LEVELS:
                        for q in range(4):
                            for name, dst in (("T", T), ("Tt", Tt)):
                                nc.scalar.activation(dst[:, 4 * q:4 * q + 4, :].rearrange("p h n -> p (h n)"), take((name, level, q))[:],
                                                     ACT.Copy).then_inc(act_taken, 1)
                    if level == LEVELS:
                        early, late = chunk.halves
                        for h in range(2):
                            nc.scalar.activation(Tt[early, 8 * h:8 * h + 8, late],
                                                 take(("Tt", level, h))[early, :].rearrange("p (h n) -> p h n", n=HD), ACT.Copy
                                                 ).then_inc(act_taken, 1)
                    if after is not None:
                        prepare(after, level)
                for name, dst in (("rhs", rhs), ("U", U)):
                    for s in range(2):
                        nc.scalar.activation(dst.rearrange("p (q s n) -> p q s n", s=2, n=HD)[:, :, s, :],
                                             take((name, s))[:].rearrange("p (q n) -> p q n", n=HD), ACT.Copy).then_inc(act_taken, 1)

            act.wait_ge(const_loaded, 16 * 7)
            for part in range(LEVELS + 1):
                prepare(Chunk(*FIRST_CHUNK), part)
            chunk_loop(act, body)

        @block.vector
        def _(dve):
            dve.sem_inc(dve_taken, 1)
            dve.sem_inc(state_done, 1)
            dve.wait_ge(const_loaded, 16 * 7)
            nc.vector.memset(restart[:], 1.0).then_inc(start_step, 1)
            dve.wait_ge(start_step, 1)
            nc.vector.memset(restart[:, :, 0:1], 0.0)
            nc.vector.memset(zeros[:], 0.0)
            nc.vector.memset(bonus[:], 0.0).then_inc(start_step, 1)
            dve.wait_ge(start_step, 2)

            def prepare(chunk, part, c):
                n, lat, d = chunk.n, chunk.lat, chunk.d
                if part == 1:
                    dve.wait_ge(raw_loaded, chunk.loads_end)
                    c.ordered(nc.vector.tensor_tensor(kraw[:], k[:], bcast(vec[:, 4, :], C), ALU.mult))
                    nc.vector.tensor_tensor(sq[:], kraw[:], kraw[:], ALU.mult).then_inc(sq_ready, 1)
                if part == 3:
                    dve.wait_ge(lora_taken, 4 * n + 2)
                    flat = lambda t: t[:].rearrange("p h n -> p (h n)")
                    flip = slice(None, None, -1) if d else slice(None)
                    c.ordered(nc.vector.tensor_tensor_scan(flat(cum)[:, flip], flat(restart), flat(sg)[:, flip], 0.0, ALU.mult, ALU.add))
                    m = C // 2 if d else C // 2 - 1
                    c.ordered(nc.vector.tensor_copy(mid[:], cum[:, :, m]))
                    c.ordered(nc.vector.tensor_tensor(cum[:], cum[:], bcast(mid, C), ALU.subtract))
                if part == 4:
                    dve.wait_ge(lora_taken, 4 * n + 4)
                    c.ordered(nc.vector.scalar_tensor_tensor(out=kd[:], in0=rate[:], scalar=1.0, in1=bcast(vec[:, 5, :], C),
                                                             op0=ALU.subtract, op1=ALU.mult))
                    c.ordered(nc.vector.scalar_tensor_tensor(out=kd[:], in0=kd[:], scalar=1.0, in1=k[:], op0=ALU.add, op1=ALU.mult))
                    if lat:
                        c.ordered(nc.vector.tensor_tensor(rk[:], r[:], kd[:], ALU.mult))
                        nc.vector.tensor_tensor(rk[:], rk[:], bcast(vec[:, 6, :], C), ALU.mult).then_inc(rk_ready, 1)
                    for h in range(2):
                        dve.wait_ge(norm_filled, 2 * n + h + 1)
                        nc.vector.tensor_scalar(nrm[:, 4 * h:4 * h + 4, :].rearrange("p h n -> p (h n)"), pre_bank[h][:],
                                                1e-24, None, ALU.max).then_inc(norm_taken, 1)
                    c.ordered(nc.vector.tensor_tensor(w_ex[:], cum[:], sg[:], ALU.subtract))
                if part == 5:
                    if lat:
                        for h in range(2):
                            half = slice(4 * h, 4 * h + 4)
                            dve.wait_ge(bonus_filled, 2 * chunk.n_lat + h + 1)
                            nc.vector.tensor_tensor(Kt[:, half, :], pre_bank[h][:].rearrange("p (h n) -> p h n", n=C), v[:, half, :],
                                                    ALU.mult).then_inc(bonus_taken, 1)
                        dve.wait_ge(bonus_taken, 2 * chunk.n_lat + 2)
                        tok = bass.ds(dve.snap(chunk.token), C)
                        c.ordered(nc.vector.tensor_tensor(bonus[:, :, tok], bonus[:, :, tok], Kt[:], ALU.add))
                    dve.sem_inc(cum_ready, 1)
                if part == 6:
                    dve.wait_ge(rsqrt_ready, n + 1)
                    c.ordered(nc.vector.tensor_tensor(kraw[:], kraw[:], nrm[:], ALU.mult))
                    c.ordered(nc.vector.tensor_tensor(rate[:], rate[:], kraw[:], ALU.mult))
                if part == 7:
                    dve.wait_ge(weights_ready, n + 1)
                    nc.vector.scalar_tensor_tensor(out=AR[:, :, 0, :], in0=kraw[:], scalar=-1.0, in1=w_ex[:], op0=ALU.mult, op1=ALU.mult)
                    nc.vector.tensor_tensor(Bt[:], rate[:], w_inv[:], ALU.mult)
                    if lat:
                        nc.vector.tensor_tensor(AR[:, :, 1, :], r[:], w_r[:], ALU.mult)
                    c.ordered(nc.vector.tensor_tensor(Kt[:], kd[:], w_inv[:], ALU.mult))
                    dve.sem_inc(tilde_ready, 1)
                    assert c.n == PRE_STEPS[lat], c.n

            def body(chunk, after):
                bank_of, count_at, per_chunk = TABLES[chunk.lat]
                d, lat = chunk.d, chunk.lat
                c = after and Chain(dve, pre_step, after.steps)

                def take(name):
                    dve.wait_ge(filled_dve, chunk.dve + count_at[name])
                    return banks[bank_of[name]]

                if chunk.first_of_direction:
                    nc.vector.memset(S[:], 0.0).then_inc(state_cleared, 1)
                    dve.wait_ge(state_cleared, d + 1)
                end = 0 if d else C - 1
                nc.vector.tensor_copy(w_end[:], w_r[:, :, end])
                nc.vector.tensor_tensor(S_mid[:], S[:], bcast(w_mid, HD), ALU.mult).then_inc(state_ready, 1)
                for q in range(4):
                    for m_, dst in (("Mb", Mb), ("Mk", Mk)):
                        for s in range(2):
                            src = take((m_, q, s))
                            at = slice(4 * q + 2 * s, 4 * q + 2 * s + 2)
                            if lat:
                                mask = tri[:, d, None, :, :].to_broadcast([P, 2, 2, C])
                                nc.vector.tensor_tensor(dst[:, at, :, :], src[:].rearrange("p (h m n) -> p h m n", h=2, m=2),
                                                        mask, ALU.mult).then_inc(dve_taken, 1)
                            else:
                                mask = tri[:, d, 0, None, :].to_broadcast([P, 2, C])
                                nc.vector.tensor_tensor(dst[:, at, 0, :], src[:, 0:2 * C].rearrange("p (h n) -> p h n", h=2),
                                                        mask, ALU.mult).then_inc(dve_taken, 1)
                    quad = slice(4 * q, 4 * q + 4)
                    dve.wait_ge(dve_taken, chunk.dve + count_at[("Mb", q, 1)] + 1)
                    nc.vector.tensor_tensor(Mb[:, quad, 0, :], Mb[:, quad, 0, :], ident[:, None, :].to_broadcast([P, 4, C]), ALU.add
                                            ).then_inc(one_plus_m, 1)
                    dve.wait_ge(one_plus_m, 4 * chunk.n + q + 1)
                    nc.vector.tensor_tensor(Tt[:, quad, :], Mb[:, quad, 0, :], level_mask[:, 1 - d, 0, None, :].to_broadcast([P, 4, C]),
                                            ALU.mult).then_inc(first_level, 1)
                    if q == 1:
                        dve.wait_ge(act_taken, chunk.act + count_at[("vT", 1)] + 1)
                        dve.sem_inc(raw_free, 1)
                for level in range(1, LEVELS + 1):
                    if level == LEVELS:
                        early, late = chunk.halves
                        for h in range(2):
                            nc.vector.tensor_copy(X[late, 8 * h:8 * h + 8, early],
                                                  take(("X", level, h))[late, :].rearrange("p (h n) -> p h n", n=HD)).then_inc(dve_taken, 1)
                    for q in range(4 if level < LEVELS else 0):
                        mask = level_mask[:, d, level - 1, None, :].to_broadcast([P, 4, C])
                        nc.vector.tensor_tensor((X if level > 1 else T)[:, 4 * q:4 * q + 4, :],
                                                take(("X", level, q))[:].rearrange("p (h n) -> p h n", h=4), mask, ALU.mult
                                                ).then_inc(dve_taken, 1)
                    if after is not None:
                        if level == 7:
                            dve.wait_ge(kept, chunk.n + 1)
                        prepare(after, level, c)
                if lat:
                    tok = bass.ds(dve.snap(chunk.token), C)
                    for h in range(2):
                        half = slice(4 * h, 4 * h + 4)
                        src = take(("Y", h))[:].rearrange("p (h n) -> p h n", n=C)
                        if d:
                            ins = nc.vector.tensor_tensor(y_acc[:, half, tok], y_acc[:, half, tok], src, ALU.add)
                        else:
                            ins = nc.vector.tensor_copy(y_acc[:, half, tok], src)
                        ins.then_inc(dve_taken, 1)
                nc.vector.tensor_tensor(S_sum[:], take(("S",))[:].rearrange("p (h n) -> p h n", n=HD), S_mid[:], ALU.add
                                        ).then_inc(dve_taken, 1)
                dve.wait_ge(dve_taken, chunk.dve + per_chunk["dve"] + 1)
                nc.vector.tensor_tensor(S[:], S_sum[:], bcast(w_end, HD), ALU.mult).then_inc(state_done, 1)
                dve.wait_ge(state_done, chunk.n + 2)

            first = Chunk(*FIRST_CHUNK)
            c = Chain(dve, pre_step, first.steps)
            for part in range(LEVELS + 1):
                prepare(first, part, c)
            chunk_loop(dve, body)

        @block.tensor
        def _(pe):
            pe.wait_ge(start_step, 2)

            def prepare(chunk, part):
                n = chunk.n
                rows = slice(chunk.d * HD, (chunk.d + 1) * HD)
                if part in (1, 2):
                    wt, src = ((w2, tw[rows, :]), (a2, lora[rows, 1, :]))[part - 1]
                    if part == 1:
                        pe.wait_ge(tanh_done, n + 1)
                    for h in range(2):
                        if part == 2:
                            pe.wait_ge(lora_taken, 4 * n + h + 1)
                        for q in range(4):
                            p = 4 * h + q
                            ins = nc.tensor.matmul(pre_bank[h][:, q * C:(q + 1) * C], wt[rows, p * P:(p + 1) * P], src, start=True, stop=True)
                        ins.then_inc(lora_filled, 1)
                if part == 3:
                    pe.wait_ge(sq_ready, n + 1)
                    for h in range(2):
                        pe.wait_ge(lora_taken, 4 * n + h + 3)
                        nc.tensor.matmul(pre_bank[h][:], ones[:], sq[:, 4 * h:4 * h + 4, :], start=True, stop=True).then_inc(norm_filled, 1)
                if part == 4 and chunk.lat:
                    pe.wait_ge(rk_ready, chunk.n_lat + 1)
                    for h in range(2):
                        pe.wait_ge(norm_taken, 2 * n + h + 1)
                        nc.tensor.matmul(pre_bank[h][:], ones[:], rk[:, 4 * h:4 * h + 4, :], start=True, stop=True).then_inc(bonus_filled, 1)

            def body(chunk, after):
                bank_of, count_at, per_chunk = TABLES[chunk.lat]
                n, lat = chunk.n, chunk.lat

                def fill(name):
                    return banks[bank_of[name]]

                def wait_act(name):
                    pe.wait_ge(act_taken, chunk.act + count_at[name] + 1)

                def wait_dve(name):
                    pe.wait_ge(dve_taken, chunk.dve + count_at[name] + 1)

                pe.wait_ge(act_taken, chunk.act + 1)
                pe.wait_ge(dve_taken, chunk.dve + 1)
                pe.wait_ge(tilde_ready, n + 1)
                for kind, src in (("bT", Bt), ("kT", Kt), ("vT", v)):
                    for h in range(2):
                        out = fill((kind, h))
                        for q in range(4):
                            ins = nc.tensor.transpose(out[:, q * C:(q + 1) * C], src[:, 4 * h + q, :], ident[:])
                        ins.then_inc(filled_act, 1)
                width = 2 if lat else 1
                for q in range(4):
                    if q == 0:
                        wait_act(("kT", 1))
                    elif q == 1:
                        wait_act(("vT", 1))
                        wait_dve(("Mb", 0, 1))
                    else:
                        wait_dve(("Mb", q - 1, 1))
                    for m, src in (("Mb", Bt), ("Mk", Kt)):
                        for s in range(2):
                            out = fill((m, q, s))
                            half = slice(s * HD, (s + 1) * HD)
                            for pp in range(2):
                                p = 2 * q + pp
                                ins = nc.tensor.matmul(out[:, pp * width * C:(pp + 1) * width * C], src[half, p, :],
                                                       AR[half, p, 0:width, :], start=True, stop=True)
                            ins.then_inc(filled_dve, 1)
                for level in range(1, LEVELS):
                    for q in range(4):
                        if level == 1:
                            pe.wait_ge(one_plus_m, 4 * n + q + 1)
                            wait_dve(("Mk", 2, 1) if q < 2 else ("Mk", 3, 1))
                        elif level == 2:
                            wait_dve(("X", 1, q))
                            pe.wait_ge(first_level, 4 * n + q + 1)
                        else:
                            wait_act((("T", level - 1, 1), ("Tt", level - 1, 1), ("T", level - 1, 2), ("T", level - 1, 3))[q])
                        out = fill(("X", level, q))
                        for j in range(4):
                            sl = 4 * q + j
                            ins = nc.tensor.matmul(out[:, j * C:(j + 1) * C], Mb[:, sl, 0, :],
                                                   ident[:] if level == 1 else T[:, sl, :], start=True, stop=True)
                        ins.then_inc(filled_dve, 1)
                    for q in range(4 if level > 1 else 0):
                        if level > 2 and q == 0:
                            wait_act(("Tt", level - 1, 3))
                        wait_dve(("X", level, q if q < 2 else 3))
                        if q == 3:
                            wait_act(("Tt", level, 0))
                        for name, first, second in (("T", Tt, X), ("Tt", X, Tt)):
                            out = fill((name, level, q))
                            for j in range(4):
                                sl = 4 * q + j
                                ins = nc.tensor.matmul(out[:, j * C:(j + 1) * C], first[:, sl, :], second[:, sl, :], start=True, stop=True)
                            ins.then_inc(filled_act, 1)
                    if after is not None:
                        prepare(after, level)
                early, late = chunk.halves
                wait_act(("T", LEVELS - 1, 3))
                for h in range(2):
                    out = fill(("X", LEVELS, h))
                    for j in range(8):
                        sl = 8 * h + j
                        if j == 0:
                            nc.tensor.matmul(out[:, 0:HD], Mb[:, sl, 0, :], T[:, sl, early], start=True, stop=True)
                        else:
                            ins = nc.tensor.matmul(out[late, j * HD:(j + 1) * HD], Mb[early, sl, 0, late], T[early, sl, early],
                                                   start=True, stop=True)
                    ins.then_inc(filled_dve, 1)
                wait_act(("Tt", LEVELS - 1, 3))
                for h in range(2):
                    wait_dve(("X", LEVELS, h))
                    out = fill(("Tt", LEVELS, h))
                    for j in range(8):
                        sl = 8 * h + j
                        if j == 0:
                            nc.tensor.matmul(out[:, 0:HD], X[:, sl, :], Tt[:, sl, late], start=True, stop=True)
                        else:
                            ins = nc.tensor.matmul(out[early, j * HD:(j + 1) * HD], X[late, sl, early], Tt[late, sl, late],
                                                   start=True, stop=True)
                    ins.then_inc(filled_act, 1)
                if after is not None:
                    prepare(after, LEVELS)
                pe.wait_ge(state_ready, n + 1)
                pe.wait_ge(kept, n + 1)
                for s in range(2):
                    half = slice(s * HD, (s + 1) * HD)
                    out = fill(("rhs", s))
                    for p in range(PAIRS):
                        at = slice(p * HD, (p + 1) * HD)
                        nc.tensor.matmul(out[:, at], Mk[:, slot(p, s), 0, :], VT[:, p * P + s * HD:p * P + (s + 1) * HD], start=True, stop=False)
                        ins = nc.tensor.matmul(out[:, at], AR_kept[half, p, 0, :], S_mid[half, p, :], start=False, stop=True)
                    ins.then_inc(filled_act, 1)

                def begin(out):
                    nc.tensor.matmul(out[:], zeros[:], zeros[:, None, :].to_broadcast([P, 4, P]), start=True, stop=False)

                def y_without_u(h):
                    out = fill(("Y", h))
                    begin(out)
                    for q in range(4):
                        p, at = 4 * h + q, slice(q * C, (q + 1) * C)
                        for s in range(2):
                            half = slice(s * HD, (s + 1) * HD)
                            nc.tensor.matmul(out[half, at], VT[:, p * P + s * HD:p * P + (s + 1) * HD], Mk[:, slot(p, s), 1, :],
                                             start=False, stop=False)
                            nc.tensor.matmul(out[half, at], S_mid[half, p, :], AR_kept[half, p, 1, :], start=False, stop=False)

                wait_act(("Tt", LEVELS, 1))
                if lat:
                    y_without_u(0)
                for s in range(2):
                    wait_act(("rhs", s))
                    out = fill(("U", s))
                    for p in range(PAIRS):
                        ins = nc.tensor.matmul(out[:, p * HD:(p + 1) * HD], Tt[:, slot(p, s), :], rhs[:, p * P + s * HD:p * P + (s + 1) * HD],
                                               start=True, stop=True)
                    ins.then_inc(filled_act, 1)
                if lat:
                    y_without_u(1)
                pairs = [(p, s) for p in range(PAIRS) for s in range(2)]
                state = fill(("S",))
                begin(state)
                for p, s in pairs:
                    col = slice(p * P + s * HD, p * P + (s + 1) * HD)
                    nc.tensor.matmul(state[s * HD:(s + 1) * HD, p * HD:(p + 1) * HD], KTT[:, col], VT[:, col], start=False, stop=False)
                wait_act(("U", 1))
                for p, s in pairs if lat else ():
                    h, q, half, col = p // 4, p % 4, slice(s * HD, (s + 1) * HD), slice(p * P + s * HD, p * P + (s + 1) * HD)
                    ins = nc.tensor.matmul(fill(("Y", h))[half, q * C:(q + 1) * C], U[:, col], Mb[:, slot(p, s), 1, :], start=False,
                                           stop=q == 3)
                    if (q, s) == (3, 1):
                        ins.then_inc(filled_dve, 1)
                for p, s in pairs:
                    col = slice(p * P + s * HD, p * P + (s + 1) * HD)
                    ins = nc.tensor.matmul(state[s * HD:(s + 1) * HD, p * HD:(p + 1) * HD], BT[:, col], U[:, col], start=False,
                                           stop=p == PAIRS - 1)
                ins.then_inc(filled_dve, 1)

            for part in range(LEVELS + 1):
                prepare(Chunk(*FIRST_CHUNK), part)
            chunk_loop(pe, body)


def rwkv_out(nc, e, a, y_acc, bonus, ones, vec):
    with ExitStack() as ctx:
        sb = lambda n, s, d=FP32: ctx.enter_context(nc.sbuf_tensor("ro_" + n, s, d))
        gd, g2 = sb("gd", [P, 2, LAT]), sb("g2", [P, 2, LRU])
        yc, sq, rstd = ([sb(f"{n}{b}", [P, LAT]) for b in range(2)] for n in ("yc", "sq", "rstd"))
        eps = sb("eps", [P, 1])
        psum = lambda n: [ctx.enter_context(nc.psum_tensor(f"ro_{n}{b}", [P, LAT], FP32)) for b in range(2)]
        mean, var, gate = psum("mean"), psum("var"), psum("gate")
        loaded, gd_ready, eps_ready, summed, centred, squared, var_done, rstd_done, gate_done, finished, stored, a_step, v_step = sems(
            nc, ctx, "ro_loaded", "gd_ready", "ro_eps_ready", "ro_summed", "ro_centred", "ro_squared", "ro_var_done", "ro_rstd_done",
            "ro_gate_done", "ro_finished", "ro_stored", "ro_a_step", "ro_v_step")
        rest = 32
        with nc.Block() as block:
            @block.sync
            def _(sp):
                sp.dma_start(gd[:], e.p_dram[GD0:GD0 + 2].rearrange("t p n -> p t n")[:, :, LAT0:]).then_inc(loaded, 16)
                sp.dma_start(g2[:], a["rwkv_g2"]).then_inc(loaded, 16)
                sp.wait_ge(finished, PAIRS)
                sp.dma_start(e.merged_dram[LT:].rearrange("t p n -> p t n"), y_acc[:]).then_inc(stored, 16)
                sp.wait_ge(stored, 16)

            @block.tensor
            def _(pe):
                for p in range(PAIRS):
                    b = p % 2
                    if p >= 2:
                        pe.wait_ge(finished, p - 1)
                    nc.tensor.matmul(mean[b][:], ones[:], y_acc[:, p, :], start=True, stop=True).then_inc(summed, 1)
                    if p == 0:
                        pe.wait_ge(gd_ready, 1)
                    nc.tensor.matmul(gate[b][:], g2[:, 0, p * P:(p + 1) * P], gd[:, 0, :], start=True, stop=False)
                    nc.tensor.matmul(gate[b][:], g2[0:rest, 1, p * P:(p + 1) * P], gd[0:rest, 1, :], start=False, stop=True
                                     ).then_inc(gate_done, 1)
                    pe.wait_ge(squared, p + 1)
                    nc.tensor.matmul(var[b][:], ones[:], sq[b][:], start=True, stop=True).then_inc(var_done, 1)

            @block.scalar
            def _(act):
                act.wait_ge(loaded, 32)
                nc.scalar.activation(gd[:], gd[:], ACT.Sigmoid).then_inc(gd_ready, 1)
                act.wait_ge(eps_ready, 1)
                for p in range(PAIRS):
                    b = p % 2
                    act.wait_ge(var_done, p + 1)
                    nc.scalar.activation(rstd[b][:], var[b][:], ACT.Ln, bias=eps[:], scale=1.0 / HD).then_inc(a_step, 1)
                    act.wait_ge(a_step, p + 1)
                    nc.scalar.activation(rstd[b][:], rstd[b][:], ACT.Exp, scale=-0.5).then_inc(rstd_done, 1)

            @block.vector
            def _(dve):
                nc.vector.memset(eps[:], GN_EPS).then_inc(eps_ready, 1)
                c = Chain(dve, v_step)
                for p in range(PAIRS):
                    b = p % 2
                    y = y_acc[:, p, :]
                    dve.wait_ge(summed, p + 1)
                    c.ordered(nc.vector.scalar_tensor_tensor(out=yc[b][:], in0=mean[b][:], scalar=-1.0 / HD, in1=y, op0=ALU.mult, op1=ALU.add))
                    nc.vector.tensor_tensor(sq[b][:], yc[b][:], yc[b][:], ALU.mult).then_inc(squared, 1)
                    dve.wait_ge(rstd_done, p + 1)
                    c.ordered(nc.vector.tensor_tensor(yc[b][:], yc[b][:], rstd[b][:], ALU.mult))
                    c.ordered(nc.vector.tensor_scalar(yc[b][:], yc[b][:], vec[:, 7, p:p + 1], vec[:, 8, p:p + 1], ALU.mult, ALU.add))
                    c.ordered(nc.vector.tensor_tensor(yc[b][:], yc[b][:], bonus[:, p, :], ALU.add))
                    dve.wait_ge(gate_done, p + 1)
                    nc.vector.tensor_tensor(y, yc[b][:], gate[b][:], ALU.mult).then_inc(finished, 1)


def residual_input(nc, e, a, z, hi, lo):
    with ExitStack() as ctx:
        sb = lambda n, s, d=FP32: ctx.enter_context(nc.sbuf_tensor("ri_" + n, s, d))
        rows, cols = sb("rows", [P, KT // 2, 8]), sb("cols", [P, KT // 2, 64])
        merged = [sb(f"merged{b}", [P, 4, LAT]) for b in range(2)]
        x_loaded, hi_done, lo_done, posed, scaled = sems(nc, ctx, "ri_x_loaded", "ri_hi_done", "ri_lo_done", "ri_posed", "ri_scaled")
        loaded = sems(nc, ctx, "ri_merged0_loaded", "ri_merged1_loaded")
        with nc.Block() as block:
            @block.sync
            def _(sp):
                sp.dma_start(rows[:], a["pos_rows"]).then_inc(x_loaded, 16)
                sp.dma_start(cols[:], a["pos_cols"]).then_inc(x_loaded, 16)
                sp.dma_start(z[:], a["x"].rearrange("t p n -> p t n")).then_inc(x_loaded, 16)
                for q in range(4):
                    if q >= 2:
                        sp.wait_ge(hi_done, q - 1)
                        sp.wait_ge(lo_done, q - 1)
                    sp.dma_start(merged[q % 2][:], e.merged_dram[4 * q:4 * q + 4].rearrange("t p n -> p t n")).then_inc(loaded[q % 2], 16)

            @block.scalar
            def _(act):
                for q in range(4):
                    act.wait_ge(loaded[q % 2], 16 * (q // 2 + 1))
                    nc.scalar.activation(hi[:, 4 * q:4 * q + 4, :], merged[q % 2][:], ACT.Copy).then_inc(hi_done, 1)

            @block.vector
            def _(dve):
                for q in range(4):
                    dve.wait_ge(hi_done, q + 1)
                    at = slice(4 * q, 4 * q + 4)
                    nc.vector.tensor_tensor(lo[:, at, :], merged[q % 2][:], hi[:, at, :].bitcast(FP32), ALU.subtract).then_inc(lo_done, 1)
                dve.wait_ge(x_loaded, 48)
                for k in range(KT):
                    table = (rows[:, k, :, None].to_broadcast([P, 8, 64]) if k < KT // 2
                             else cols[:, k - KT // 2, None, :].to_broadcast([P, 8, 64]))
                    grid = z[:, k, :].rearrange("p (r c) -> p r c", c=64)
                    ins = nc.vector.tensor_tensor(grid, grid, table, ALU.add)
                ins.then_inc(posed, 1)
                dve.wait_ge(posed, 1)
                nc.vector.tensor_scalar(z[:], z[:], ALPHA, None, ALU.mult).then_inc(scaled, 1)
                dve.wait_ge(scaled, 1)


def layer_norm(nc, a, name, z, gain, bias, finish):
    with ExitStack() as ctx:
        sb = lambda n, s, d=FP32: ctx.enter_context(nc.sbuf_tensor(name + n, s, d))
        mean_of = sb("mean_of", [P, P])
        eps, rstd = sb("eps", [P, 1]), sb("rstd", [P, LAT])
        sq = [sb(f"sq{b}", [P, LAT]) for b in range(2)]
        mean, var = (ctx.enter_context(nc.psum_tensor(name + n, [P, LAT], FP32)) for n in ("mean", "var"))
        const, mean_done, centred, squared, sq_used, var_done, rstd_done, scaled, normed, a_step, g_loaded = sems(
            nc, ctx, *(name + n for n in ("const", "mean_done", "centred", "squared", "sq_used", "var_done", "rstd_done", "scaled",
                                          "normed", "a_step", "g_loaded")))
        gb = sb("gain_bias", [P, 2, KT])
        on_act, on_dve, on_sp = finish(ctx, sb, normed)
        with nc.Block() as block:
            @block.sync
            def _(sp):
                sp.dma_start(gb[:, 0, :], gain).then_inc(g_loaded, 16)
                sp.dma_start(gb[:, 1, :], bias).then_inc(g_loaded, 16)
                on_sp(sp)

            @block.tensor
            def _(pe):
                pe.wait_ge(const, 1)
                for k in range(KT):
                    ins = nc.tensor.matmul(mean[:], mean_of[:], z[:, k, :], start=(k == 0), stop=(k == KT - 1))
                ins.then_inc(mean_done, 1)
                for k in range(KT):
                    pe.wait_ge(squared, k + 1)
                    nc.tensor.matmul(var[:], mean_of[:], sq[k % 2][:], start=(k == 0), stop=(k == KT - 1)).then_inc(sq_used, 1)

            @block.scalar
            def _(act):
                for k in range(KT):
                    act.wait_ge(centred, k + 1)
                    if k >= 2:
                        act.wait_ge(sq_used, k - 1)
                    nc.scalar.activation(sq[k % 2][:], z[:, k, :], ACT.Square).then_inc(squared, 1)
                act.wait_ge(sq_used, KT)
                nc.scalar.activation(rstd[:], var[:], ACT.Ln, bias=eps[:]).then_inc(a_step, 1)
                act.wait_ge(a_step, 1)
                nc.scalar.activation(rstd[:], rstd[:], ACT.Exp, scale=-0.5).then_inc(rstd_done, 1)
                on_act(act)

            @block.vector
            def _(dve):
                nc.vector.memset(mean_of[:], 1.0 / D)
                nc.vector.memset(eps[:], LN_EPS).then_inc(const, 1)
                dve.wait_ge(mean_done, 1)
                for k in range(KT):
                    nc.vector.tensor_tensor(z[:, k, :], z[:, k, :], mean[:], ALU.subtract).then_inc(centred, 1)
                dve.wait_ge(rstd_done, 1)
                dve.wait_ge(g_loaded, 32)
                for k in range(KT):
                    nc.vector.tensor_tensor(z[:, k, :], z[:, k, :], rstd[:], ALU.mult).then_inc(scaled, 1)
                    if k:
                        dve.wait_ge(scaled, k)
                        nc.vector.tensor_scalar(z[:, k - 1, :], z[:, k - 1, :], gb[:, 0, k - 1:k], gb[:, 1, k - 1:k], ALU.mult, ALU.add
                                                ).then_inc(normed, 1)
                        if k >= 2:
                            on_dve(dve, k - 2)
                dve.wait_ge(scaled, KT)
                nc.vector.tensor_scalar(z[:, KT - 1, :], z[:, KT - 1, :], gb[:, 0, KT - 1:KT], gb[:, 1, KT - 1:KT], ALU.mult, ALU.add
                                        ).then_inc(normed, 1)
                on_dve(dve, KT - 2)
                on_dve(dve, KT - 1)


def out_projection(nc, e, a):
    with ExitStack() as ctx:
        sb = lambda n, s, d=FP32: ctx.enter_context(nc.sbuf_tensor(n, s, d))
        z = sb("z1", [P, KT, LAT])
        with ExitStack() as inner:
            hi, lo = e.h_hi, e.h_lo
            landing = [inner.enter_context(nc.sbuf_tensor(f"o_landing{b}", [P, LAT], FP32)) for b in range(2)]
            residual_input(nc, e, a, z, hi, lo)

            def add(dve, unit, b):
                at = bass.ds(unit, 1)
                zt = z[:, at, :].rearrange("p o n -> p (o n)")
                return nc.vector.scalar_tensor_tensor(out=zt, in0=landing[b][:], scalar=e.mod[:, bass.ds(unit + 2 * KT, 1), 0],
                                                      in1=zt, op0=ALU.mult, op1=ALU.add)

            projection(nc, "o_", a["w_out"], 0, KT, hi, lo, [(0, LAT, 0)], add, landing, None)

        def finish(ctx, sb, normed):
            h2 = [sb(f"h2{b}", [P, LAT]) for b in range(2)]
            modded, hi_done, lo_done, stored = sems(nc, ctx, "h2_modded", "h2_hi_done", "h2_lo_done", "x1_stored")

            def on_dve(dve, k):
                dve.wait_ge(normed, k + 1)
                nc.vector.tensor_scalar(h2[k % 2][:], z[:, k, :], e.one_plus_scale2[:, k:k + 1], e.mod[:, 3 * KT + k, 0:1], ALU.mult, ALU.add
                                        ).then_inc(modded, 1)
                dve.wait_ge(hi_done, k + 1)
                nc.vector.tensor_tensor(e.h_lo[:, k, :], h2[k % 2][:], e.h_hi[:, k, :].bitcast(FP32), ALU.subtract).then_inc(lo_done, 1)

            def on_act(act):
                for k in range(KT):
                    act.wait_ge(modded, k + 1)
                    nc.scalar.activation(e.h_hi[:, k, :], h2[k % 2][:], ACT.Copy).then_inc(hi_done, 1)

            def on_sp(sp):
                sp.wait_ge(normed, KT)
                sp.dma_start(e.x1_dram, z[:]).then_inc(stored, 16)
                sp.wait_ge(stored, 16)

            return on_act, on_dve, on_sp

        layer_norm(nc, a, "ln1_", z, a["ln1_g"], a["ln1_b"], finish)


def queries(nc, e, a):
    with ExitStack() as ctx:
        landing = [ctx.enter_context(nc.sbuf_tensor(f"q_landing{b}", [P, LAT], FP32)) for b in range(2)]
        q = [ctx.enter_context(nc.sbuf_tensor(f"q_out{b}", [P, LAT], FP32)) for b in range(2)]

        def copy(dve, unit, b):
            return nc.vector.tensor_copy(q[b][:], landing[b][:])

        def store(eng, unit, b):
            return eng.dma_start(e.q_dram[bass.ds(unit, 1)].rearrange("o p n -> p (o n)"), q[b][:])

        projection(nc, "q_", a["peer_wq"], 0, KT, e.h_hi, e.h_lo, [(0, LAT, 0)], copy, landing, store)


R_STEPS = 21
ONE_HOTS = 8
SPREAD = 16
BANKFUL = 4


def route(nc, e, a):
    with ExitStack() as ctx:
        sb = lambda n, s, d=FP32: ctx.enter_context(nc.sbuf_tensor("rt_" + n, s, d))
        keys, q = sb("keys", [P, HP, NK]), sb("q", [P, HP, P])
        ident, iota = sb("ident", [P, P]), sb("iota", [P, P])
        score, rest = sb("score", [P, HP, NK]), sb("rest", [P, HP, NK])
        one_of = score
        val, idx, idx_f = sb("val", [P, HP, TOPK]), sb("idx", [P, HP, TOPK], U32), sb("idx_f", [P, HP, TOPK])
        top, pos = sb("top", [P, PEER_HEADS, TOPK]), sb("pos", [P, PEER_HEADS, TOPK], U32)
        k12, k12_f = sb("k12", [P, 2, P], U32), sb("k12_f", [P, 2, P])
        chosen = sb("chosen", [P, 3, P])
        total, landed = sb("total", [P, PEER_HEADS]), sb("landed", [P, 1])
        sel = sb("sel", [P, 3, P])
        now = [sb(f"now{b}", [P, 3, SPREAD]) for b in range(2)]
        hot1, hot2 = ([sb(f"{n}{b}", [P, NK]) for b in range(ONE_HOTS)] for n in ("hot1_", "hot2_"))
        dense = sb("dense", [P, NK, P])
        s_acc = [ctx.enter_context(nc.psum_tensor(f"rt_s{b}", [P, 4 * NK], FP32)) for b in range(2)]
        t_acc = ctx.enter_context(nc.psum_tensor("rt_t", [P, 3 * P], FP32))
        g_acc = [ctx.enter_context(nc.psum_tensor(f"rt_g{b}", [P, BANKFUL * NK], FP32)) for b in range(4)]
        (const_loaded, q_loaded, scored, score_read, shifted, exp_done, chosen_ready, turned, sel_ready, sel_used, hot_ready, hot_used,
         dense_free, bank_read, stored, v_step) = sems(
            nc, ctx, "rt_const_loaded", "rt_q_loaded", "scored", "score_read", "top_shifted", "top_exp_done", "chosen_ready", "turned",
            "sel_ready", "sel_used", "hot_ready", "hot_used", "dense_free", "gate_bank_read", "gates_stored", "rt_v_step")
        tiles, turns, fills = LAT // P, P // SPREAD, P // BANKFUL
        per_turn = SPREAD // BANKFUL
        with nc.Block() as block:
            @block.sync
            def _(sp):
                sp.sem_inc(dense_free, 1)
                for dst, src in ((keys, a["peer_keys"]), (ident, a["ident"]), (iota, a["iota"])):
                    sp.dma_start(dst[:], src).then_inc(const_loaded, 16)
                with sp.Fori(0, tiles) as t:
                    at = bass.ds(t * P, P)
                    sp.wait_ge(scored, 4 * t + 1)
                    sp.dma_start(q[:], e.q_dram.rearrange("t p n -> p t n")[:, :, at]).then_inc(q_loaded, 16)
                    sp.wait_ge(bank_read, (t + 1) * fills + 4)
                    sp.dma_start(e.gates_dram[:, :, at], dense[:]).then_inc(stored, 16)
                    sp.wait_ge(stored, 16 * t + 16)
                    sp.sem_inc(dense_free, 1)

            @block.tensor
            def _(pe):
                pe.sem_inc(hot_used, ONE_HOTS)
                pe.sem_inc(scored, 1)
                pe.sem_inc(turned, 1)
                pe.wait_ge(const_loaded, 48)
                with pe.Fori(0, tiles) as t:
                    pe.wait_ge(q_loaded, 16 * t + 16)
                    for g in range(4):
                        pe.wait_ge(score_read, 4 * t + g + 1)
                        for j in range(4):
                            last = nc.tensor.matmul(s_acc[g % 2][:, j * NK:(j + 1) * NK], q[:, 4 * g + j, :], keys[:, 4 * g + j, :],
                                                    start=True, stop=True)
                        last.then_inc(scored, 1)
                    pe.wait_ge(chosen_ready, t + 2)
                    pe.wait_ge(sel_ready, t + 1)
                    for j in range(3):
                        last = nc.tensor.transpose(t_acc[:, j * P:(j + 1) * P], chosen[:, j, :], ident[:])
                    last.then_inc(turned, 1)
                    with pe.Fori(0, turns) as i:
                        turn = pe.snap(t * turns + i)
                        for n in range(SPREAD):
                            if n % BANKFUL == 0:
                                pe.wait_ge(bank_read, turn * per_turn + n // BANKFUL + 1)
                            pe.wait_ge(hot_ready, turn * SPREAD + n + 1)
                            ins = nc.tensor.matmul(g_acc[n // BANKFUL % 4][:, (n % BANKFUL) * NK:(n % BANKFUL + 1) * NK],
                                                   hot1[n % ONE_HOTS][:], hot2[n % ONE_HOTS][:], start=True, stop=True)
                            ins.then_inc(hot_used, 1)

            @block.scalar
            def _(act):
                act.sem_inc(score_read, 2)
                act.sem_inc(sel_ready, 1)
                act.sem_inc(bank_read, 4)
                with act.Fori(0, tiles) as t:
                    for g in range(4):
                        act.wait_ge(scored, 4 * t + g + 2)
                        if g == 0:
                            act.wait_ge(chosen_ready, t + 1)
                        nc.scalar.activation(score[:, 4 * g:4 * g + 4, :].rearrange("p h n -> p (h n)"), s_acc[g % 2][:], ACT.Copy
                                             ).then_inc(score_read, 1)
                    act.wait_ge(shifted, t + 1)
                    nc.scalar.activation(chosen[:, 2, :], top[:].rearrange("p h k -> p (h k)"), ACT.Exp).then_inc(exp_done, 1)
                    act.wait_ge(turned, t + 2)
                    act.wait_ge(sel_used, turns * t + 1)
                    nc.scalar.activation(sel[:].rearrange("p a n -> p (a n)"), t_acc[:], ACT.Copy).then_inc(sel_ready, 1)
                    act.wait_ge(dense_free, t + 1)
                    with act.Fori(0, turns) as i:
                        turn = act.snap(t * turns + i)
                        for f in range(per_turn):
                            act.wait_ge(hot_used, turn * SPREAD + (f + 1) * BANKFUL + ONE_HOTS)
                            at = bass.ds(i * SPREAD + f * BANKFUL, BANKFUL)
                            nc.scalar.activation(dense[:, :, at].rearrange("p i t -> p t i"),
                                                 g_acc[f % 4][:].rearrange("p (t i) -> p t i", i=NK), ACT.Copy).then_inc(bank_read, 1)

            @block.vector
            def _(dve):
                dve.sem_inc(chosen_ready, 1)
                dve.sem_inc(sel_used, 1)
                dve.wait_ge(const_loaded, 48)
                with dve.Fori(0, tiles) as t:
                    c = Chain(dve, v_step, t * R_STEPS)

                    def best(vals, positions, source, other, n):
                        for half in range(2):
                            at = slice(8 * half, 8 * half + 8)
                            src = other if half else source
                            nc.vector.tensor_copy(landed[:], iota[:, 0:1])
                            for r in range(n):
                                ins = nc.vector.max(vals[:, r, at], src[:, r, :])
                            c.ordered(ins)
                            nc.vector.tensor_copy(landed[:], iota[:, 0:1])
                            for r in range(n):
                                ins = nc.vector.max_index(positions[:, r, at], vals[:, r, at], src[:, r, :])
                            if not half:
                                for r in range(n):
                                    ins = nc.vector.match_replace(other[:, r, :], vals[:, r, at], src[:, r, :], LOWEST)
                            c.ordered(ins)

                    dve.wait_ge(score_read, 4 * t + 6)
                    best(val, idx, score, rest, HP)
                    c.ordered(nc.vector.tensor_copy(idx_f[:], idx[:]))
                    halves = val[:].rearrange("p (h s) k -> p h s k", s=2)
                    cand = score[:].rearrange("p (h s) n -> p h (s n)", s=2)
                    left = rest[:].rearrange("p (h s) n -> p h (s n)", s=2)
                    full = [P, PEER_HEADS, TOPK, TOPK]
                    c.ordered(nc.vector.tensor_tensor(cand.rearrange("p h (i j) -> p h i j", j=TOPK), halves[:, :, 0, :, None].to_broadcast(full),
                                                      halves[:, :, 1, None, :].to_broadcast(full), ALU.add))
                    best(top, pos, cand, left, PEER_HEADS)
                    flat_pos = pos[:].rearrange("p h k -> p (h k)")
                    nc.vector.tensor_scalar(k12[:, 0, :], flat_pos, 4, None, ALU.logical_shift_right)
                    nc.vector.tensor_scalar(k12[:, 1, :], flat_pos, 15, None, ALU.bitwise_and)
                    best_of = total[:]
                    c.ordered(nc.vector.tensor_copy(best_of, top[:, :, 0]))
                    c.ordered(nc.vector.tensor_copy(k12_f[:], k12[:]))
                    dve.wait_ge(turned, t + 1)
                    nc.vector.tensor_tensor(top[:], top[:], best_of[:, :, None].to_broadcast([P, PEER_HEADS, TOPK]), ALU.subtract
                                            ).then_inc(shifted, 1)
                    by_half = idx_f[:].rearrange("p (h s) k -> p h s k", s=2)
                    for s in range(2):
                        one = one_of[:].rearrange("p h n -> p (h n)").rearrange("p (k j) -> p k j", j=TOPK)
                        c.ordered(nc.vector.tensor_tensor(one, iota[:, None, 0:TOPK].to_broadcast([P, P, TOPK]),
                                                          k12_f[:, s, :, None].to_broadcast([P, P, TOPK]), ALU.is_equal))
                        four = one.rearrange("p (h k) j -> p h k j", h=PEER_HEADS)
                        c.ordered(nc.vector.tensor_tensor(four, four, by_half[:, :, s, None, :].to_broadcast(full), ALU.mult))
                        c.ordered(nc.vector.tensor_reduce(chosen[:, s, :], one, AX, ALU.add))
                    dve.wait_ge(exp_done, t + 1)
                    gate = chosen[:, 2, :].rearrange("p (h k) -> p h k", k=TOPK)
                    c.ordered(nc.vector.tensor_reduce(total[:], gate, AX, ALU.add))
                    c.ordered(nc.vector.reciprocal(total[:], total[:]))
                    c.ordered(nc.vector.tensor_tensor(gate, gate, total[:, :, None].to_broadcast([P, PEER_HEADS, TOPK]), ALU.mult))
                    dve.sem_inc(chosen_ready, 1)
                    assert c.n == R_STEPS, c.n
                    with dve.Fori(0, turns // 2) as i:
                        for half in range(2):
                            turn = t * turns + 2 * i + half
                            cur = now[half]
                            if half == 0:
                                dve.wait_ge(sel_ready, t + 2)
                            nc.vector.tensor_copy(cur[:], sel[:, :, bass.ds((2 * i + half) * SPREAD, SPREAD)]).then_inc(sel_used, 1)
                            dve.wait_ge(sel_used, turn + 2)
                            for n in range(SPREAD):
                                dve.wait_ge(hot_used, turn * SPREAD + n + 1)
                                nc.vector.tensor_scalar(hot1[n % ONE_HOTS][:], iota[:], cur[:, 0, n:n + 1], cur[:, 2, n:n + 1],
                                                        ALU.is_equal, ALU.mult)
                                nc.vector.tensor_scalar(hot2[n % ONE_HOTS][:], iota[:], cur[:, 1, n:n + 1], None, ALU.is_equal
                                                        ).then_inc(hot_ready, 1)


def experts(nc, e, a, f):
    chunks, v_units = NK, D // DU
    groups, units = chunks // GROUP, GROUP + v_units
    with ExitStack() as ctx:
        sb = lambda n, s, d=FP32: ctx.enter_context(nc.sbuf_tensor("ex_" + n, s, d))
        raw = [sb(f"raw{b}", [P, KT * P]) for b in range(2)]
        hi, lo = ([sb(f"{n}{b}", [P, KT * P], FP32R) for b in range(2)] for n in ("hi", "lo"))
        w_hi, w_lo = (sb(n, [P, GROUP, LAT], FP32R) for n in ("w_hi", "w_lo"))
        gates, act_, w = ([sb(f"{n}{b}", [P, LAT]) for b in range(2)] for n in ("gates", "act", "w"))
        u_acc = [ctx.enter_context(nc.psum_tensor(f"ex_u{b}", [P, LAT], FP32)) for b in range(2)]
        v_acc = [[ctx.enter_context(nc.psum_tensor(f"ex_v{b}{h}", [P, LAT], FP32)) for h in range(2)] for b in range(2)]
        hi_done, lo_done, products, gelu_done, weighted, w_ready, added, w_step, gates_free = sems(
            nc, ctx, "ex_hi_done", "ex_lo_done", "ex_products", "gelu_ready", "act_weighted", "w_ready", "v_added", "w_step", "gates_free")
        loaded = sems(nc, ctx, "ex_raw0_loaded", "ex_raw1_loaded")
        g_loaded = sems(nc, ctx, "gates0_loaded", "gates1_loaded")
        assert units % 2 == 0 and GROUP % 2 == 0
        with nc.Block() as block:
            @block.sync
            def _(sp):
                with sp.Fori(0, groups) as g:
                    for u in range(units):
                        sp.wait_ge(hi_done, g * units + u + 1)
                        sp.wait_ge(lo_done, g * units + u + 1)
                        src = (a["peer_u"][bass.ds(g * GROUP + u, 1)] if u < GROUP
                               else a["peer_v"][bass.ds(g * v_units + (u - GROUP), 1)])
                        sp.dma_start(raw[u % 2][:], src.rearrange("o p n -> p (o n)")).then_inc(loaded[u % 2], 16)

            @block.gpsimd
            def _(pool):
                with pool.Fori(0, groups) as g:
                    for c in range(GROUP):
                        pool.wait_ge(weighted, g * GROUP + c + 1)
                        pool.dma_start(gates[c % 2][:], e.gates_dram[:, bass.ds(g * GROUP + c, 1), :].rearrange("p o n -> p (o n)")
                                       ).then_inc(g_loaded[c % 2], 16)

            @block.scalar
            def _(act):
                act.sem_inc(hi_done, 2)
                with act.Fori(0, groups) as g:
                    for u in range(units):
                        act.wait_ge(loaded[u % 2], (g * (units // 2) + u // 2 + 1) * 16)
                        act.wait_ge(products, g * units + u + 1)
                        nc.scalar.activation(hi[u % 2][:], raw[u % 2][:], ACT.Copy).then_inc(hi_done, 1)
                        if 0 < u <= GROUP:
                            c = u - 1
                            act.wait_ge(products, g * units + c + 3)
                            act.wait_ge(weighted, g * GROUP + c + 1)
                            nc.scalar.activation(act_[c % 2][:], u_acc[c % 2][:], ACT.Gelu).then_inc(gelu_done, 1)

            @block.vector
            def _(dve):
                dve.sem_inc(lo_done, 2)
                dve.sem_inc(weighted, 2)

                def low(g, u):
                    dve.wait_ge(hi_done, g * units + u + 3)
                    nc.vector.tensor_tensor(lo[u % 2][:], raw[u % 2][:], hi[u % 2][:].bitcast(FP32), ALU.subtract).then_inc(lo_done, 1)

                def weigh(g, c):
                    n = g * GROUP + c
                    dve.wait_ge(gelu_done, n + 1)
                    dve.wait_ge(g_loaded[c % 2], (g * (GROUP // 2) + c // 2 + 1) * 16)
                    nc.vector.tensor_tensor(w[c % 2][:], act_[c % 2][:], gates[c % 2][:], ALU.mult).then_inc(weighted, 1)
                    dve.wait_ge(weighted, n + 3)
                    nc.vector.tensor_copy(w_hi[:, c, :], w[c % 2][:]).then_inc(w_step, 1)
                    dve.wait_ge(w_step, n + 1)
                    nc.vector.tensor_tensor(w_lo[:, c, :], w[c % 2][:], w_hi[:, c, :].bitcast(FP32), ALU.subtract).then_inc(w_ready, 1)

                def add(g, v):
                    dve.wait_ge(products, g * units + GROUP + v + 3)
                    for h in range(2):
                        t = f[:, 2 * v + h, :]
                        nc.vector.tensor_tensor(t, t, v_acc[v % 2][h][:], ALU.add).then_inc(added, 1)

                def group(g, last):
                    for u in range(1, units):
                        low(g, u)
                        if u <= GROUP:
                            weigh(g, u - 1)
                        else:
                            add(g, u - GROUP - 1)
                    if not last:
                        low(g + 1, 0)
                    add(g, v_units - 1)

                nc.vector.memset(f[:], 0.0).then_inc(added, 4)
                dve.wait_ge(added, 4)
                low(0, 0)
                with dve.Fori(0, groups - 1) as g:
                    group(g, False)
                group(groups - 1, True)

            @block.tensor
            def _(pe):
                pe.sem_inc(products, 2)

                def three(out, ws, xs, first, last):
                    for n, (wt, x) in enumerate(((ws[0], xs[0]), (ws[0], xs[1]), (ws[1], xs[0]))):
                        ins = nc.tensor.matmul(out, wt, x, start=first and n == 0, stop=last and n == 2)
                    return ins

                with pe.Fori(0, groups) as g:
                    for u in range(units):
                        b = u % 2
                        pe.wait_ge(lo_done, g * units + u + 3)
                        if u < GROUP:
                            pe.wait_ge(gelu_done, g * GROUP + u - 1) if u >= 2 else None
                            for k in range(KT):
                                ks = slice(k * P, (k + 1) * P)
                                ins = three(u_acc[b][:], (hi[b][:, ks], lo[b][:, ks]), (e.h_hi[:, k, :], e.h_lo[:, k, :]), k == 0, k == KT - 1)
                        else:
                            v = u - GROUP
                            for h in range(2):
                                pe.wait_ge(added, (g * v_units + v) * 2 + h + 1)
                                for c in range(GROUP):
                                    if v == 0 and h == 0:
                                        pe.wait_ge(w_ready, g * GROUP + c + 1)
                                    ds = slice(c * DU + h * P, c * DU + (h + 1) * P)
                                    ins = three(v_acc[v % 2][h][:], (hi[b][:, ds], lo[b][:, ds]), (w_hi[:, c, :], w_lo[:, c, :]),
                                                c == 0, c == GROUP - 1)
                        ins.then_inc(products, 1)


def final(nc, e, a, f, out):
    with ExitStack() as ctx:
        x1 = [ctx.enter_context(nc.sbuf_tensor(f"x1_{b}", [P, LAT], FP32)) for b in range(2)]
        scaled, added, step = sems(nc, ctx, "x1_scaled", "x1_added", "gate2_step")
        loaded = sems(nc, ctx, "x1_0_loaded", "x1_1_loaded")
        with nc.Block() as block:
            @block.sync
            def _(sp):
                for k in range(KT):
                    if k >= 2:
                        sp.wait_ge(added, k - 1)
                    sp.dma_start(x1[k % 2][:], e.x1_dram[:, k, :]).then_inc(loaded[k % 2], 16)

            @block.vector
            def _(dve):
                for k in range(KT):
                    nc.vector.tensor_scalar(f[:, k, :], f[:, k, :], e.mod[:, 5 * KT + k, 0:1], None, ALU.mult).then_inc(step, 1)
                for k in range(KT):
                    dve.wait_ge(step, KT)
                    dve.wait_ge(loaded[k % 2], 16 * (k // 2 + 1))
                    nc.vector.scalar_tensor_tensor(out=f[:, k, :], in0=x1[k % 2][:], scalar=ALPHA, in1=f[:, k, :], op0=ALU.mult, op1=ALU.add
                                                   ).then_inc(added, 1)

        def finish(ctx, sb, normed):
            (stored,) = sems(nc, ctx, "out_stored")

            def on_sp(sp):
                for q in range(4):
                    sp.wait_ge(normed, 4 * q + 4)
                    sp.dma_start(out[4 * q:4 * q + 4].rearrange("t p n -> p t n"), f[:, 4 * q:4 * q + 4, :]).then_inc(stored, 16)
                sp.wait_ge(stored, 64)

            return (lambda act: None), (lambda dve, k: None), on_sp

        layer_norm(nc, a, "ln2_", f, a["ln2_g"], a["ln2_b"], finish)


def build(nc, a, out, dbg=None, only=False):
    e = Env()
    with ExitStack() as ctx:
        sb = lambda n, s, d=FP32: ctx.enter_context(nc.sbuf_tensor(n, s, d))
        e.p_dram = nc.dram_tensor("p_scratch", [TILES, P, TW], FP32, kind="Internal").ap()
        e.merged_dram = nc.dram_tensor("merged_scratch", [KT, P, LAT], FP32, kind="Internal").ap()
        e.bias, e.mod = sb("ada_bias", [P, MOD_TILES, 2]), sb("mod", [P, MOD_TILES, 2])
        e.one_plus_scale, e.one_plus_scale2 = sb("one_plus_scale", [P, KT, 2]), sb("one_plus_scale2", [P, KT])
        e.x1_dram = nc.dram_tensor("x1_scratch", [P, KT, LAT], FP32, kind="Internal").ap()
        e.q_dram = nc.dram_tensor("q_scratch", [KT, P, LAT], FP32, kind="Internal").ap()
        e.gates_dram = nc.dram_tensor("gates_scratch", [NK, NK, LAT], FP32, kind="Internal").ap()
        if dbg == "tail":
            e.merged_dram = a["merged"]
            with nc.semaphore("dbg_mod") as dm, nc.Block() as block:
                @block.sync
                def _(sp):
                    sp.dma_start(e.mod[:], a["mod"]).then_inc(dm, 16)
                    sp.wait_ge(dm, 16)
                    sp.dma_start(e.one_plus_scale2[:], a["ops2"]).then_inc(dm, 16)
                    sp.wait_ge(dm, 32)
            return tail(nc, e, a, out)
        if only:
            e.p_dram = a["p"]
            {"lru": rglru, "rwkv": rwkv}[dbg](nc, e, a)
            return dump(nc, e.merged_dram[0:LT] if dbg == "lru" else e.merged_dram[LT:], out)
        modulation(nc, e, a)
        if dbg == "mod":
            return dump(nc, e.mod[:].rearrange("p a b -> p (a b)"), out)
        in_projection(nc, e, a)
        if dbg == "p":
            dump(nc, e.p_dram[0:BOTH_TILES], out[0:BOTH_TILES])
            return dump(nc, e.p_dram[BOTH_TILES:, :, LAT0:], out[BOTH_TILES:, :, LAT0:])
        rglru(nc, e, a)
        if dbg == "lru":
            return dump(nc, e.merged_dram[0:LT], out)
        rwkv(nc, e, a)
        tail(nc, e, a, out)


def tail(nc, e, a, out):
    with ExitStack() as ctx:
        with ExitStack() as inner:
            e.h_hi, e.h_lo = (inner.enter_context(nc.sbuf_tensor(n, [P, KT, LAT], FP32R)) for n in ("h_hi", "h_lo"))
            out_projection(nc, e, a)
            queries(nc, e, a)
            route(nc, e, a)
            f = inner.enter_context(nc.sbuf_tensor("f", [P, KT, LAT], FP32))
            experts(nc, e, a, f)
            final(nc, e, a, f, out)


def dump(nc, src, out):
    with nc.semaphore(f"dumped{id(src)}") as s, nc.Block() as block:
        @block.sync
        def _(sp):
            sp.dma_start(out, src).then_inc(s, 16)
            sp.wait_ge(s, 16)


def position_tables():
    quarter = D // 4
    freq = (1.0 / (10000.0 ** (np.arange(quarter, dtype=np.float32) / quarter))).astype(np.float32)

    def table(n):
        ang = (np.arange(n, dtype=np.float32)[:, None] * freq[None, :]).astype(np.float32)
        t = np.concatenate([np.sin(ang), np.cos(ang)], axis=-1).T.astype(np.float32)
        return np.ascontiguousarray(t.reshape(KT // 2, P, n).transpose(1, 0, 2))

    return table(LAT // 64), table(64)


def shape_constants():
    i = np.arange(P)
    row, col = i[:, None], i[None, :]
    f = lambda m: np.asarray(m, np.float32)
    tri = np.stack([np.stack([f(row < col), f(row <= col)], 1), np.stack([f(row > col), f(row >= col)], 1)], 1)
    levels = []
    for d in range(2):
        late, early = (row, col) if d == 0 else (col, row)
        levels.append(np.stack([f((row == col) | ((row >> k == col >> k) & (late >> (k - 1) & 1 == 1) & (early >> (k - 1) & 1 == 0)))
                                for k in range(1, LEVELS + 1)], 1))
    return {"iota": f(0 * row + col), "two_by_two": np.eye(2, dtype=np.float32), "ident": f(row == col), "rwkv_ones": f(row // HD == col // HD), "rwkv_tri": np.ascontiguousarray(tri),
            "rwkv_level": np.ascontiguousarray(np.stack(levels, 1))}


def weight_tiles(w):
    n = w.shape[1] // P
    return np.ascontiguousarray(w.reshape(KT, P, n, P).transpose(2, 1, 0, 3)).reshape(n, P, KT * P)


def columns(v):
    return np.ascontiguousarray(np.asarray(v).reshape(-1, P).T)


def lay_out(inputs):
    g = {k: np.asarray(v) for k, v in inputs.items()}
    a = {}
    a["cond"] = np.ascontiguousarray(np.stack([columns(g["c"][0]), columns(g["c_ctx"])], axis=-1))
    a["ada_w"] = np.ascontiguousarray(g["ada_w"][0].reshape(KT, P, MOD_UNITS, MW).transpose(2, 1, 0, 3)).reshape(MOD_UNITS, P, KT * MW)
    b = columns(g["ada_b"][0])
    a["ada_b"] = np.ascontiguousarray(np.stack([b, b], axis=-1))
    a["pos_rows"], a["pos_cols"] = position_tables()
    a["ctx"] = np.ascontiguousarray(g["ctx"][0].T).reshape(KT, P, CTX)
    a["x"] = np.ascontiguousarray(g["x"][0].T).reshape(KT, P, LAT)
    w = g["w_in"][0]
    o = 2 * LRU
    r, k, v, lora, gd = o, o + LRU, o + 2 * LRU, o + 3 * LRU, o + 3 * LRU + 2 * P
    order = [w[:, 0:LRU], w[:, k:v], w[:, v:lora], w[:, lora:gd], w[:, LRU:o], w[:, r:k],
             w[:, gd:], np.zeros((D, 2 * P - (w.shape[1] - gd)), w.dtype)]
    a["w_in"] = weight_tiles(np.concatenate(order, axis=1))
    m = g["rwkv_mu"][0]
    z = np.zeros((2, LRU), m.dtype)
    m = np.concatenate([z, m[:, LRU:2 * LRU], m[:, 2 * LRU:3 * LRU], m[:, 3 * LRU:3 * LRU + 2 * P], z, m[:, 0:LRU],
                        m[:, 3 * LRU + 2 * P:], np.zeros((2, 2 * P - (w.shape[1] - gd)), m.dtype)], axis=1)
    a["mu"] = np.ascontiguousarray(np.stack([columns(m[0]), columns(m[1])], axis=-1))
    more_layout(g, a)
    return a


def more_layout(g, a):
    v = [columns(g["lru_conv_w"][0, t]) for t in range(4)] + [columns(g["lru_conv_b"][0])]
    v += [columns(g[n][0, d]) for n in ("lru_ba", "lru_bx", "lru_lambda") for d in range(2)]
    a["lru_vec"] = np.ascontiguousarray(np.stack(v, axis=1))
    for n in ("lru_wa", "lru_wx"):
        a[n] = np.ascontiguousarray(g[n][0].reshape(2 * LT, 2, HD, HD).transpose(1, 2, 0, 3))
    v = [columns(g[n][0, d]) for n in ("rwkv_w0", "rwkv_a0") for d in range(2)]
    v += [columns(g[n][0].reshape(-1)) for n in ("rwkv_k_k", "rwkv_k_a", "rwkv_r_k", "rwkv_gn_g", "rwkv_gn_b")]
    a["rwkv_vec"] = np.ascontiguousarray(np.stack(v, axis=1))
    a["rwkv_w2"], a["rwkv_a2"] = g["rwkv_w2"][0].reshape(P, LRU), g["rwkv_a2"][0].reshape(P, LRU)
    g2 = g["rwkv_g2"][0]
    a["rwkv_g2"] = np.ascontiguousarray(np.concatenate([g2, np.zeros((2 * P - len(g2), LRU), g2.dtype)]).reshape(2, P, LRU).transpose(1, 0, 2))
    a.update(shape_constants())
    a["w_out"], a["peer_wq"] = weight_tiles(g["w_out"][0]), weight_tiles(g["peer_wq"][0])
    for n in ("ln1_g", "ln1_b", "ln2_g", "ln2_b"):
        a[n] = columns(g[n][0])
    a["peer_keys"] = np.ascontiguousarray(g["peer_subkeys"][0].reshape(HP, NK, P).transpose(2, 0, 1))
    a["peer_u"] = np.ascontiguousarray(g["peer_u"][0].reshape(NK, NK, KT, P).transpose(1, 3, 2, 0)).reshape(NK, P, KT * P)
    a["peer_v"] = np.ascontiguousarray(g["peer_v"][0].reshape(NK, NK // GROUP, GROUP, D // DU, DU).transpose(1, 3, 0, 2, 4)
                                       ).reshape(NK, P, GROUP * DU)


_OUT = (KT, P, LAT)


def kernel(**inputs):
    import concourse.bacc as bacc
    from concourse.bass_utils import run_bass_kernel_spmd

    arrays = lay_out(inputs)
    nc = bacc.Bacc("TRN2", target_bir_lowering=False, num_devices=1)
    a = {n: nc.dram_tensor("in_" + n, v.shape, mybir.dt.from_np(v.dtype), kind="ExternalInput").ap() for n, v in arrays.items()}
    out = nc.dram_tensor("out_dram", _OUT, FP32, kind="ExternalOutput").ap()
    build(nc, a, out)
    r = run_bass_kernel_spmd(nc, [{"in_" + n: v for n, v in arrays.items()}], core_ids=[0])
    return np.ascontiguousarray(r.results[0]["out_dram"].reshape(D, LAT).T)[None]
```

```python
from contextlib import ExitStack

import numpy as np
import concourse.bass as bass
from concourse import mybir

FP32 = mybir.dt.float32
FP32R = mybir.dt.float32r
BF16 = mybir.dt.bfloat16
U32 = mybir.dt.uint32
ALU = mybir.AluOpType
ACT = mybir.ActivationFunctionType
AX = mybir.AxisListType.X

P = 128
D = 2048
KT = D // P
LAT, CTX = 512, 256
LAT0 = CTX + 1
TW = LAT0 + LAT
LRU = 1024
LT = LRU // P
N_U, N_K, N_V, N_L = LT, LT, LT, 2
BOTH_TILES = N_U + N_K + N_V + N_L
LAT_TILES = LT + LT + 2
TILES = BOTH_TILES + LAT_TILES
U0, K0, V0, LORA0 = 0, N_U, N_U + N_K, N_U + N_K + N_V
GATE0, R0, GD0 = BOTH_TILES, BOTH_TILES + LT, BOTH_TILES + 2 * LT
HD = 64
HEADS = 16
C = 128
PEER_HEADS, NK, TOPK = 8, 128, 16
HP = 2 * PEER_HEADS
GROUP = 8
DU = 256
ALPHA = 2.0 ** 0.25
LN_EPS, GN_EPS = 1e-5, 64e-5
DECAY = float(np.exp(-0.5))
LOWEST = -3.0e38
SECTIONS = 6
MOD_TILES = SECTIONS * KT
MW = 512
MOD_UNITS = 2 * D // MW
LATE = MOD_TILES - 2 * KT
MOD_BUFS = 4


class Env:
    pass


def sems(nc, ctx, *names):
    handles = [nc.alloc_semaphore(n) for n in names]

    def release():
        nc.clear_and_free_semaphores(handles)
        nc.all_engine_barrier()

    ctx.callback(release)
    return handles


def modulation(nc, e, a):
    with ExitStack() as ctx:
        sb = lambda n, s, d=FP32: ctx.enter_context(nc.sbuf_tensor(n, s, d))
        cond = sb("cond", [P, KT, 2])
        cond_act = e.cond_act
        two = sb("two_by_two", [2, 2])
        w = [sb(f"ada_w{b}", [P, KT, MW]) for b in range(MOD_BUFS)]
        row = [sb(f"ada_row{b}", [2, MW]) for b in range(2)]
        acc = [ctx.enter_context(nc.psum_tensor(f"ada_acc{b}", [2, MW], FP32)) for b in range(2)]
        turned = [ctx.enter_context(nc.psum_tensor(f"ada_turned{b}", [P, MW // P, 2], FP32)) for b in range(2)]
        cond_loaded, bias_loaded, act_ready, used, row_ready, columns_ready, evicted = sems(
            nc, ctx, "cond_loaded", "adab_loaded", "cond_act_ready", "ada_w_used", "ada_row_ready", "ada_columns_ready", "ada_evicted")
        loaded = sems(nc, ctx, *[f"ada_w{b}_loaded" for b in range(MOD_BUFS)])
        with nc.Block() as block:
            @block.sync
            def _(sp):
                sp.dma_start(cond[:], a["cond"]).then_inc(cond_loaded, 16)
                for u in range(MOD_UNITS):
                    if u >= MOD_BUFS:
                        sp.wait_ge(used, u - MOD_BUFS + 1)
                    sp.dma_start(w[u % MOD_BUFS][:], a["ada_w"][u].rearrange("p (k n) -> p k n", k=KT)
                                 ).then_inc(loaded[u % MOD_BUFS], 16)

            @block.scalar
            def _(act):
                act.dma_start(e.bias[:], a["ada_b"]).then_inc(bias_loaded, 16)
                act.dma_start(two[:], a["two_by_two"]).then_inc(bias_loaded, 16)
                act.wait_ge(cond_loaded, 16)
                nc.scalar.activation(cond_act[:], cond[:], ACT.Silu).then_inc(act_ready, 1)
                for u in range(MOD_UNITS):
                    act.wait_ge(used, u + 1)
                    if u >= 2:
                        act.wait_ge(columns_ready, u - 1)
                    nc.scalar.activation(row[u % 2][:], acc[u % 2][:], ACT.Copy).then_inc(row_ready, 1)

            @block.tensor
            def _(pe):
                def turn(u):
                    pe.wait_ge(row_ready, u + 1)
                    if u >= 2:
                        pe.wait_ge(evicted, u - 1)
                    for j in range(MW // P):
                        last = nc.tensor.matmul(turned[u % 2][:, j, :], row[u % 2][:, j * P:(j + 1) * P], two[:],
                                                start=True, stop=True)
                    last.then_inc(columns_ready, 1)

                pe.wait_ge(act_ready, 1)
                pe.wait_ge(bias_loaded, 32)
                for u in range(MOD_UNITS):
                    pe.wait_ge(loaded[u % MOD_BUFS], 16 * (u // MOD_BUFS + 1))
                    if u >= 2:
                        pe.wait_ge(row_ready, u - 1)
                    for k in range(KT):
                        last = nc.tensor.matmul(acc[u % 2][:], cond_act[:, k, :], w[u % MOD_BUFS][:, k, :],
                                                start=(k == 0), stop=(k == KT - 1))
                    last.then_inc(used, 1)
                    if u >= 1:
                        turn(u - 1)
                turn(MOD_UNITS - 1)

            @block.vector
            def _(dve):
                dve.wait_ge(bias_loaded, 32)
                for u in range(MOD_UNITS):
                    dve.wait_ge(columns_ready, u + 1)
                    t = slice(u * (MW // P), (u + 1) * (MW // P))
                    nc.vector.tensor_tensor(e.mod[:, t, :], turned[u % 2][:], e.bias[:, t, :], ALU.add).then_inc(evicted, 1)


def projection(nc, name, weights, first, count, rhs_hi, rhs_lo, spans, evict_vector, evict_bufs, store, follow=None):
    with ExitStack() as ctx:
        sb = lambda n, s, d=FP32: ctx.enter_context(nc.sbuf_tensor(name + n, s, d))
        raw = [sb(f"raw{b}", [P, KT * P]) for b in range(2)]
        hi = [sb(f"hi{b}", [P, KT * P], FP32R) for b in range(2)]
        lo = [sb(f"lo{b}", [P, KT * P], FP32R) for b in range(2)]
        acc = [[ctx.enter_context(nc.psum_tensor(f"{name}acc{b}{s}", [P, w], FP32)) for s, (_, w, _) in enumerate(spans)]
               for b in range(2)]
        hi_done, lo_done, products, landed, evicted = sems(
            nc, ctx, name + "hi_done", name + "lo_done", name + "products", name + "landed", name + "evicted")
        loaded = sems(nc, ctx, name + "loaded0", name + "loaded1")
        stored, output_free = sems(nc, ctx, name + "stored", name + "output_free")
        assert count % 2 == 0
        with nc.Block() as block:
            @block.sync
            def _(sp):
                for b in range(2):
                    sp.dma_start(raw[b][:], weights[first + b]).then_inc(loaded[b], 16)
                with sp.Fori(0, count // 2 - 1) as i:
                    for b in range(2):
                        sp.wait_ge(hi_done, 2 * i + b + 1)
                        sp.wait_ge(lo_done, 2 * i + b + 1)
                        sp.dma_start(raw[b][:], weights[bass.ds(2 * i + (b + 2 + first), 1)].rearrange("o p n -> p (o n)")
                                     ).then_inc(loaded[b], 16)

            @block.scalar
            def _(act):
                act.sem_inc(landed, 2)

                def high(i, b):
                    act.wait_ge(loaded[b], 16 * i + 16)
                    act.wait_ge(products, 2 * i + b + 1)
                    nc.scalar.activation(hi[b][:], raw[b][:], ACT.Copy).then_inc(hi_done, 1)

                def land(i, b):
                    act.wait_ge(products, 2 * i + b + 3)
                    act.wait_ge(evicted, 2 * i + b + 1)
                    for s, (_, w, col) in enumerate(spans):
                        last = nc.scalar.activation(evict_bufs[b][:, col:col + w], acc[b][s][:], ACT.Copy)
                    last.then_inc(landed, 1)

                high(0, 0)
                high(0, 1)
                with act.Fori(0, count // 2 - 1) as i:
                    for b in range(2):
                        high(i + 1, b)
                        land(i, b)
                land(count // 2 - 1, 0)
                land(count // 2 - 1, 1)

            @block.vector
            def _(dve):
                dve.sem_inc(evicted, 2)

                def low(i, b):
                    dve.wait_ge(hi_done, 2 * i + b + 1)
                    nc.vector.tensor_tensor(lo[b][:], raw[b][:], hi[b][:].bitcast(FP32), ALU.subtract).then_inc(lo_done, 1)

                def evict(i, b):
                    dve.wait_ge(landed, 2 * i + b + 3)
                    if store is not None:
                        dve.wait_ge(output_free, 2 * i + b + 1)
                    dve.wait_ge(evicted, 2 * i + b + 2)
                    evict_vector(dve, 2 * i + b, b).then_inc(evicted, 1)

                low(0, 0)
                low(0, 1)
                with dve.Fori(0, count // 2 - 1) as i:
                    for b in range(2):
                        low(i + 1, b)
                        evict(i, b)
                evict(count // 2 - 1, 0)
                evict(count // 2 - 1, 1)

            @block.tensor
            def _(pe):
                pe.sem_inc(products, 2)

                def multiply(i, b):
                    pe.wait_ge(lo_done, 2 * i + b + 1)
                    pe.wait_ge(landed, 2 * i + b + 1)
                    for k in range(KT):
                        ks = slice(k * P, (k + 1) * P)
                        for n, (wt, x) in enumerate(((hi, rhs_hi), (hi, rhs_lo), (lo, rhs_hi))):
                            for s, (c0, w, _) in enumerate(spans):
                                last = nc.tensor.matmul(acc[b][s][:], wt[b][:, ks], x[:, k, c0:c0 + w],
                                                        start=(k == 0 and n == 0), stop=(k == KT - 1 and n == 2))
                    last.then_inc(products, 1)

                def go_on(i, b):
                    if follow is not None:
                        pe.wait_ge(landed, 2 * i + b + 3)
                        follow(pe, 2 * i + b, b)

                multiply(0, 0)
                with pe.Fori(0, count // 2 - 1) as i:
                    multiply(i, 1)
                    go_on(i, 0)
                    multiply(i + 1, 0)
                    go_on(i, 1)
                multiply(count // 2 - 1, 1)
                go_on(count // 2 - 1, 0)
                go_on(count // 2 - 1, 1)

            @block.gpsimd
            def _(pool):
                if store is not None:
                    pool.sem_inc(output_free, 2)
                    with pool.Fori(0, count // 2) as i:
                        for b in range(2):
                            pool.wait_ge(evicted, 2 * i + b + 3)
                            store(pool, 2 * i + b, b).then_inc(stored, 16)
                            pool.wait_ge(stored, 32 * i + 16 * b + 16)
                            pool.sem_inc(output_free, 1)


IN_BUFS = 4


def modulated_input(nc, e, a, x_hi, x_lo):
    with ExitStack() as ctx:
        sb = lambda n, s, d=FP32: ctx.enter_context(nc.sbuf_tensor(n, s, d))
        rows, cols = sb("pos_rows", [P, KT // 2, 8]), sb("pos_cols", [P, KT // 2, 64])
        xc = [sb(f"in_ctx{b}", [P, CTX]) for b in range(IN_BUFS)]
        xl = [sb(f"in_lat{b}", [P, LAT]) for b in range(IN_BUFS)]
        hc = [sb(f"mod_ctx{b}", [P, CTX]) for b in range(2)]
        hl = [sb(f"mod_lat{b}", [P, LAT]) for b in range(2)]
        tables_loaded, one_plus, posed, modded, hi_done, lo_done = sems(
            nc, ctx, "pos_loaded", "scale_ready", "posed", "modded", "x_hi_done", "x_lo_done")
        loaded = sems(nc, ctx, *[f"x{b}_loaded" for b in range(IN_BUFS)])
        sc1 = e.one_plus_scale
        with nc.Block() as block:
            @block.sync
            def _(sp):
                sp.dma_start(rows[:], a["pos_rows"]).then_inc(tables_loaded, 16)
                sp.dma_start(cols[:], a["pos_cols"]).then_inc(tables_loaded, 16)
                for k in range(KT):
                    b = k % IN_BUFS
                    if k >= IN_BUFS:
                        sp.wait_ge(modded, k - IN_BUFS + 1)
                    sp.dma_start(xc[b][:], a["ctx"][k]).then_inc(loaded[b], 16)
                    sp.dma_start(xl[b][:], a["x"][k]).then_inc(loaded[b], 16)

            @block.gpsimd
            def _(pool):
                pool.wait_ge(tables_loaded, 32)
                for k in range(KT):
                    b = k % IN_BUFS
                    pool.wait_ge(loaded[b], 32 * (k // IN_BUFS + 1))
                    table = (rows[:, k, :, None].to_broadcast([P, 8, 64]) if k < KT // 2
                             else cols[:, k - KT // 2, None, :].to_broadcast([P, 8, 64]))
                    grid = xl[b][:].rearrange("p (r c) -> p r c", c=64)
                    nc.gpsimd.tensor_tensor(grid, grid, table, ALU.add).then_inc(posed, 1)

            @block.vector
            def _(dve):
                nc.vector.tensor_scalar(sc1[:], e.mod[:, KT:2 * KT, :], 1.0, None, ALU.add).then_inc(one_plus, 1)
                dve.wait_ge(one_plus, 1)
                for k in range(KT):
                    b = k % 2
                    dve.wait_ge(posed, k + 1)
                    if k >= 2:
                        dve.wait_ge(lo_done, k - 1)
                    nc.vector.tensor_scalar(hc[b][:], xc[k % IN_BUFS][:], sc1[:, k, 1:2], e.mod[:, k, 1:2], ALU.mult, ALU.add)
                    nc.vector.tensor_scalar(hl[b][:], xl[k % IN_BUFS][:], sc1[:, k, 0:1], e.mod[:, k, 0:1], ALU.mult, ALU.add
                                            ).then_inc(modded, 1)
                    dve.wait_ge(hi_done, k + 1)
                    nc.vector.tensor_tensor(x_lo[:, k, 0:CTX], hc[b][:], x_hi[:, k, 0:CTX].bitcast(FP32), ALU.subtract)
                    nc.vector.tensor_tensor(x_lo[:, k, CTX:], hl[b][:], x_hi[:, k, CTX:].bitcast(FP32), ALU.subtract
                                            ).then_inc(lo_done, 1)

            @block.scalar
            def _(act):
                for k in range(KT):
                    b = k % 2
                    act.wait_ge(modded, k + 1)
                    nc.scalar.activation(x_hi[:, k, 0:CTX], hc[b][:], ACT.Copy)
                    nc.scalar.activation(x_hi[:, k, CTX:], hl[b][:], ACT.Copy).then_inc(hi_done, 1)


def in_projection(nc, e, a):
    with ExitStack() as ctx:
        sb = lambda n, s, d=FP32: ctx.enter_context(nc.sbuf_tensor(n, s, d))
        x_hi, x_lo = sb("x_hi", [P, KT, CTX + LAT], FP32R), sb("x_lo", [P, KT, CTX + LAT], FP32R)
        modulated_input(nc, e, a, x_hi, x_lo)
        mu = sb("mu", [P, TILES, 2])
        landing = [sb(f"p_landing{b}", [P, TW + 2]) for b in range(2)]
        mixed = [sb(f"p_mixed{b}", [P, TW]) for b in range(2)]
        diff, half = sb("p_diff", [P, TW]), sb("p_half", [P, TW])
        (mu_loaded, cleared) = sems(nc, ctx, "mu_loaded", "landing_cleared")
        with nc.Block() as block:
            @block.sync
            def _(sp):
                sp.dma_start(mu[:], a["mu"]).then_inc(mu_loaded, 16)
                sp.wait_ge(mu_loaded, 16)

            @block.vector
            def _(dve):
                for b in range(2):
                    nc.vector.memset(landing[b][:], 0.0)
                nc.vector.memset(diff[:], 0.0)
                nc.vector.memset(half[:], 0.0)
                for b in range(2):
                    nc.vector.memset(mixed[b][:], 0.0)
        for tag, first, count, lat_only in (("pb_", 0, BOTH_TILES, False), ("pl_", BOTH_TILES, LAT_TILES, True)):
            (step,) = sems(nc, ctx, tag + "shift_step")
            cols = slice(LAT0, TW) if lat_only else slice(0, TW)
            n_cols = cols.stop - cols.start
            prev, cur, nxt = (slice(cols.start + s, cols.start + s + n_cols) for s in range(3))

            def shift(dve, unit, b, first=first, step=step, cols=cols, prev=prev, cur=cur, nxt=nxt):
                at = bass.ds(unit + first, 1)
                m = landing[b]
                n = unit * 3
                nc.vector.tensor_tensor(diff[:, cols], m[:, prev], m[:, cur], ALU.subtract).then_inc(step, 1)
                dve.wait_ge(step, n + 1)
                nc.vector.scalar_tensor_tensor(out=half[:, cols], in0=diff[:, cols], scalar=mu[:, at, 0], in1=m[:, cur],
                                               op0=ALU.mult, op1=ALU.add).then_inc(step, 1)
                dve.wait_ge(step, n + 2)
                nc.vector.tensor_tensor(diff[:, cols], m[:, nxt], m[:, cur], ALU.subtract).then_inc(step, 1)
                dve.wait_ge(step, n + 3)
                return nc.vector.scalar_tensor_tensor(out=mixed[b][:, cols], in0=diff[:, cols], scalar=mu[:, at, 1],
                                                      in1=half[:, cols], op0=ALU.mult, op1=ALU.add)

            def store(eng, unit, b, first=first, cols=cols):
                dst = e.p_dram[bass.ds(unit + first, 1)].rearrange("o p n -> p (o n)")
                return eng.dma_start(dst[:, cols], mixed[b][:, cols])

            spans = [(CTX, LAT, LAT0 + 1)] if lat_only else [(CTX, LAT, LAT0 + 1), (0, CTX, 1)]
            projection(nc, tag, a["w_in"], first, count, x_hi, x_lo, spans, shift, landing, store)

ZW = 2 + CTX + 3 + LAT + 1
XW = ZW - 3
XL = CTX + 3
X_SEGS = ((0, CTX), (XL, LAT))
GT = 4
LATE_BUFS = 3
BANK = 512


class Chain:

    def __init__(self, engine, sem, base=0):
        self.engine, self.sem, self.base, self.n = engine, sem, base, 0

    def step(self, ins):
        self.n += 1
        return ins.then_inc(self.sem, 1)

    def ordered(self, ins):
        self.step(ins)
        self.engine.wait_ge(self.sem, self.base + self.n)


def rglru(nc, e, a):
    with ExitStack() as ctx:
        sb = lambda n, s, d=FP32: ctx.enter_context(nc.sbuf_tensor("lru_" + n, s, d))
        z, xc = sb("z", [P, LT, ZW]), sb("xc", [P, LT, XW])
        gate_a, gate_x, th = sb("gate_a", [P, LT, XW]), sb("gate_x", [P, LT, XW]), sb("tanh", [P, LT, XW])
        y, gate, h = sb("y", [P, LT, LAT]), sb("gate", [P, LT, LAT]), sb("h", [P, LAT])
        h_ctx = sb("h_ctx", [P, CTX])
        w = [sb("wa", [P, 2 * LT, P]), sb("wx", [P, 2 * LT, P])]
        vec = sb("vec", [P, 11, LT])
        inv, one = z[:, :, 0:XW], sb("one", [P, 1])
        decay, neg_decay = sb("decay", [P, 2, LT]), sb("neg_decay", [P, 2, LT])
        tmp = [sb(f"tmp{i}", [P, 2, LT]) for i in range(4)]
        ctx_acc = [ctx.enter_context(nc.psum_tensor(f"lru_ctx_acc{b}", [P, 2, CTX], FP32)) for b in range(2)]
        lat_acc = [[ctx.enter_context(nc.psum_tensor(f"lru_lat_acc{b}{g}", [P, LAT], FP32)) for g in range(2)] for b in range(2)]
        acc = [[(ctx_acc[b][:, g, :], lat_acc[b][g][:]) for g in range(2)] for b in range(2)]
        vec_loaded, z_loaded, w_cleared, w_loaded, gate_loaded, y_stored = sems(
            nc, ctx, "lru_vec_loaded", "z_loaded", "lru_w_cleared", "lru_w_loaded", "gate_loaded", "y_stored")
        abs_ready, exp_ready, decay_ready, conv_done, gates, gates_read, tanh_done, root, scanned, gelu_done, merged, v_step, a_step = sems(
            nc, ctx, "lam_abs", "lam_exp", "decay_ready", "conv_done", "gate_products", "gates_ready", "tanh_done",
            "root_done", "scanned", "gelu_done", "lru_merged", "lru_v_step", "lru_a_step")
        late_w = [sb(f"late_w{b}", [P, KT * P]) for b in range(LATE_BUFS)]
        late_row = [sb(f"late_row{n}", [P, BANK]) for n in range(4)]
        one_col = sb("one_col", [P, 1])
        late_acc = [ctx.enter_context(nc.psum_tensor(f"late_acc{b}", [P, BANK], FP32)) for b in range(2)]
        turned = [late_acc[0], late_acc[1]] + [t[:].rearrange("p g n -> p (g n)") for t in ctx_acc]
        late_loaded = sems(nc, ctx, *[f"late_w{b}_loaded" for b in range(LATE_BUFS)])
        late_used, late_taken, late_turned, late_added, one_col_loaded = sems(
            nc, ctx, "late_used", "late_rows_taken", "late_turned", "late_added", "one_col_loaded")
        turns = [(d, g) for d in range(2) for g in range(LT // GT)]
        with nc.Block() as block:
            @block.sync
            def _(sp):
                sp.dma_start(vec[:], a["lru_vec"]).then_inc(vec_loaded, 16)
                sp.dma_start(one_col[:], a["ones_column"]).then_inc(one_col_loaded, 16)
                tiles = e.p_dram[U0:U0 + LT].rearrange("t p n -> p t n")
                sp.dma_start(z[:, :, 2:2 + CTX], tiles[:, :, 0:CTX]).then_inc(z_loaded, 16)
                sp.dma_start(z[:, :, 2 + XL:2 + XL + LAT], tiles[:, :, LAT0:]).then_inc(z_loaded, 16)
                sp.wait_ge(w_cleared, 1)
                for g, name in enumerate(("lru_wa", "lru_wx")):
                    for s in range(2):
                        sp.dma_start(w[g][s * HD:(s + 1) * HD, :, s * HD:(s + 1) * HD], a[name][s]).then_inc(w_loaded, 16)
                sp.dma_start(gate[:], e.p_dram[GATE0:GATE0 + LT].rearrange("t p n -> p t n")[:, :, LAT0:]).then_inc(gate_loaded, 16)
                sp.wait_ge(merged, 1)
                sp.dma_start(e.merged_dram[0:LT].rearrange("t p n -> p t n"), y[:]).then_inc(y_stored, 16)
                sp.wait_ge(y_stored, 16)

            @block.gpsimd
            def _(pool):
                nc.gpsimd.memset(w[0][:], 0.0)
                nc.gpsimd.memset(w[1][:], 0.0).then_inc(w_cleared, 1)
                for n in range(LATE):
                    if n >= LATE_BUFS:
                        pool.wait_ge(late_used, n - LATE_BUFS + 1)
                    pool.dma_start(late_w[n % LATE_BUFS][:], a["ada_late"][n]).then_inc(late_loaded[n % LATE_BUFS], 16)

            @block.vector
            def _(dve):
                c = Chain(dve, v_step)
                for seg in ((0, 2), (2 + CTX, 3), (ZW - 1, 1)):
                    nc.vector.memset(z[:, :, seg[0]:seg[0] + seg[1]], 0.0)
                c.ordered(nc.vector.memset(one[:], 1.0))
                for t in (gate_a, gate_x):
                    c.ordered(nc.vector.memset(t[:, :, CTX:XL], 0.0))
                dve.wait_ge(exp_ready, 1)
                lam, (ex, s1, s2, poly) = vec[:, 9:11, :], (t[:] for t in tmp)
                c.ordered(nc.vector.tensor_scalar(s1, ex, 2.0, None, ALU.add))
                c.ordered(nc.vector.reciprocal(s1, s1))
                c.ordered(nc.vector.tensor_tensor(s1, s1, ex, ALU.mult))
                c.ordered(nc.vector.tensor_tensor(s2, s1, s1, ALU.mult))
                c.ordered(nc.vector.memset(poly, 1.0 / 19))
                for k in range(8, -1, -1):
                    c.ordered(nc.vector.tensor_tensor(poly, poly, s2, ALU.mult))
                    c.ordered(nc.vector.tensor_scalar(poly, poly, 1.0 / (2 * k + 1), None, ALU.add))
                c.ordered(nc.vector.tensor_tensor(poly, poly, s1, ALU.mult))
                c.ordered(nc.vector.tensor_scalar(s2, lam, -1.0, 0.0, ALU.mult, ALU.max))
                c.ordered(nc.vector.scalar_tensor_tensor(out=poly, in0=poly, scalar=2.0, in1=s2, op0=ALU.mult, op1=ALU.add))
                c.ordered(nc.vector.tensor_scalar(decay[:], poly, 8.0, None, ALU.mult))
                nc.vector.tensor_scalar(neg_decay[:], poly, -8.0, None, ALU.mult).then_inc(decay_ready, 1)
                dve.wait_ge(z_loaded, 32)
                for j in range(LT):
                    c.step(nc.vector.tensor_scalar(xc[:, j, :], z[:, j, 0:XW], vec[:, 0, j:j + 1], vec[:, 4, j:j + 1], ALU.mult, ALU.add))
                for tap in range(1, 4):
                    for j in range(LT):
                        dve.wait_ge(v_step, c.n - LT + 1)
                        ins = nc.vector.scalar_tensor_tensor(out=xc[:, j, :], in0=z[:, j, tap:tap + XW], scalar=vec[:, tap, j:j + 1],
                                                             in1=xc[:, j, :], op0=ALU.mult, op1=ALU.add)
                        c.step(ins)
                        if tap == 3:
                            dve.wait_ge(v_step, c.n)
                            dve.sem_inc(conv_done, 1)

                def take_rows(n):
                    dve.wait_ge(late_used, 16 * (n + 1))
                    for part in range(0, P, 32):
                        nc.vector.tensor_copy(late_row[n][part:part + 1, :], late_acc[n % 2][part:part + 1, :]).then_inc(late_taken, 1)

                for d, g in turns:
                    tiles = slice(g * GT, (g + 1) * GT)
                    n = d * (LT // GT) + g + 1
                    b_in = gate_x[:, tiles, :]
                    dve.wait_ge(gates_read, 2 * GT * n)
                    c.ordered(nc.vector.tensor_tensor(b_in, b_in, xc[:, tiles, :], ALU.mult))
                    dve.wait_ge(root, n)
                    c.ordered(nc.vector.tensor_tensor(b_in, b_in, th[:, tiles, :], ALU.mult))
                    c.ordered(nc.vector.tensor_tensor(b_in, b_in, inv[:, tiles, :], ALU.mult))
                    take_rows(n - 1)
                    for j in range(tiles.start, tiles.stop):
                        flip = slice(None, None, -1) if d else slice(None)
                        h_out = h[:] if d else y[:, j, :]
                        A, B = gate_a[:, j, :], gate_x[:, j, :]
                        c.ordered(nc.vector.tensor_tensor_scan(h_ctx[:, flip], A[:, 0:CTX][:, flip], B[:, 0:CTX][:, flip], 0.0,
                                                               ALU.mult, ALU.add))
                        end = h_ctx[:, 0:1] if d else h_ctx[:, CTX - 1:CTX]
                        c.ordered(nc.vector.tensor_tensor_scan(h_out[:, flip], A[:, XL:][:, flip], B[:, XL:][:, flip], end,
                                                               ALU.mult, ALU.add))
                        if d:
                            c.ordered(nc.vector.tensor_tensor(y[:, j, :], y[:, j, :], h[:], ALU.add))
                    dve.sem_inc(scanned, 1)
                dve.wait_ge(late_turned, 1)
                by_row = lambda t: t[:, 2 * KT:, 0].rearrange("p (r q c) -> p r q c", r=4, q=4)
                for q in range(4):
                    nc.vector.tensor_tensor(by_row(e.mod)[:, :, q, :], turned[q][:, 0:16].rearrange("p (r c) -> p r c", r=4),
                                            by_row(e.bias)[:, :, q, :], ALU.add).then_inc(late_added, 1)
                dve.wait_ge(late_added, 4)
                nc.vector.tensor_scalar(e.one_plus_scale2[:], e.mod[:, 4 * KT:5 * KT, 0], 1.0, None, ALU.add)
                dve.wait_ge(gelu_done, 1)
                nc.vector.tensor_tensor(y[:], y[:], gate[:], ALU.mult).then_inc(merged, 1)

            @block.scalar
            def _(act):
                c = Chain(act, a_step)
                act.wait_ge(vec_loaded, 16)
                c.ordered(nc.scalar.activation(tmp[1][:], vec[:, 9:11, :], ACT.Abs))
                nc.scalar.activation(tmp[0][:], tmp[1][:], ACT.Exp, scale=-1.0).then_inc(exp_ready, 1)
                for d, g in turns:
                    tiles = range(g * GT, (g + 1) * GT)
                    rows = slice(g * GT, (g + 1) * GT)
                    n = d * (LT // GT) + g + 1
                    if d:
                        act.wait_ge(scanned, g + 1)
                    for j in tiles:
                        m = d * LT + j
                        act.wait_ge(gates, m + 1)
                        for k, (dst, bias) in enumerate(((gate_a, 5 + d), (gate_x, 7 + d))):
                            for s, (c0, w_) in enumerate(X_SEGS):
                                ins = nc.scalar.activation(dst[:, j, c0:c0 + w_], acc[m % 2][k][s], ACT.Sigmoid,
                                                           bias=vec[:, bias, j:j + 1])
                            ins.then_inc(gates_read, 1)
                    act.wait_ge(gates_read, 2 * GT * n)
                    act.wait_ge(decay_ready, 1)
                    for j in tiles:
                        ins = nc.scalar.activation(th[:, j, :], gate_a[:, j, :], ACT.Tanh, scale=decay[:, d, j:j + 1])
                    ins.then_inc(tanh_done, 1)
                    act.wait_ge(tanh_done, n)
                    for j in tiles:
                        ins = nc.scalar.activation(gate_a[:, j, :], gate_a[:, j, :], ACT.Exp, scale=neg_decay[:, d, j:j + 1])
                    c.ordered(ins)
                    act.wait_ge(conv_done, LT)
                    c.ordered(nc.scalar.activation(inv[:, rows, :], th[:, rows, :], ACT.Ln, bias=one[:]))
                    nc.scalar.activation(inv[:, rows, :], inv[:, rows, :], ACT.Exp, scale=-0.5)
                    nc.scalar.activation(th[:, rows, :], th[:, rows, :], ACT.Sqrt, scale=2.0).then_inc(root, 1)
                act.wait_ge(gate_loaded, 16)
                nc.scalar.activation(gate[:], gate[:], ACT.Gelu_apprx_tanh).then_inc(gelu_done, 1)

            @block.tensor
            def _(pe):
                def late(tiles):
                    for n in tiles:
                        rows, at = n // 16, n % 16
                        pe.wait_ge(late_loaded[n % LATE_BUFS], 16 * (n // LATE_BUFS + 1))
                        if at == 0 and rows >= 2:
                            pe.wait_ge(late_taken, 4 * (rows - 1))
                        part, col = 32 * (at // 4), (at % 4) * P
                        for k in range(KT):
                            last = nc.tensor.matmul(late_acc[rows % 2][part:part + 1, col:col + P], e.cond_act[:, k, 0:1],
                                                    late_w[n % LATE_BUFS][:, k * P:(k + 1) * P], start=(k == 0), stop=(k == KT - 1))
                        last.then_inc(late_used, 1)

                late(range(0, 8))
                pe.wait_ge(w_loaded, 64)
                for d in range(2):
                    for j in range(LT):
                        n = d * LT + j
                        pe.wait_ge(conv_done, j + 1)
                        if n >= 2:
                            pe.wait_ge(gates_read, 2 * (n - 1))
                        for g in range(2):
                            for s, (c0, w_) in enumerate(X_SEGS):
                                last = nc.tensor.matmul(acc[n % 2][g][s], w[g][:, d * LT + j, :], xc[:, j, c0:c0 + w_],
                                                        start=True, stop=True)
                        last.then_inc(gates, 1)
                        late(range(min(8 + 4 * n, LATE), min(12 + 4 * n, LATE)))
                pe.wait_ge(late_taken, 16)
                pe.wait_ge(one_col_loaded, 16)
                pe.wait_ge(gates_read, 4 * LT)
                for rows in range(4):
                    for q in range(4):
                        for col in range(4):
                            ins = nc.tensor.matmul(turned[q][:, rows * 4 + col:rows * 4 + col + 1],
                                                   late_row[rows][32 * q:32 * q + 1, col * P:(col + 1) * P], one_col[32 * q:32 * q + 1, :],
                                                   start=True, stop=True)
                ins.then_inc(late_turned, 1)


LEVELS = 7
PAIRS = HEADS // 2
BANKS = 6


def slot(p, s):
    return (p // 2) * 4 + s * 2 + p % 2


def chunk_fills(lat):
    fills = [((t, h), "act") for t in ("bT", "kT", "vT") for h in range(2)]
    fills += [((m, q, s), "dve") for q in range(4) for m in ("Mb", "Mk") for s in range(2)]
    for level in range(1, LEVELS):
        fills += [(("X", level, q), "dve") for q in range(4)]
        if level > 1:
            fills += [((t, level, q), "act") for q in range(4) for t in ("T", "Tt")]
    fills += [(("X", LEVELS, h), "dve") for h in range(2)] + [(("Tt", LEVELS, h), "act") for h in range(2)]
    fills += [(("rhs", s), "act") for s in range(2)] + [(("U", s), "act") for s in range(2)]
    if lat:
        fills += [(("Y", h), "dve") for h in range(2)]
    return fills + [(("S",), "dve")]


def fill_tables(lat):
    bank, count, total = {}, {}, {"act": 0, "dve": 0}
    for n, (name, engine) in enumerate(chunk_fills(lat)):
        bank[name] = n % BANKS
        total[engine] += 1
        count[name] = total[engine]
    return bank, count, total


TABLES = {lat: fill_tables(lat) for lat in (False, True)}
PRE_STEPS = {False: 10, True: 12}


class Chunk:

    def __init__(self, d, lat, count, base, i):
        self.d, self.lat, self.i = d, lat, i
        self.n = base["n"] + i
        self.n_lat = base["n_lat"] + i
        self.act = base["act"] + i * TABLES[lat][2]["act"]
        self.dve = base["dve"] + i * TABLES[lat][2]["dve"]
        self.steps = base["steps"] + i * PRE_STEPS[lat]
        self.loads_end = base["loads"] + i * (64 if lat else 48) + (64 if lat else 48)
        self.first_of_direction = not lat and isinstance(i, int) and i == 0
        halves = (slice(0, HD), slice(HD, C))
        self.halves = (halves[1], halves[0]) if d else halves
        self.token = i * -C + (count - 1) * C if d else i * C


def chunk_loop(engine, body):
    runs, base = [], dict(n=0, n_lat=0, act=0, dve=0, steps=0, loads=0)
    for d in range(2):
        for lat, count in ((False, CTX // C), (True, LAT // C)):
            runs.append((d, lat, count, dict(base)))
            base["n"] += count
            base["n_lat"] += count * lat
            base["act"] += count * TABLES[lat][2]["act"]
            base["dve"] += count * TABLES[lat][2]["dve"]
            base["steps"] += count * PRE_STEPS[lat]
            base["loads"] += count * (64 if lat else 48)
    for k, run in enumerate(runs):
        count = run[2]
        if count > 2:
            with engine.Fori(0, count - 1) as i:
                body(Chunk(*run, i), Chunk(*run, i + 1))
        else:
            body(Chunk(*run, 0), Chunk(*run, 1))
        body(Chunk(*run, count - 1), Chunk(*runs[k + 1], 0) if k + 1 < len(runs) else None)


FIRST_CHUNK = (0, False, CTX // C, dict(n=0, n_lat=0, act=0, dve=0, steps=0, loads=0), 0)


def rwkv(nc, e, a):
    with ExitStack() as ctx:
        sb = lambda n, s, d=FP32: ctx.enter_context(nc.sbuf_tensor("rw_" + n, s, d))
        y_acc, bonus = sb("y_acc", [P, PAIRS, LAT]), sb("bonus_acc", [P, PAIRS, LAT])
        ident, ones = sb("ident", [P, P]), sb("head_ones", [P, P])
        vec = sb("vec", [P, 9, PAIRS])
        with ExitStack() as inner:
            rwkv_scan(nc, e, a, ctx, inner, y_acc, bonus, ident, ones, vec)
        rwkv_out(nc, e, a, y_acc, bonus, ones, vec)


def rwkv_scan(nc, e, a, ctx, inner, y_acc, bonus, ident, ones, vec):
    sb = lambda n, s, d=FP32: inner.enter_context(nc.sbuf_tensor("rw_" + n, s, d))
    full = [P, PAIRS, C]
    k, v, r = sb("k", full), sb("v", full), sb("r", full)
    lora = sb("lora", [P, 2, C])
    w2, a2 = sb("w2", [P, LRU]), sb("a2", [P, LRU])
    zeros = sb("zeros", [P, P], BF16)
    pool_scratch = sb("pool_scratch", [P, 1])
    tri = sb("tri", [P, 2, 2, C])
    level_mask = sb("level_mask", [P, 2, LEVELS, C])
    restart = sb("restart", full)
    tw = sb("tanh_w", [P, C])
    sg, rate, kraw, kd, cum, nrm = (sb(n, full) for n in ("sg", "rate", "kraw", "kd", "cum", "nrm"))
    w_r, w_inv, w_ex = (sb(n, full) for n in ("w_r", "w_inv", "w_ex"))
    sq, rk = w_ex, w_r
    mid, w_mid, w_end = (sb(n, [P, PAIRS]) for n in ("mid", "w_mid", "w_end"))
    AR, Bt, Kt = sb("AR", [P, PAIRS, 2, C]), sb("Bt", full), sb("Kt", full)
    AR_kept = sb("AR_kept", [P, PAIRS, 2, C])
    BT, KTT, VT = (sb(n, [P, LRU]) for n in ("B_T", "K_T", "V_T"))
    Mb, Mk = sb("Mb", [P, HEADS, 2, C]), sb("Mk", [P, HEADS, 2, C])
    X, T, Tt = (sb(n, [P, HEADS, C]) for n in ("X", "T", "Tt"))
    rhs, U = (t[:].rearrange("p h n -> p (h n)")[:, 0:LRU] for t in (X, T))
    S, S_mid, S_sum = (sb(n, [P, PAIRS, HD]) for n in ("S", "S_mid", "S_sum"))
    banks = [inner.enter_context(nc.psum_tensor(f"rw_bank{b}", [P, BANK], FP32)) for b in range(BANKS)]
    pre_bank = [inner.enter_context(nc.psum_tensor(f"rw_pre_bank{h}", [P, BANK], FP32)) for h in range(2)]
    (const_loaded, raw_loaded, tanh_done, sq_ready, rsqrt_ready, rk_ready, cum_ready, weights_ready, tilde_ready) = sems(
        nc, ctx, "rw_const_loaded", "rw_raw_loaded", "rw_tanh_done", "sq_ready", "rsqrt_ready", "rk_ready", "cum_ready",
        "weights_ready", "tilde_ready")
    lora_filled, lora_taken, norm_filled, norm_taken, bonus_filled, bonus_taken = sems(
        nc, ctx, "lora_filled", "lora_taken", "norm_filled", "norm_taken", "bonus_filled", "bonus_taken")
    filled_act, filled_dve, act_taken, dve_taken = sems(nc, ctx, "filled_for_act", "filled_for_dve", "act_taken", "dve_taken")
    state_ready, state_done, kept, one_plus_m, first_level, start_step, pre_step, raw_free, ln_done, state_cleared = sems(
        nc, ctx, "state_ready", "state_done", "AR_is_kept", "one_plus_m", "first_level", "rw_start_step", "rw_pre_step", "raw_free", "ln_done", "state_cleared")

    def bcast(t, n):
        return t[:, :, None].to_broadcast([P, PAIRS, n])

    with nc.Block() as block:
        @block.sync
        def _(sp):
            consts = [(ident, a["ident"]), (ones, a["rwkv_ones"]), (vec, a["rwkv_vec"]), (w2, a["rwkv_w2"]), (a2, a["rwkv_a2"]),
                      (tri, a["rwkv_tri"]), (level_mask, a["rwkv_level"])]

            def load(chunk):
                at = bass.ds(sp.snap(chunk.token + (LAT0 if chunk.lat else 0)), C)
                for dst, tile in ((k, K0), (v, V0)) + (((r, R0),) if chunk.lat else ()):
                    sp.dma_start(dst[:], e.p_dram[tile:tile + LT].rearrange("t p n -> p t n")[:, :, at]).then_inc(raw_loaded, 16)
                sp.dma_start(lora[:], e.p_dram[LORA0:LORA0 + 2].rearrange("t p n -> p t n")[:, :, at]).then_inc(raw_loaded, 16)

            def body(chunk, after):
                if after is not None:
                    sp.wait_ge(raw_free, chunk.n + 1)
                    load(after)

            load(Chunk(*FIRST_CHUNK))
            for dst, src in consts:
                sp.dma_start(dst[:], src).then_inc(const_loaded, 16)
            chunk_loop(sp, body)

        @block.gpsimd
        def _(pool):
            def body(chunk, after):
                pool.wait_ge(tilde_ready, chunk.n + 1)
                pool.wait_ge(state_done, chunk.n + 1)
                width = 2 if chunk.lat else 1
                nc.gpsimd.tensor_tensor(pool_scratch[:], AR[:, 0, 0, 0:1], AR[:, 0, 0, 0:1], ALU.mult)
                nc.gpsimd.tensor_copy(AR_kept[:, :, 0:width, :], AR[:, :, 0:width, :]).then_inc(kept, 1)

            chunk_loop(pool, body)

        @block.scalar
        def _(act):
            act.sem_inc(act_taken, 1)

            def prepare(chunk, part):
                n = chunk.n
                if part == 0:
                    act.wait_ge(raw_loaded, chunk.loads_end)
                    nc.scalar.activation(tw[:], lora[:, 0, :], ACT.Tanh).then_inc(tanh_done, 1)
                if part in (2, 3):
                    dst, row, turn = ((sg, 0, 0), (rate, 2, 2))[part - 2]
                    for h in range(2):
                        act.wait_ge(lora_filled, 4 * n + turn + h + 1)
                        for q in range(4):
                            p = 4 * h + q
                            ins = nc.scalar.activation(dst[:, p, :], pre_bank[h][:, q * C:(q + 1) * C], ACT.Sigmoid,
                                                       bias=vec[:, row + chunk.d, p:p + 1])
                        ins.then_inc(lora_taken, 1)
                if part == 5:
                    act.wait_ge(norm_taken, 2 * n + 2)
                    nc.scalar.activation(nrm[:], nrm[:], ACT.Ln).then_inc(ln_done, 1)
                    act.wait_ge(ln_done, n + 1)
                    nc.scalar.activation(nrm[:], nrm[:], ACT.Exp, scale=-0.5).then_inc(rsqrt_ready, 1)
                if part == 6:
                    act.wait_ge(cum_ready, n + 1)
                    nc.scalar.activation(w_inv[:], cum[:], ACT.Exp, scale=DECAY)
                    nc.scalar.activation(w_r[:], cum[:], ACT.Exp, scale=-DECAY)
                    nc.scalar.activation(w_ex[:], w_ex[:], ACT.Exp, scale=-DECAY)
                    nc.scalar.activation(w_mid[:], mid[:], ACT.Exp, scale=-DECAY).then_inc(weights_ready, 1)

            def body(chunk, after):
                bank_of, count_at, _ = TABLES[chunk.lat]

                def take(name):
                    act.wait_ge(filled_act, chunk.act + count_at[name])
                    return banks[bank_of[name]]

                for kind, dst in (("bT", BT), ("kT", KTT), ("vT", VT)):
                    for h in range(2):
                        nc.scalar.activation(dst[:, h * BANK:(h + 1) * BANK], take((kind, h))[:], ACT.Copy).then_inc(act_taken, 1)
                if after is not None:
                    prepare(after, 0)
                for level in range(1, LEVELS + 1):
                    if 1 < level < LEVELS:
                        for q in range(4):
                            for name, dst in (("T", T), ("Tt", Tt)):
                                nc.scalar.activation(dst[:, 4 * q:4 * q + 4, :].rearrange("p h n -> p (h n)"), take((name, level, q))[:],
                                                     ACT.Copy).then_inc(act_taken, 1)
                    if level == LEVELS:
                        early, late = chunk.halves
                        for h in range(2):
                            nc.scalar.activation(Tt[early, 8 * h:8 * h + 8, late],
                                                 take(("Tt", level, h))[early, :].rearrange("p (h n) -> p h n", n=HD), ACT.Copy
                                                 ).then_inc(act_taken, 1)
                    if after is not None:
                        prepare(after, level)
                for name, dst in (("rhs", rhs), ("U", U)):
                    for s in range(2):
                        nc.scalar.activation(dst.rearrange("p (q s n) -> p q s n", s=2, n=HD)[:, :, s, :],
                                             take((name, s))[:].rearrange("p (q n) -> p q n", n=HD), ACT.Copy).then_inc(act_taken, 1)

            act.wait_ge(const_loaded, 16 * 7)
            for part in range(LEVELS + 1):
                prepare(Chunk(*FIRST_CHUNK), part)
            chunk_loop(act, body)

        @block.vector
        def _(dve):
            dve.sem_inc(dve_taken, 1)
            dve.sem_inc(state_done, 1)
            dve.wait_ge(const_loaded, 16 * 7)
            nc.vector.memset(restart[:], 1.0).then_inc(start_step, 1)
            dve.wait_ge(start_step, 1)
            nc.vector.memset(restart[:, :, 0:1], 0.0)
            nc.vector.memset(zeros[:], 0.0)
            nc.vector.memset(bonus[:], 0.0).then_inc(start_step, 1)
            dve.wait_ge(start_step, 2)

            def prepare(chunk, part, c):
                n, lat, d = chunk.n, chunk.lat, chunk.d
                if part == 1:
                    dve.wait_ge(raw_loaded, chunk.loads_end)
                    c.ordered(nc.vector.tensor_tensor(kraw[:], k[:], bcast(vec[:, 4, :], C), ALU.mult))
                    nc.vector.tensor_tensor(sq[:], kraw[:], kraw[:], ALU.mult).then_inc(sq_ready, 1)
                if part == 3:
                    dve.wait_ge(lora_taken, 4 * n + 2)
                    flat = lambda t: t[:].rearrange("p h n -> p (h n)")
                    flip = slice(None, None, -1) if d else slice(None)
                    c.ordered(nc.vector.tensor_tensor_scan(flat(cum)[:, flip], flat(restart), flat(sg)[:, flip], 0.0, ALU.mult, ALU.add))
                    m = C // 2 if d else C // 2 - 1
                    c.ordered(nc.vector.tensor_copy(mid[:], cum[:, :, m]))
                    c.ordered(nc.vector.tensor_tensor(cum[:], cum[:], bcast(mid, C), ALU.subtract))
                if part == 4:
                    dve.wait_ge(lora_taken, 4 * n + 4)
                    c.ordered(nc.vector.scalar_tensor_tensor(out=kd[:], in0=rate[:], scalar=1.0, in1=bcast(vec[:, 5, :], C),
                                                             op0=ALU.subtract, op1=ALU.mult))
                    c.ordered(nc.vector.scalar_tensor_tensor(out=kd[:], in0=kd[:], scalar=1.0, in1=k[:], op0=ALU.add, op1=ALU.mult))
                    if lat:
                        c.ordered(nc.vector.tensor_tensor(rk[:], r[:], kd[:], ALU.mult))
                        nc.vector.tensor_tensor(rk[:], rk[:], bcast(vec[:, 6, :], C), ALU.mult).then_inc(rk_ready, 1)
                    for h in range(2):
                        dve.wait_ge(norm_filled, 2 * n + h + 1)
                        nc.vector.tensor_scalar(nrm[:, 4 * h:4 * h + 4, :].rearrange("p h n -> p (h n)"), pre_bank[h][:],
                                                1e-24, None, ALU.max).then_inc(norm_taken, 1)
                    c.ordered(nc.vector.tensor_tensor(w_ex[:], cum[:], sg[:], ALU.subtract))
                if part == 5:
                    if lat:
                        for h in range(2):
                            half = slice(4 * h, 4 * h + 4)
                            dve.wait_ge(bonus_filled, 2 * chunk.n_lat + h + 1)
                            nc.vector.tensor_tensor(Kt[:, half, :], pre_bank[h][:].rearrange("p (h n) -> p h n", n=C), v[:, half, :],
                                                    ALU.mult).then_inc(bonus_taken, 1)
                        dve.wait_ge(bonus_taken, 2 * chunk.n_lat + 2)
                        tok = bass.ds(dve.snap(chunk.token), C)
                        c.ordered(nc.vector.tensor_tensor(bonus[:, :, tok], bonus[:, :, tok], Kt[:], ALU.add))
                    dve.sem_inc(cum_ready, 1)
                if part == 6:
                    dve.wait_ge(rsqrt_ready, n + 1)
                    c.ordered(nc.vector.tensor_tensor(kraw[:], kraw[:], nrm[:], ALU.mult))
                    c.ordered(nc.vector.tensor_tensor(rate[:], rate[:], kraw[:], ALU.mult))
                if part == 7:
                    dve.wait_ge(weights_ready, n + 1)
                    nc.vector.scalar_tensor_tensor(out=AR[:, :, 0, :], in0=kraw[:], scalar=-1.0, in1=w_ex[:], op0=ALU.mult, op1=ALU.mult)
                    nc.vector.tensor_tensor(Bt[:], rate[:], w_inv[:], ALU.mult)
                    if lat:
                        nc.vector.tensor_tensor(AR[:, :, 1, :], r[:], w_r[:], ALU.mult)
                    c.ordered(nc.vector.tensor_tensor(Kt[:], kd[:], w_inv[:], ALU.mult))
                    dve.sem_inc(tilde_ready, 1)
                    assert c.n == PRE_STEPS[lat], c.n

            def body(chunk, after):
                bank_of, count_at, per_chunk = TABLES[chunk.lat]
                d, lat = chunk.d, chunk.lat
                c = after and Chain(dve, pre_step, after.steps)

                def take(name):
                    dve.wait_ge(filled_dve, chunk.dve + count_at[name])
                    return banks[bank_of[name]]

                if chunk.first_of_direction:
                    nc.vector.memset(S[:], 0.0).then_inc(state_cleared, 1)
                    dve.wait_ge(state_cleared, d + 1)
                end = 0 if d else C - 1
                nc.vector.tensor_copy(w_end[:], w_r[:, :, end])
                nc.vector.tensor_tensor(S_mid[:], S[:], bcast(w_mid, HD), ALU.mult).then_inc(state_ready, 1)
                for q in range(4):
                    for m_, dst in (("Mb", Mb), ("Mk", Mk)):
                        for s in range(2):
                            src = take((m_, q, s))
                            at = slice(4 * q + 2 * s, 4 * q + 2 * s + 2)
                            if lat:
                                mask = tri[:, d, None, :, :].to_broadcast([P, 2, 2, C])
                                nc.vector.tensor_tensor(dst[:, at, :, :], src[:].rearrange("p (h m n) -> p h m n", h=2, m=2),
                                                        mask, ALU.mult).then_inc(dve_taken, 1)
                            else:
                                mask = tri[:, d, 0, None, :].to_broadcast([P, 2, C])
                                nc.vector.tensor_tensor(dst[:, at, 0, :], src[:, 0:2 * C].rearrange("p (h n) -> p h n", h=2),
                                                        mask, ALU.mult).then_inc(dve_taken, 1)
                    quad = slice(4 * q, 4 * q + 4)
                    dve.wait_ge(dve_taken, chunk.dve + count_at[("Mb", q, 1)] + 1)
                    nc.vector.tensor_tensor(Mb[:, quad, 0, :], Mb[:, quad, 0, :], ident[:, None, :].to_broadcast([P, 4, C]), ALU.add
                                            ).then_inc(one_plus_m, 1)
                    dve.wait_ge(one_plus_m, 4 * chunk.n + q + 1)
                    nc.vector.tensor_tensor(Tt[:, quad, :], Mb[:, quad, 0, :], level_mask[:, 1 - d, 0, None, :].to_broadcast([P, 4, C]),
                                            ALU.mult).then_inc(first_level, 1)
                    if q == 1:
                        dve.wait_ge(act_taken, chunk.act + count_at[("vT", 1)] + 1)
                        dve.sem_inc(raw_free, 1)
                for level in range(1, LEVELS + 1):
                    if level == LEVELS:
                        early, late = chunk.halves
                        for h in range(2):
                            nc.vector.tensor_copy(X[late, 8 * h:8 * h + 8, early],
                                                  take(("X", level, h))[late, :].rearrange("p (h n) -> p h n", n=HD)).then_inc(dve_taken, 1)
                    for q in range(4 if level < LEVELS else 0):
                        mask = level_mask[:, d, level - 1, None, :].to_broadcast([P, 4, C])
                        nc.vector.tensor_tensor((X if level > 1 else T)[:, 4 * q:4 * q + 4, :],
                                                take(("X", level, q))[:].rearrange("p (h n) -> p h n", h=4), mask, ALU.mult
                                                ).then_inc(dve_taken, 1)
                    if after is not None:
                        if level == 7:
                            dve.wait_ge(kept, chunk.n + 1)
                        prepare(after, level, c)
                if lat:
                    tok = bass.ds(dve.snap(chunk.token), C)
                    for h in range(2):
                        half = slice(4 * h, 4 * h + 4)
                        src = take(("Y", h))[:].rearrange("p (h n) -> p h n", n=C)
                        if d:
                            ins = nc.vector.tensor_tensor(y_acc[:, half, tok], y_acc[:, half, tok], src, ALU.add)
                        else:
                            ins = nc.vector.tensor_copy(y_acc[:, half, tok], src)
                        ins.then_inc(dve_taken, 1)
                nc.vector.tensor_tensor(S_sum[:], take(("S",))[:].rearrange("p (h n) -> p h n", n=HD), S_mid[:], ALU.add
                                        ).then_inc(dve_taken, 1)
                dve.wait_ge(dve_taken, chunk.dve + per_chunk["dve"] + 1)
                nc.vector.tensor_tensor(S[:], S_sum[:], bcast(w_end, HD), ALU.mult).then_inc(state_done, 1)
                dve.wait_ge(state_done, chunk.n + 2)

            first = Chunk(*FIRST_CHUNK)
            c = Chain(dve, pre_step, first.steps)
            for part in range(LEVELS + 1):
                prepare(first, part, c)
            chunk_loop(dve, body)

        @block.tensor
        def _(pe):
            pe.wait_ge(start_step, 2)

            def prepare(chunk, part):
                n = chunk.n
                rows = slice(chunk.d * HD, (chunk.d + 1) * HD)
                if part in (1, 2):
                    wt, src = ((w2, tw[rows, :]), (a2, lora[rows, 1, :]))[part - 1]
                    if part == 1:
                        pe.wait_ge(tanh_done, n + 1)
                    for h in range(2):
                        if part == 2:
                            pe.wait_ge(lora_taken, 4 * n + h + 1)
                        for q in range(4):
                            p = 4 * h + q
                            ins = nc.tensor.matmul(pre_bank[h][:, q * C:(q + 1) * C], wt[rows, p * P:(p + 1) * P], src, start=True, stop=True)
                        ins.then_inc(lora_filled, 1)
                if part == 3:
                    pe.wait_ge(sq_ready, n + 1)
                    for h in range(2):
                        pe.wait_ge(lora_taken, 4 * n + h + 3)
                        nc.tensor.matmul(pre_bank[h][:], ones[:], sq[:, 4 * h:4 * h + 4, :], start=True, stop=True).then_inc(norm_filled, 1)
                if part == 4 and chunk.lat:
                    pe.wait_ge(rk_ready, chunk.n_lat + 1)
                    for h in range(2):
                        pe.wait_ge(norm_taken, 2 * n + h + 1)
                        nc.tensor.matmul(pre_bank[h][:], ones[:], rk[:, 4 * h:4 * h + 4, :], start=True, stop=True).then_inc(bonus_filled, 1)

            def body(chunk, after):
                bank_of, count_at, per_chunk = TABLES[chunk.lat]
                n, lat = chunk.n, chunk.lat

                def fill(name):
                    return banks[bank_of[name]]

                def wait_act(name):
                    pe.wait_ge(act_taken, chunk.act + count_at[name] + 1)

                def wait_dve(name):
                    pe.wait_ge(dve_taken, chunk.dve + count_at[name] + 1)

                pe.wait_ge(act_taken, chunk.act + 1)
                pe.wait_ge(dve_taken, chunk.dve + 1)
                pe.wait_ge(tilde_ready, n + 1)
                for kind, src in (("bT", Bt), ("kT", Kt), ("vT", v)):
                    for h in range(2):
                        out = fill((kind, h))
                        for q in range(4):
                            ins = nc.tensor.transpose(out[:, q * C:(q + 1) * C], src[:, 4 * h + q, :], ident[:])
                        ins.then_inc(filled_act, 1)
                width = 2 if lat else 1
                for q in range(4):
                    if q == 0:
                        wait_act(("kT", 1))
                    elif q == 1:
                        wait_act(("vT", 1))
                        wait_dve(("Mb", 0, 1))
                    else:
                        wait_dve(("Mb", q - 1, 1))
                    for m, src in (("Mb", Bt), ("Mk", Kt)):
                        for s in range(2):
                            out = fill((m, q, s))
                            half = slice(s * HD, (s + 1) * HD)
                            for pp in range(2):
                                p = 2 * q + pp
                                ins = nc.tensor.matmul(out[:, pp * width * C:(pp + 1) * width * C], src[half, p, :],
                                                       AR[half, p, 0:width, :], start=True, stop=True)
                            ins.then_inc(filled_dve, 1)
                for level in range(1, LEVELS):
                    for q in range(4):
                        if level == 1:
                            pe.wait_ge(one_plus_m, 4 * n + q + 1)
                            wait_dve(("Mk", 2, 1) if q < 2 else ("Mk", 3, 1))
                        elif level == 2:
                            wait_dve(("X", 1, q))
                            pe.wait_ge(first_level, 4 * n + q + 1)
                        else:
                            wait_act((("T", level - 1, 1), ("Tt", level - 1, 1), ("T", level - 1, 2), ("T", level - 1, 3))[q])
                        out = fill(("X", level, q))
                        for j in range(4):
                            sl = 4 * q + j
                            ins = nc.tensor.matmul(out[:, j * C:(j + 1) * C], Mb[:, sl, 0, :],
                                                   ident[:] if level == 1 else T[:, sl, :], start=True, stop=True)
                        ins.then_inc(filled_dve, 1)
                    for q in range(4 if level > 1 else 0):
                        if level > 2 and q == 0:
                            wait_act(("Tt", level - 1, 3))
                        wait_dve(("X", level, q if q < 2 else 3))
                        if q == 3:
                            wait_act(("Tt", level, 0))
                        for name, first, second in (("T", Tt, X), ("Tt", X, Tt)):
                            out = fill((name, level, q))
                            for j in range(4):
                                sl = 4 * q + j
                                ins = nc.tensor.matmul(out[:, j * C:(j + 1) * C], first[:, sl, :], second[:, sl, :], start=True, stop=True)
                            ins.then_inc(filled_act, 1)
                    if after is not None:
                        prepare(after, level)
                early, late = chunk.halves
                wait_act(("T", LEVELS - 1, 3))
                for h in range(2):
                    out = fill(("X", LEVELS, h))
                    for j in range(8):
                        sl = 8 * h + j
                        if j == 0:
                            nc.tensor.matmul(out[:, 0:HD], Mb[:, sl, 0, :], T[:, sl, early], start=True, stop=True)
                        else:
                            ins = nc.tensor.matmul(out[late, j * HD:(j + 1) * HD], Mb[early, sl, 0, late], T[early, sl, early],
                                                   start=True, stop=True)
                    ins.then_inc(filled_dve, 1)
                wait_act(("Tt", LEVELS - 1, 3))
                for h in range(2):
                    wait_dve(("X", LEVELS, h))
                    out = fill(("Tt", LEVELS, h))
                    for j in range(8):
                        sl = 8 * h + j
                        if j == 0:
                            nc.tensor.matmul(out[:, 0:HD], X[:, sl, :], Tt[:, sl, late], start=True, stop=True)
                        else:
                            ins = nc.tensor.matmul(out[early, j * HD:(j + 1) * HD], X[late, sl, early], Tt[late, sl, late],
                                                   start=True, stop=True)
                    ins.then_inc(filled_act, 1)
                if after is not None:
                    prepare(after, LEVELS)
                pe.wait_ge(state_ready, n + 1)
                pe.wait_ge(kept, n + 1)
                for s in range(2):
                    half = slice(s * HD, (s + 1) * HD)
                    out = fill(("rhs", s))
                    for p in range(PAIRS):
                        at = slice(p * HD, (p + 1) * HD)
                        nc.tensor.matmul(out[:, at], Mk[:, slot(p, s), 0, :], VT[:, p * P + s * HD:p * P + (s + 1) * HD], start=True, stop=False)
                        ins = nc.tensor.matmul(out[:, at], AR_kept[half, p, 0, :], S_mid[half, p, :], start=False, stop=True)
                    ins.then_inc(filled_act, 1)

                def begin(out):
                    nc.tensor.matmul(out[:], zeros[:], zeros[:, None, :].to_broadcast([P, 4, P]), start=True, stop=False)

                def y_without_u(h):
                    out = fill(("Y", h))
                    begin(out)
                    for q in range(4):
                        p, at = 4 * h + q, slice(q * C, (q + 1) * C)
                        for s in range(2):
                            half = slice(s * HD, (s + 1) * HD)
                            nc.tensor.matmul(out[half, at], VT[:, p * P + s * HD:p * P + (s + 1) * HD], Mk[:, slot(p, s), 1, :],
                                             start=False, stop=False)
                            nc.tensor.matmul(out[half, at], S_mid[half, p, :], AR_kept[half, p, 1, :], start=False, stop=False)

                wait_act(("Tt", LEVELS, 1))
                if lat:
                    y_without_u(0)
                for s in range(2):
                    wait_act(("rhs", s))
                    out = fill(("U", s))
                    for p in range(PAIRS):
                        ins = nc.tensor.matmul(out[:, p * HD:(p + 1) * HD], Tt[:, slot(p, s), :], rhs[:, p * P + s * HD:p * P + (s + 1) * HD],
                                               start=True, stop=True)
                    ins.then_inc(filled_act, 1)
                if lat:
                    y_without_u(1)
                pairs = [(p, s) for p in range(PAIRS) for s in range(2)]
                state = fill(("S",))
                begin(state)
                for p, s in pairs:
                    col = slice(p * P + s * HD, p * P + (s + 1) * HD)
                    nc.tensor.matmul(state[s * HD:(s + 1) * HD, p * HD:(p + 1) * HD], KTT[:, col], VT[:, col], start=False, stop=False)
                wait_act(("U", 1))
                for p, s in pairs if lat else ():
                    h, q, half, col = p // 4, p % 4, slice(s * HD, (s + 1) * HD), slice(p * P + s * HD, p * P + (s + 1) * HD)
                    ins = nc.tensor.matmul(fill(("Y", h))[half, q * C:(q + 1) * C], U[:, col], Mb[:, slot(p, s), 1, :], start=False,
                                           stop=q == 3)
                    if (q, s) == (3, 1):
                        ins.then_inc(filled_dve, 1)
                for p, s in pairs:
                    col = slice(p * P + s * HD, p * P + (s + 1) * HD)
                    ins = nc.tensor.matmul(state[s * HD:(s + 1) * HD, p * HD:(p + 1) * HD], BT[:, col], U[:, col], start=False,
                                           stop=p == PAIRS - 1)
                ins.then_inc(filled_dve, 1)

            for part in range(LEVELS + 1):
                prepare(Chunk(*FIRST_CHUNK), part)
            chunk_loop(pe, body)


def rwkv_out(nc, e, a, y_acc, bonus, ones, vec):
    with ExitStack() as ctx:
        sb = lambda n, s, d=FP32: ctx.enter_context(nc.sbuf_tensor("ro_" + n, s, d))
        gd, g2 = sb("gd", [P, 2, LAT]), sb("g2", [P, 2, LRU])
        yc, sq, rstd = ([sb(f"{n}{b}", [P, LAT]) for b in range(2)] for n in ("yc", "sq", "rstd"))
        eps = sb("eps", [P, 1])
        psum = lambda n, count: [ctx.enter_context(nc.psum_tensor(f"ro_{n}{b}", [P, LAT], FP32)) for b in range(count)]
        mean, var, gate = psum("mean", 3), psum("var", 2), psum("gate", 3)
        loaded, gd_ready, eps_ready, summed, centred, squared, var_done, rstd_done, gate_done, finished, stored, a_step, v_step = sems(
            nc, ctx, "ro_loaded", "gd_ready", "ro_eps_ready", "ro_summed", "ro_centred", "ro_squared", "ro_var_done", "ro_rstd_done",
            "ro_gate_done", "ro_finished", "ro_stored", "ro_a_step", "ro_v_step")
        rest = 32
        with nc.Block() as block:
            @block.sync
            def _(sp):
                sp.dma_start(gd[:], e.p_dram[GD0:GD0 + 2].rearrange("t p n -> p t n")[:, :, LAT0:]).then_inc(loaded, 16)
                sp.dma_start(g2[:], a["rwkv_g2"]).then_inc(loaded, 16)
                for q in range(2):
                    at = slice(q * PAIRS // 2, (q + 1) * PAIRS // 2)
                    sp.wait_ge(finished, at.stop)
                    sp.dma_start(e.merged_dram[LT + at.start:LT + at.stop].rearrange("t p n -> p t n"), y_acc[:, at, :]).then_inc(stored, 16)
                sp.wait_ge(stored, 32)

            @block.tensor
            def _(pe):
                def sum_and_gate(p):
                    b = p % 3
                    if p >= 3:
                        pe.wait_ge(finished, p - 2)
                    nc.tensor.matmul(mean[b][:], ones[:], y_acc[:, p, :], start=True, stop=True).then_inc(summed, 1)
                    if p == 0:
                        pe.wait_ge(gd_ready, 1)
                    nc.tensor.matmul(gate[b][:], g2[:, 0, p * P:(p + 1) * P], gd[:, 0, :], start=True, stop=False)
                    nc.tensor.matmul(gate[b][:], g2[0:rest, 1, p * P:(p + 1) * P], gd[0:rest, 1, :], start=False, stop=True
                                     ).then_inc(gate_done, 1)

                sum_and_gate(0)
                for p in range(PAIRS):
                    if p + 1 < PAIRS:
                        sum_and_gate(p + 1)
                    pe.wait_ge(squared, p + 1)
                    nc.tensor.matmul(var[p % 2][:], ones[:], sq[p % 2][:], start=True, stop=True).then_inc(var_done, 1)

            @block.scalar
            def _(act):
                act.wait_ge(loaded, 32)
                nc.scalar.activation(gd[:], gd[:], ACT.Sigmoid).then_inc(gd_ready, 1)
                act.wait_ge(eps_ready, 1)
                for p in range(PAIRS):
                    b = p % 2
                    act.wait_ge(var_done, p + 1)
                    if p >= 2:
                        act.wait_ge(finished, p - 1)
                    nc.scalar.activation(rstd[b][:], var[b][:], ACT.Ln, bias=eps[:], scale=1.0 / HD).then_inc(a_step, 1)
                    act.wait_ge(a_step, p + 1)
                    nc.scalar.activation(rstd[b][:], rstd[b][:], ACT.Exp, scale=-0.5).then_inc(rstd_done, 1)

            @block.vector
            def _(dve):
                nc.vector.memset(eps[:], GN_EPS).then_inc(eps_ready, 1)
                c = Chain(dve, v_step)

                def centre(p):
                    b = p % 2
                    dve.wait_ge(summed, p + 1)
                    c.ordered(nc.vector.scalar_tensor_tensor(out=yc[b][:], in0=mean[p % 3][:], scalar=-1.0 / HD, in1=y_acc[:, p, :],
                                                             op0=ALU.mult, op1=ALU.add))
                    nc.vector.tensor_tensor(sq[b][:], yc[b][:], yc[b][:], ALU.mult).then_inc(squared, 1)

                centre(0)
                for p in range(PAIRS):
                    if p + 1 < PAIRS:
                        if p:
                            dve.wait_ge(var_done, p)
                            dve.wait_ge(finished, p)
                        centre(p + 1)
                    b = p % 2
                    dve.wait_ge(rstd_done, p + 1)
                    c.ordered(nc.vector.tensor_tensor(yc[b][:], yc[b][:], rstd[b][:], ALU.mult))
                    c.ordered(nc.vector.tensor_scalar(yc[b][:], yc[b][:], vec[:, 7, p:p + 1], vec[:, 8, p:p + 1], ALU.mult, ALU.add))
                    c.ordered(nc.vector.tensor_tensor(yc[b][:], yc[b][:], bonus[:, p, :], ALU.add))
                    dve.wait_ge(gate_done, p + 1)
                    nc.vector.tensor_tensor(y_acc[:, p, :], yc[b][:], gate[p % 3][:], ALU.mult).then_inc(finished, 1)


def residual_input(nc, e, a, z, hi, lo):
    with ExitStack() as ctx:
        sb = lambda n, s, d=FP32: ctx.enter_context(nc.sbuf_tensor("ri_" + n, s, d))
        rows, cols = sb("rows", [P, KT // 2, 8]), sb("cols", [P, KT // 2, 64])
        merged = [sb(f"merged{b}", [P, 4, LAT]) for b in range(2)]
        tables_loaded, hi_done, lo_done, posed, scaled = sems(nc, ctx, "ri_tables_loaded", "ri_hi_done", "ri_lo_done", "ri_posed", "ri_scaled")
        loaded = sems(nc, ctx, "ri_merged0_loaded", "ri_merged1_loaded")
        x_loaded = sems(nc, ctx, *[f"ri_x_loaded{q}" for q in range(4)])
        with nc.Block() as block:
            @block.sync
            def _(sp):
                sp.dma_start(rows[:], a["pos_rows"]).then_inc(tables_loaded, 16)
                sp.dma_start(cols[:], a["pos_cols"]).then_inc(tables_loaded, 16)
                for q in range(4):
                    at = slice(4 * q, 4 * q + 4)
                    sp.dma_start(z[:, at, :], a["x"][at].rearrange("t p n -> p t n")).then_inc(x_loaded[q], 16)
                    if q >= 2:
                        sp.wait_ge(hi_done, q - 1)
                        sp.wait_ge(lo_done, q - 1)
                    sp.dma_start(merged[q % 2][:], e.merged_dram[at].rearrange("t p n -> p t n")).then_inc(loaded[q % 2], 16)

            @block.gpsimd
            def _(pool):
                pool.wait_ge(tables_loaded, 32)
                for k in range(KT):
                    if k % 4 == 0:
                        pool.wait_ge(x_loaded[k // 4], 16)
                    table = (rows[:, k, :, None].to_broadcast([P, 8, 64]) if k < KT // 2
                             else cols[:, k - KT // 2, None, :].to_broadcast([P, 8, 64]))
                    grid = z[:, k, :].rearrange("p (r c) -> p r c", c=64)
                    nc.gpsimd.tensor_tensor(grid, grid, table, ALU.add).then_inc(posed, 1)

            @block.scalar
            def _(act):
                for q in range(4):
                    act.wait_ge(loaded[q % 2], 16 * (q // 2 + 1))
                    nc.scalar.activation(hi[:, 4 * q:4 * q + 4, :], merged[q % 2][:], ACT.Copy).then_inc(hi_done, 1)

            @block.vector
            def _(dve):
                for q in range(4):
                    at = slice(4 * q, 4 * q + 4)
                    dve.wait_ge(posed, 4 * q + 4)
                    nc.vector.tensor_scalar(z[:, at, :], z[:, at, :], ALPHA, None, ALU.mult).then_inc(scaled, 1)
                    dve.wait_ge(hi_done, q + 1)
                    nc.vector.tensor_tensor(lo[:, at, :], merged[q % 2][:], hi[:, at, :].bitcast(FP32), ALU.subtract).then_inc(lo_done, 1)
                dve.wait_ge(scaled, 4)


def layer_norm(nc, a, name, z, gain, bias, finish):
    with ExitStack() as ctx:
        sb = lambda n, s, d=FP32: ctx.enter_context(nc.sbuf_tensor(name + n, s, d))
        mean_of = sb("mean_of", [P, P])
        eps, rstd = sb("eps", [P, 1]), sb("rstd", [P, LAT])
        sq = [sb(f"sq{b}", [P, LAT]) for b in range(2)]
        mean, var = (ctx.enter_context(nc.psum_tensor(name + n, [P, LAT], FP32)) for n in ("mean", "var"))
        const, mean_done, centred, squared, sq_used, var_done, rstd_done, scaled, normed, a_step, g_loaded = sems(
            nc, ctx, *(name + n for n in ("const", "mean_done", "centred", "squared", "sq_used", "var_done", "rstd_done", "scaled",
                                          "normed", "a_step", "g_loaded")))
        gb = sb("gain_bias", [P, 2, KT])
        on_act, on_dve, on_sp = finish(ctx, sb, normed)
        with nc.Block() as block:
            @block.sync
            def _(sp):
                sp.dma_start(gb[:, 0, :], gain).then_inc(g_loaded, 16)
                sp.dma_start(gb[:, 1, :], bias).then_inc(g_loaded, 16)
                on_sp(sp)

            @block.tensor
            def _(pe):
                pe.wait_ge(const, 1)
                for k in range(KT):
                    ins = nc.tensor.matmul(mean[:], mean_of[:], z[:, k, :], start=(k == 0), stop=(k == KT - 1))
                ins.then_inc(mean_done, 1)
                for k in range(KT):
                    pe.wait_ge(squared, k + 1)
                    nc.tensor.matmul(var[:], mean_of[:], sq[k % 2][:], start=(k == 0), stop=(k == KT - 1)).then_inc(sq_used, 1)

            @block.scalar
            def _(act):
                for k in range(KT):
                    act.wait_ge(centred, k + 1)
                    if k >= 2:
                        act.wait_ge(sq_used, k - 1)
                    nc.scalar.activation(sq[k % 2][:], z[:, k, :], ACT.Square).then_inc(squared, 1)
                act.wait_ge(sq_used, KT)
                nc.scalar.activation(rstd[:], var[:], ACT.Ln, bias=eps[:]).then_inc(a_step, 1)
                act.wait_ge(a_step, 1)
                nc.scalar.activation(rstd[:], rstd[:], ACT.Exp, scale=-0.5).then_inc(rstd_done, 1)
                on_act(act)

            @block.vector
            def _(dve):
                nc.vector.memset(mean_of[:], 1.0 / D)
                nc.vector.memset(eps[:], LN_EPS).then_inc(const, 1)
                dve.wait_ge(mean_done, 1)
                for k in range(KT):
                    nc.vector.tensor_tensor(z[:, k, :], z[:, k, :], mean[:], ALU.subtract).then_inc(centred, 1)
                dve.wait_ge(rstd_done, 1)
                dve.wait_ge(g_loaded, 32)
                for k in range(KT):
                    nc.vector.tensor_tensor(z[:, k, :], z[:, k, :], rstd[:], ALU.mult).then_inc(scaled, 1)
                    if k:
                        dve.wait_ge(scaled, k)
                        nc.vector.tensor_scalar(z[:, k - 1, :], z[:, k - 1, :], gb[:, 0, k - 1:k], gb[:, 1, k - 1:k], ALU.mult, ALU.add
                                                ).then_inc(normed, 1)
                        if k >= 2:
                            on_dve(dve, k - 2)
                dve.wait_ge(scaled, KT)
                nc.vector.tensor_scalar(z[:, KT - 1, :], z[:, KT - 1, :], gb[:, 0, KT - 1:KT], gb[:, 1, KT - 1:KT], ALU.mult, ALU.add
                                        ).then_inc(normed, 1)
                on_dve(dve, KT - 2)
                on_dve(dve, KT - 1)


def out_projection(nc, e, a):
    with ExitStack() as ctx:
        sb = lambda n, s, d=FP32: ctx.enter_context(nc.sbuf_tensor(n, s, d))
        z = sb("z1", [P, KT, LAT])
        with ExitStack() as inner:
            hi, lo = e.h_hi, e.h_lo
            landing = [inner.enter_context(nc.sbuf_tensor(f"o_landing{b}", [P, LAT], FP32)) for b in range(2)]
            residual_input(nc, e, a, z, hi, lo)

            def add(dve, unit, b):
                at = bass.ds(unit, 1)
                zt = z[:, at, :].rearrange("p o n -> p (o n)")
                return nc.vector.scalar_tensor_tensor(out=zt, in0=landing[b][:], scalar=e.mod[:, bass.ds(unit + 2 * KT, 1), 0],
                                                      in1=zt, op0=ALU.mult, op1=ALU.add)

            projection(nc, "o_", a["w_out"], 0, KT, hi, lo, [(0, LAT, 0)], add, landing, None)

        def finish(ctx, sb, normed):
            h2 = [sb(f"h2{b}", [P, LAT]) for b in range(2)]
            modded, hi_done, lo_done, stored = sems(nc, ctx, "h2_modded", "h2_hi_done", "h2_lo_done", "x1_stored")

            def on_dve(dve, k):
                dve.wait_ge(normed, k + 1)
                nc.vector.tensor_scalar(h2[k % 2][:], z[:, k, :], e.one_plus_scale2[:, k:k + 1], e.mod[:, 3 * KT + k, 0:1], ALU.mult, ALU.add
                                        ).then_inc(modded, 1)
                dve.wait_ge(hi_done, k + 1)
                nc.vector.tensor_tensor(e.h_lo[:, k, :], h2[k % 2][:], e.h_hi[:, k, :].bitcast(FP32), ALU.subtract).then_inc(lo_done, 1)

            def on_act(act):
                for k in range(KT):
                    act.wait_ge(modded, k + 1)
                    nc.scalar.activation(e.h_hi[:, k, :], h2[k % 2][:], ACT.Copy).then_inc(hi_done, 1)

            def on_sp(sp):
                for q in range(4):
                    sp.wait_ge(normed, 4 * q + 4)
                    sp.dma_start(e.x1_dram[:, 4 * q:4 * q + 4, :], z[:, 4 * q:4 * q + 4, :]).then_inc(stored, 16)
                sp.wait_ge(stored, 64)

            return on_act, on_dve, on_sp

        layer_norm(nc, a, "ln1_", z, a["ln1_g"], a["ln1_b"], finish)


TOK_TILES = LAT // P
Q_STEPS = 7


def best_of_rows(nc, c, landed, vals, positions, source, other, n):
    for half in range(2):
        at = slice(8 * half, 8 * half + 8)
        src = other if half else source
        nc.vector.tensor_copy(landed[:, 0:1], landed[:, 1:2])
        for r in range(n):
            ins = nc.vector.max(vals[:, r, at], src[:, r, :])
        c.ordered(ins)
        nc.vector.tensor_copy(landed[:, 0:1], landed[:, 1:2])
        for r in range(n):
            ins = nc.vector.max_index(positions[:, r, at], vals[:, r, at], src[:, r, :])
        if not half:
            for r in range(n):
                ins = nc.vector.match_replace(other[:, r, :], vals[:, r, at], src[:, r, :], LOWEST)
        c.ordered(ins)


def queries(nc, e, a):
    with ExitStack() as ctx:
        sb = lambda n, s, d=FP32: ctx.enter_context(nc.sbuf_tensor("q_" + n, s, d))
        landing = [sb(f"landing{b}", [P, LAT]) for b in range(2)]
        keys = sb("keys", [P, HP, NK])
        score, rest = sb("score", [P, TOK_TILES, NK]), sb("rest", [P, TOK_TILES, NK])
        val, idx = sb("val", [P, TOK_TILES, TOPK]), sb("idx", [P, TOK_TILES, TOPK], U32)
        landed_scratch = sb("landed_scratch", [P, 2])
        s_acc = [ctx.enter_context(nc.psum_tensor(f"q_s{b}", [P, TOK_TILES * NK], FP32)) for b in range(2)]
        keys_loaded, scratch_ready, scored, step = sems(nc, ctx, "keys_loaded", "q_scratch_ready", "scored", "q_step")
        with nc.Block() as block:
            @block.sync
            def _(sp):
                sp.dma_start(keys[:], a["peer_keys"]).then_inc(keys_loaded, 16)
                sp.wait_ge(keys_loaded, 16)

            @block.vector
            def _(dve):
                nc.vector.memset(landed_scratch[:], 0.0).then_inc(scratch_ready, 1)
                dve.wait_ge(scratch_ready, 1)

        def scores(pe, unit, b):
            for t in range(TOK_TILES):
                last = nc.tensor.matmul(s_acc[b][:, t * NK:(t + 1) * NK], landing[b][:, t * P:(t + 1) * P],
                                        keys[:, bass.ds(unit, 1), :].rearrange("p o n -> p (o n)"), start=True, stop=True)
            last.then_inc(scored, 1)

        def choose(dve, unit, b):
            c = Chain(dve, step, unit * Q_STEPS)
            dve.wait_ge(scored, unit + 1)
            c.ordered(nc.vector.tensor_copy(score[:].rearrange("p t n -> p (t n)"), s_acc[b][:]))
            best_of_rows(nc, c, landed_scratch, val, idx, score, rest, TOK_TILES)
            at = bass.ds(unit, 1)
            c.ordered(nc.vector.tensor_copy(e.best_key[:, :, at, :].rearrange("p t o k -> p t (o k)"), idx[:]))
            c.step(nc.vector.tensor_copy(landed_scratch[:, 0:1], landed_scratch[:, 1:2]))
            assert c.n == Q_STEPS, c.n
            return nc.vector.tensor_copy(e.best_val[:, :, at, :].rearrange("p t o k -> p t (o k)"), val[:])

        projection(nc, "q_", a["peer_wq"], 0, KT, e.h_hi, e.h_lo, [(0, LAT, 0)], choose, landing, None, scores)


R_STEPS = 16
SPREAD = 4
DEPTH = 4
BANKFUL = 4


def route(nc, e, a):
    with ExitStack() as ctx:
        sb = lambda n, s, d=FP32: ctx.enter_context(nc.sbuf_tensor("rt_" + n, s, d))
        ident, iota = sb("ident", [P, P]), sb("iota", [P, P])
        score, rest = sb("score", [P, HP, NK]), sb("rest", [P, HP, NK])
        one_of = score
        top, pos = sb("top", [P, PEER_HEADS, TOPK]), sb("pos", [P, PEER_HEADS, TOPK], U32)
        k12, k12_f = sb("k12", [P, 2, P], U32), sb("k12_f", [P, 2, P])
        chosen = sb("chosen", [P, 3, P])
        total, landed = sb("total", [P, PEER_HEADS]), sb("landed", [P, 2])
        sel = sb("sel", [P, 3, P])
        hot1, hot2, gated = ([sb(f"{n}{b}", [P, SPREAD, NK]) for b in range(DEPTH)] for n in ("hot1_", "hot2_", "gated"))
        dense = sb("dense", [P, NK, P])
        t_acc = ctx.enter_context(nc.psum_tensor("rt_t", [P, 3 * P], FP32))
        g_acc = [ctx.enter_context(nc.psum_tensor(f"rt_g{b}", [P, BANKFUL * NK], FP32)) for b in range(4)]
        (const_loaded, scratch_ready, shifted, exp_done, chosen_ready, turned, sel_ready, hot_ready, gated_ready,
         hot_used, sel_used, dense_free, bank_read, stored, v_step) = sems(
            nc, ctx, "rt_const_loaded", "rt_scratch_ready", "top_shifted", "top_exp_done", "chosen_ready", "turned",
            "sel_ready", "hot_ready", "gated_ready", "hot_used", "sel_used", "dense_free", "gate_bank_read", "gates_stored", "rt_v_step")
        tiles, turns, fills = LAT // P, P // SPREAD, P // BANKFUL
        per_turn = SPREAD // BANKFUL
        with nc.Block() as block:
            @block.sync
            def _(sp):
                for dst, src in ((ident, a["ident"]), (iota, a["iota"])):
                    sp.dma_start(dst[:], src).then_inc(const_loaded, 16)
                sp.sem_inc(dense_free, 1)

                with sp.Fori(0, tiles) as t:
                    sp.wait_ge(bank_read, (t + 1) * fills + 4)
                    sp.dma_start(e.gates_dram[:, :, bass.ds(t * P, P)], dense[:]).then_inc(stored, 16)
                    sp.wait_ge(stored, 16 * t + 16)
                    sp.sem_inc(dense_free, 1)

            @block.gpsimd
            def _(pool):
                with pool.Fori(0, tiles) as t:
                    with pool.Fori(0, turns // DEPTH) as i:
                        for b in range(DEPTH):
                            pool.wait_ge(hot_ready, t * turns + DEPTH * i + b + 1)
                            at = bass.ds((DEPTH * i + b) * SPREAD, SPREAD)
                            nc.gpsimd.tensor_tensor(gated[b][:], hot2[b][:], sel[:, 2, at, None].to_broadcast([P, SPREAD, NK]),
                                                    ALU.mult).then_inc(gated_ready, 1)

            @block.tensor
            def _(pe):
                pe.sem_inc(hot_used, DEPTH * per_turn)
                pe.sem_inc(turned, 1)
                pe.wait_ge(const_loaded, 32)
                with pe.Fori(0, tiles) as t:
                    pe.wait_ge(chosen_ready, t + 2)
                    pe.wait_ge(sel_ready, t + 1)
                    for j in range(3):
                        last = nc.tensor.transpose(t_acc[:, j * P:(j + 1) * P], chosen[:, j, :], ident[:])
                    last.then_inc(turned, 1)
                    with pe.Fori(0, turns // DEPTH) as i:
                        for b in range(DEPTH):
                            turn = t * turns + DEPTH * i + b
                            pe.wait_ge(gated_ready, turn + 1)
                            for n in range(SPREAD):
                                f = n // BANKFUL
                                if n % BANKFUL == 0:
                                    pe.wait_ge(bank_read, turn * per_turn + f + 1)
                                ins = nc.tensor.matmul(g_acc[(b * per_turn + f) % 4][:, (n % BANKFUL) * NK:(n % BANKFUL + 1) * NK],
                                                       hot1[b][:, n, :], gated[b][:, n, :], start=True, stop=True)
                                if n % BANKFUL == BANKFUL - 1:
                                    ins.then_inc(hot_used, 1)

            @block.scalar
            def _(act):
                act.sem_inc(sel_ready, 1)
                act.sem_inc(bank_read, 4)
                with act.Fori(0, tiles) as t:
                    act.wait_ge(shifted, t + 1)
                    nc.scalar.activation(chosen[:, 2, :], top[:].rearrange("p h k -> p (h k)"), ACT.Exp).then_inc(exp_done, 1)
                    act.wait_ge(turned, t + 2)
                    act.wait_ge(sel_used, t + 1)
                    nc.scalar.activation(sel[:].rearrange("p a n -> p (a n)"), t_acc[:], ACT.Copy).then_inc(sel_ready, 1)
                    act.wait_ge(dense_free, t + 1)

                    def land(i, b):
                        for f in range(per_turn):
                            act.wait_ge(hot_used, (t * turns + DEPTH * i + b + DEPTH) * per_turn + f + 1)
                            at = bass.ds((DEPTH * i + b) * SPREAD + f * BANKFUL, BANKFUL)
                            nc.scalar.activation(dense[:, :, at].rearrange("p i t -> p t i"),
                                                 g_acc[(b * per_turn + f) % 4][:].rearrange("p (t i) -> p t i", i=NK), ACT.Copy
                                                 ).then_inc(bank_read, 1)

                    with act.Fori(0, turns // DEPTH) as i:
                        for b in range(DEPTH):
                            land(i, b)

            @block.vector
            def _(dve):
                dve.sem_inc(chosen_ready, 1)
                dve.sem_inc(sel_used, 1)
                nc.vector.memset(landed[:], 0.0).then_inc(scratch_ready, 1)
                dve.wait_ge(scratch_ready, 1)
                dve.wait_ge(const_loaded, 32)
                with dve.Fori(0, tiles) as t:
                    c = Chain(dve, v_step, t * R_STEPS)

                    at = bass.ds(t, 1)
                    halves = e.best_val[:, at, :, :].rearrange("p o (h s) k -> p (o h) s k", s=2)
                    cand = score[:].rearrange("p (h s) n -> p h (s n)", s=2)
                    left = rest[:].rearrange("p (h s) n -> p h (s n)", s=2)
                    full = [P, PEER_HEADS, TOPK, TOPK]
                    c.ordered(nc.vector.tensor_tensor(cand.rearrange("p h (i j) -> p h i j", j=TOPK), halves[:, :, 0, :, None].to_broadcast(full),
                                                      halves[:, :, 1, None, :].to_broadcast(full), ALU.add))
                    best_of_rows(nc, c, landed, top, pos, cand, left, PEER_HEADS)
                    flat_pos = pos[:].rearrange("p h k -> p (h k)")
                    nc.vector.tensor_scalar(k12[:, 0, :], flat_pos, 4, None, ALU.logical_shift_right)
                    nc.vector.tensor_scalar(k12[:, 1, :], flat_pos, 15, None, ALU.bitwise_and)
                    best_of = total[:]
                    c.ordered(nc.vector.tensor_copy(best_of, top[:, :, 0]))
                    c.ordered(nc.vector.tensor_copy(k12_f[:], k12[:]))
                    dve.wait_ge(turned, t + 1)
                    nc.vector.tensor_tensor(top[:], top[:], best_of[:, :, None].to_broadcast([P, PEER_HEADS, TOPK]), ALU.subtract
                                            ).then_inc(shifted, 1)
                    by_half = e.best_key[:, at, :, :].rearrange("p o (h s) k -> p (o h) s k", s=2)
                    for s in range(2):
                        one = one_of[:].rearrange("p h n -> p (h n)").rearrange("p (k j) -> p k j", j=TOPK)
                        c.ordered(nc.vector.tensor_tensor(one, iota[:, None, 0:TOPK].to_broadcast([P, P, TOPK]),
                                                          k12_f[:, s, :, None].to_broadcast([P, P, TOPK]), ALU.is_equal))
                        four = one.rearrange("p (h k) j -> p h k j", h=PEER_HEADS)
                        c.ordered(nc.vector.tensor_tensor(four, four, by_half[:, :, s, None, :].to_broadcast(full), ALU.mult))
                        c.ordered(nc.vector.tensor_reduce(chosen[:, s, :], one, AX, ALU.add))
                    dve.wait_ge(exp_done, t + 1)
                    gate = chosen[:, 2, :].rearrange("p (h k) -> p h k", k=TOPK)
                    c.ordered(nc.vector.tensor_reduce(total[:], gate, AX, ALU.add))
                    c.ordered(nc.vector.reciprocal(total[:], total[:]))
                    c.ordered(nc.vector.tensor_tensor(gate, gate, total[:, :, None].to_broadcast([P, PEER_HEADS, TOPK]), ALU.mult))
                    dve.sem_inc(chosen_ready, 1)
                    assert c.n == R_STEPS, c.n
                    with dve.Fori(0, turns // DEPTH) as i:
                        for b in range(DEPTH):
                            turn = t * turns + DEPTH * i + b
                            if b == 0:
                                dve.wait_ge(sel_ready, t + 2)
                            dve.wait_ge(hot_used, (turn + 1) * per_turn)
                            for m, dst in ((0, hot1[b]), (1, hot2[b])):
                                at = bass.ds((DEPTH * i + b) * SPREAD, SPREAD)
                                full = [P, SPREAD, NK]
                                ins = nc.vector.tensor_tensor(dst[:], iota[:, None, :].to_broadcast(full), sel[:, m, at, None].to_broadcast(full),
                                                              ALU.is_equal)
                            ins.then_inc(hot_ready, 1)
                    dve.wait_ge(gated_ready, (t + 1) * turns)
                    dve.sem_inc(sel_used, 1)


def experts(nc, e, a, f):
    chunks, v_units = NK, D // DU
    groups, units = chunks // GROUP, GROUP + v_units
    with ExitStack() as ctx:
        sb = lambda n, s, d=FP32: ctx.enter_context(nc.sbuf_tensor("ex_" + n, s, d))
        raw = [sb(f"raw{b}", [P, KT * P]) for b in range(2)]
        hi, lo = ([sb(f"{n}{b}", [P, KT * P], FP32R) for b in range(2)] for n in ("hi", "lo"))
        w_hi, w_lo = (sb(n, [P, GROUP, LAT], FP32R) for n in ("w_hi", "w_lo"))
        gates, act_, w = ([sb(f"{n}{b}", [P, LAT]) for b in range(2)] for n in ("gates", "act", "w"))
        u_acc = [ctx.enter_context(nc.psum_tensor(f"ex_u{b}", [P, LAT], FP32)) for b in range(2)]
        v_acc = [[ctx.enter_context(nc.psum_tensor(f"ex_v{b}{h}", [P, LAT], FP32)) for h in range(2)] for b in range(2)]
        hi_done, lo_done, products, gelu_done, weighted, w_ready, added, w_step, gates_free = sems(
            nc, ctx, "ex_hi_done", "ex_lo_done", "ex_products", "gelu_ready", "act_weighted", "w_ready", "v_added", "w_step", "gates_free")
        loaded = sems(nc, ctx, "ex_raw0_loaded", "ex_raw1_loaded")
        g_loaded = sems(nc, ctx, "gates0_loaded", "gates1_loaded")
        assert units % 2 == 0 and GROUP % 2 == 0
        with nc.Block() as block:
            @block.sync
            def _(sp):
                with sp.Fori(0, groups) as g:
                    for u in range(units):
                        sp.wait_ge(hi_done, g * units + u + 1)
                        sp.wait_ge(lo_done, g * units + u + 1)
                        src = (a["peer_u"][bass.ds(g * GROUP + u, 1)] if u < GROUP
                               else a["peer_v"][bass.ds(g * v_units + (u - GROUP), 1)])
                        sp.dma_start(raw[u % 2][:], src.rearrange("o p n -> p (o n)")).then_inc(loaded[u % 2], 16)

            @block.gpsimd
            def _(pool):
                with pool.Fori(0, groups) as g:
                    for c in range(GROUP):
                        pool.wait_ge(weighted, g * GROUP + c + 1)
                        pool.dma_start(gates[c % 2][:], e.gates_dram[:, bass.ds(g * GROUP + c, 1), :].rearrange("p o n -> p (o n)")
                                       ).then_inc(g_loaded[c % 2], 16)

            @block.scalar
            def _(act):
                act.sem_inc(hi_done, 2)
                with act.Fori(0, groups) as g:
                    for u in range(units):
                        act.wait_ge(loaded[u % 2], (g * (units // 2) + u // 2 + 1) * 16)
                        act.wait_ge(products, g * units + u + 1)
                        nc.scalar.activation(hi[u % 2][:], raw[u % 2][:], ACT.Copy).then_inc(hi_done, 1)
                        if 0 < u <= GROUP:
                            c = u - 1
                            act.wait_ge(products, g * units + c + 3)
                            act.wait_ge(weighted, g * GROUP + c + 1)
                            nc.scalar.activation(act_[c % 2][:], u_acc[c % 2][:], ACT.Gelu).then_inc(gelu_done, 1)

            @block.vector
            def _(dve):
                dve.sem_inc(lo_done, 2)
                dve.sem_inc(weighted, 2)

                def low(g, u):
                    dve.wait_ge(hi_done, g * units + u + 3)
                    nc.vector.tensor_tensor(lo[u % 2][:], raw[u % 2][:], hi[u % 2][:].bitcast(FP32), ALU.subtract).then_inc(lo_done, 1)

                def weigh(g, c):
                    n = g * GROUP + c
                    dve.wait_ge(gelu_done, n + 1)
                    dve.wait_ge(g_loaded[c % 2], (g * (GROUP // 2) + c // 2 + 1) * 16)
                    nc.vector.tensor_tensor(w[c % 2][:], act_[c % 2][:], gates[c % 2][:], ALU.mult).then_inc(weighted, 1)
                    dve.wait_ge(weighted, n + 3)
                    nc.vector.tensor_copy(w_hi[:, c, :], w[c % 2][:]).then_inc(w_step, 1)
                    dve.wait_ge(w_step, n + 1)
                    nc.vector.tensor_tensor(w_lo[:, c, :], w[c % 2][:], w_hi[:, c, :].bitcast(FP32), ALU.subtract).then_inc(w_ready, 1)

                def add(g, v):
                    dve.wait_ge(products, g * units + GROUP + v + 3)
                    for h in range(2):
                        t = f[:, 2 * v + h, :]
                        nc.vector.tensor_tensor(t, t, v_acc[v % 2][h][:], ALU.add).then_inc(added, 1)

                def group(g, last):
                    for u in range(1, units):
                        low(g, u)
                        if u <= GROUP:
                            weigh(g, u - 1)
                        else:
                            add(g, u - GROUP - 1)
                    if not last:
                        low(g + 1, 0)
                    add(g, v_units - 1)

                nc.vector.memset(f[:], 0.0).then_inc(added, 4)
                dve.wait_ge(added, 4)
                low(0, 0)
                with dve.Fori(0, groups - 1) as g:
                    group(g, False)
                group(groups - 1, True)

            @block.tensor
            def _(pe):
                pe.sem_inc(products, 2)

                def three(out, ws, xs, first, last):
                    for n, (wt, x) in enumerate(((ws[0], xs[0]), (ws[0], xs[1]), (ws[1], xs[0]))):
                        ins = nc.tensor.matmul(out, wt, x, start=first and n == 0, stop=last and n == 2)
                    return ins

                with pe.Fori(0, groups) as g:
                    for u in range(units):
                        b = u % 2
                        pe.wait_ge(lo_done, g * units + u + 3)
                        if u < GROUP:
                            pe.wait_ge(gelu_done, g * GROUP + u - 1) if u >= 2 else None
                            for k in range(KT):
                                ks = slice(k * P, (k + 1) * P)
                                ins = three(u_acc[b][:], (hi[b][:, ks], lo[b][:, ks]), (e.h_hi[:, k, :], e.h_lo[:, k, :]), k == 0, k == KT - 1)
                        else:
                            v = u - GROUP
                            for h in range(2):
                                pe.wait_ge(added, (g * v_units + v) * 2 + h + 1)
                                for c in range(GROUP):
                                    if v == 0 and h == 0:
                                        pe.wait_ge(w_ready, g * GROUP + c + 1)
                                    ds = slice(c * DU + h * P, c * DU + (h + 1) * P)
                                    ins = three(v_acc[v % 2][h][:], (hi[b][:, ds], lo[b][:, ds]), (w_hi[:, c, :], w_lo[:, c, :]),
                                                c == 0, c == GROUP - 1)
                        ins.then_inc(products, 1)


def final(nc, e, a, f, out):
    with ExitStack() as ctx:
        x1 = ctx.enter_context(nc.sbuf_tensor("x1", [P, KT, LAT], FP32))
        scaled, added, step = sems(nc, ctx, "x1_scaled", "x1_added", "gate2_step")
        loaded = sems(nc, ctx, *[f"x1_loaded{q}" for q in range(4)])
        with nc.Block() as block:
            @block.sync
            def _(sp):
                for q in range(4):
                    sp.dma_start(x1[:, 4 * q:4 * q + 4, :], e.x1_dram[:, 4 * q:4 * q + 4, :]).then_inc(loaded[q], 16)

            @block.scalar
            def _(act):
                for k in range(KT):
                    nc.scalar.activation(f[:, k, :], f[:, k, :], ACT.Copy, scale=e.mod[:, 5 * KT + k, 0:1]).then_inc(step, 1)

            @block.vector
            def _(dve):
                for k in range(KT):
                    dve.wait_ge(step, k + 1)
                    dve.wait_ge(loaded[k // 4], 16)
                    nc.vector.scalar_tensor_tensor(out=f[:, k, :], in0=x1[:, k, :], scalar=ALPHA, in1=f[:, k, :], op0=ALU.mult, op1=ALU.add
                                                   ).then_inc(added, 1)

        def finish(ctx, sb, normed):
            (stored,) = sems(nc, ctx, "out_stored")

            def on_sp(sp):
                for q in range(4):
                    sp.wait_ge(normed, 4 * q + 4)
                    sp.dma_start(out[4 * q:4 * q + 4].rearrange("t p n -> p t n"), f[:, 4 * q:4 * q + 4, :]).then_inc(stored, 16)
                sp.wait_ge(stored, 64)

            return (lambda act: None), (lambda dve, k: None), on_sp

        layer_norm(nc, a, "ln2_", f, a["ln2_g"], a["ln2_b"], finish)


def build(nc, a, out):
    e = Env()
    with ExitStack() as ctx:
        sb = lambda n, s, d=FP32: ctx.enter_context(nc.sbuf_tensor(n, s, d))
        e.p_dram = nc.dram_tensor("p_scratch", [TILES, P, TW], FP32, kind="Internal").ap()
        e.merged_dram = nc.dram_tensor("merged_scratch", [KT, P, LAT], FP32, kind="Internal").ap()
        e.cond_act = sb("cond_act", [P, KT, 2])
        e.bias, e.mod = sb("ada_bias", [P, MOD_TILES, 2]), sb("mod", [P, MOD_TILES, 2])
        e.one_plus_scale, e.one_plus_scale2 = sb("one_plus_scale", [P, KT, 2]), sb("one_plus_scale2", [P, KT])
        e.x1_dram = nc.dram_tensor("x1_scratch", [P, KT, LAT], FP32, kind="Internal").ap()
        e.gates_dram = nc.dram_tensor("gates_scratch", [NK, NK, LAT], FP32, kind="Internal").ap()
        modulation(nc, e, a)
        in_projection(nc, e, a)
        rglru(nc, e, a)
        rwkv(nc, e, a)
        tail(nc, e, a, out)


def tail(nc, e, a, out):
    with ExitStack() as ctx:
        with ExitStack() as inner:
            e.h_hi, e.h_lo = (inner.enter_context(nc.sbuf_tensor(n, [P, KT, LAT], FP32R)) for n in ("h_hi", "h_lo"))
            out_projection(nc, e, a)
            with ExitStack() as picks:
                e.best_key, e.best_val = (picks.enter_context(nc.sbuf_tensor(n, [P, TOK_TILES, HP, TOPK], FP32))
                                          for n in ("best_key", "best_val"))
                queries(nc, e, a)
                route(nc, e, a)
            f = inner.enter_context(nc.sbuf_tensor("f", [P, KT, LAT], FP32))
            experts(nc, e, a, f)
            final(nc, e, a, f, out)


def position_tables():
    quarter = D // 4
    freq = (1.0 / (10000.0 ** (np.arange(quarter, dtype=np.float32) / quarter))).astype(np.float32)

    def table(n):
        ang = (np.arange(n, dtype=np.float32)[:, None] * freq[None, :]).astype(np.float32)
        t = np.concatenate([np.sin(ang), np.cos(ang)], axis=-1).T.astype(np.float32)
        return np.ascontiguousarray(t.reshape(KT // 2, P, n).transpose(1, 0, 2))

    return table(LAT // 64), table(64)


def shape_constants():
    i = np.arange(P)
    row, col = i[:, None], i[None, :]
    f = lambda m: np.asarray(m, np.float32)
    tri = np.stack([np.stack([f(row < col), f(row <= col)], 1), np.stack([f(row > col), f(row >= col)], 1)], 1)
    levels = []
    for d in range(2):
        late, early = (row, col) if d == 0 else (col, row)
        levels.append(np.stack([f((row == col) | ((row >> k == col >> k) & (late >> (k - 1) & 1 == 1) & (early >> (k - 1) & 1 == 0)))
                                for k in range(1, LEVELS + 1)], 1))
    return {"iota": f(0 * row + col), "two_by_two": np.eye(2, dtype=np.float32), "ones_column": np.ones((P, 1), np.float32), "ident": f(row == col), "rwkv_ones": f(row // HD == col // HD), "rwkv_tri": np.ascontiguousarray(tri),
            "rwkv_level": np.ascontiguousarray(np.stack(levels, 1))}


def weight_tiles(w):
    n = w.shape[1] // P
    return np.ascontiguousarray(w.reshape(KT, P, n, P).transpose(2, 1, 0, 3)).reshape(n, P, KT * P)


def columns(v):
    return np.ascontiguousarray(np.asarray(v).reshape(-1, P).T)


def lay_out(inputs):
    g = {k: np.asarray(v) for k, v in inputs.items()}
    a = {}
    a["cond"] = np.ascontiguousarray(np.stack([columns(g["c"][0]), columns(g["c_ctx"])], axis=-1))
    a["ada_w"] = np.ascontiguousarray(g["ada_w"][0][:, :2 * D].reshape(KT, P, MOD_UNITS, MW).transpose(2, 1, 0, 3)).reshape(MOD_UNITS, P, KT * MW)
    a["ada_late"] = weight_tiles(g["ada_w"][0][:, 2 * D:])
    b = columns(g["ada_b"][0])
    a["ada_b"] = np.ascontiguousarray(np.stack([b, b], axis=-1))
    a["pos_rows"], a["pos_cols"] = position_tables()
    a["ctx"] = np.ascontiguousarray(g["ctx"][0].T).reshape(KT, P, CTX)
    a["x"] = np.ascontiguousarray(g["x"][0].T).reshape(KT, P, LAT)
    w = g["w_in"][0]
    o = 2 * LRU
    r, k, v, lora, gd = o, o + LRU, o + 2 * LRU, o + 3 * LRU, o + 3 * LRU + 2 * P
    order = [w[:, 0:LRU], w[:, k:v], w[:, v:lora], w[:, lora:gd], w[:, LRU:o], w[:, r:k],
             w[:, gd:], np.zeros((D, 2 * P - (w.shape[1] - gd)), w.dtype)]
    a["w_in"] = weight_tiles(np.concatenate(order, axis=1))
    m = g["rwkv_mu"][0]
    z = np.zeros((2, LRU), m.dtype)
    m = np.concatenate([z, m[:, LRU:2 * LRU], m[:, 2 * LRU:3 * LRU], m[:, 3 * LRU:3 * LRU + 2 * P], z, m[:, 0:LRU],
                        m[:, 3 * LRU + 2 * P:], np.zeros((2, 2 * P - (w.shape[1] - gd)), m.dtype)], axis=1)
    a["mu"] = np.ascontiguousarray(np.stack([columns(m[0]), columns(m[1])], axis=-1))
    more_layout(g, a)
    return a


def more_layout(g, a):
    v = [columns(g["lru_conv_w"][0, t]) for t in range(4)] + [columns(g["lru_conv_b"][0])]
    v += [columns(g[n][0, d]) for n in ("lru_ba", "lru_bx", "lru_lambda") for d in range(2)]
    a["lru_vec"] = np.ascontiguousarray(np.stack(v, axis=1))
    for n in ("lru_wa", "lru_wx"):
        a[n] = np.ascontiguousarray(g[n][0].reshape(2 * LT, 2, HD, HD).transpose(1, 2, 0, 3))
    v = [columns(g[n][0, d]) for n in ("rwkv_w0", "rwkv_a0") for d in range(2)]
    v += [columns(g[n][0].reshape(-1)) for n in ("rwkv_k_k", "rwkv_k_a", "rwkv_r_k", "rwkv_gn_g", "rwkv_gn_b")]
    a["rwkv_vec"] = np.ascontiguousarray(np.stack(v, axis=1))
    a["rwkv_w2"], a["rwkv_a2"] = g["rwkv_w2"][0].reshape(P, LRU), g["rwkv_a2"][0].reshape(P, LRU)
    g2 = g["rwkv_g2"][0]
    a["rwkv_g2"] = np.ascontiguousarray(np.concatenate([g2, np.zeros((2 * P - len(g2), LRU), g2.dtype)]).reshape(2, P, LRU).transpose(1, 0, 2))
    a.update(shape_constants())
    a["w_out"], a["peer_wq"] = weight_tiles(g["w_out"][0]), weight_tiles(g["peer_wq"][0])
    for n in ("ln1_g", "ln1_b", "ln2_g", "ln2_b"):
        a[n] = columns(g[n][0])
    a["peer_keys"] = np.ascontiguousarray(g["peer_subkeys"][0].reshape(HP, NK, P).transpose(2, 0, 1))
    a["peer_u"] = np.ascontiguousarray(g["peer_u"][0].reshape(NK, NK, KT, P).transpose(1, 3, 2, 0)).reshape(NK, P, KT * P)
    a["peer_v"] = np.ascontiguousarray(g["peer_v"][0].reshape(NK, NK // GROUP, GROUP, D // DU, DU).transpose(1, 3, 0, 2, 4)
                                       ).reshape(NK, P, GROUP * DU)


_OUT = (KT, P, LAT)


def kernel(**inputs):
    import concourse.bacc as bacc
    from concourse.bass_utils import run_bass_kernel_spmd

    arrays = lay_out(inputs)
    nc = bacc.Bacc("TRN2", target_bir_lowering=False, num_devices=1)
    a = {n: nc.dram_tensor("in_" + n, v.shape, mybir.dt.from_np(v.dtype), kind="ExternalInput").ap() for n, v in arrays.items()}
    out = nc.dram_tensor("out_dram", _OUT, FP32, kind="ExternalOutput").ap()
    build(nc, a, out)
    r = run_bass_kernel_spmd(nc, [{"in_" + n: v for n, v in arrays.items()}], core_ids=[0])
    return np.ascontiguousarray(r.results[0]["out_dram"].reshape(D, LAT).T)[None]
```
